# Optimizing a Trainium2 kernel written in Bass

```python
import math
import jax, jax.numpy as jnp
from jax import lax
import numpy as np

D_MODEL = 1024
BATCH = 1
SEQ = 1024
DEPTH = 1
DEC_BATCH = 1
DEC_SEQ = 64
PAST_LEN = 128

CHUNK = 64
SB_HEADS = 8
SB_HEAD_DIM = 128
SB_WIDTH = SB_HEADS * SB_HEAD_DIM
Q_BLOCK = 128
HG_HEADS = 8
HG_KEY_DIM = 128
HG_VAL_DIM = 128
HG_KEY_WIDTH = HG_HEADS * HG_KEY_DIM
HG_VAL_WIDTH = HG_HEADS * HG_VAL_DIM
HG_BLOCK = CHUNK // 4
LB_FLOOR = 1e-30
N_EXPERTS = 64
TOP_K = 8
N_GROUPS = 8
TOPK_GROUPS = 4
D_EXPERT = 256
D_SHARED = 256
ROUTE_SCALE = 2.5
EXPERT_BLOCK = 128
NEG_BIG = -1e9
ALPHA = (2 * DEPTH) ** 0.25
BETA = (8 * DEPTH) ** -0.25
LN_EPS = 1e-5
RMS_EPS = 1e-6
IN_SPLITS = (SB_WIDTH, SB_WIDTH, SB_WIDTH, HG_KEY_WIDTH, HG_KEY_WIDTH, HG_VAL_WIDTH, HG_VAL_WIDTH, D_MODEL, D_MODEL)
IN_WIDTH = sum(IN_SPLITS)

kernel_name = "stickbreak_hgrn2_moe_deepnorm_stream"

F32 = jnp.float32

def layer_norm(x, g, b):
    xf = x.astype(F32)
    mu = jnp.mean(xf, -1, keepdims=True)
    var = jnp.mean(jnp.square(xf - mu), -1, keepdims=True)
    return ((xf - mu) * lax.rsqrt(var + LN_EPS) * g.astype(F32) + b.astype(F32)).astype(x.dtype)

def rms_norm(x, g):
    xf = x.astype(F32)
    return xf * lax.rsqrt(jnp.mean(xf * xf, -1, keepdims=True) + RMS_EPS) * g.astype(F32)

def stick_breaking_block(q, k, v, q_pos, k_pos):
    z = jnp.einsum('bqhd,bkhd->bhqk', q, k).astype(F32) / math.sqrt(SB_HEAD_DIM)
    mask = k_pos[None, :] < q_pos[:, None]
    log_keep = jnp.where(mask, jax.nn.log_sigmoid(-z), 0.0)
    after = lax.cumsum(log_keep, axis=3, reverse=True) - log_keep
    log_w = jnp.where(mask, jax.nn.log_sigmoid(z) + after, 0.0)
    w = jnp.where(mask, jnp.exp(log_w), 0.0)
    return jnp.einsum('bhqk,bkhd->bqhd', w.astype(v.dtype), v)

def stick_breaking_prompt(q, k, v):
    B, S, H, Dh = q.shape
    nb = S // Q_BLOCK
    k_pos = jnp.arange(S)
    qb = q.reshape(B, nb, Q_BLOCK, H, Dh).transpose(1, 0, 2, 3, 4)

    def one_block(args):
        qi, i = args
        q_pos = i * Q_BLOCK + jnp.arange(Q_BLOCK)
        return stick_breaking_block(qi, k, v, q_pos, k_pos)

    out = lax.map(one_block, (qb, jnp.arange(nb)))
    return out.transpose(1, 0, 2, 3, 4).reshape(B, S, H, Dh)

def hgrn2_chunked(q, logf, kk, v, s0):
    B, T, H, _ = q.shape
    pad = (-T) % HG_BLOCK
    padw = ((0, 0), (0, pad), (0, 0), (0, 0))
    q, logf, kk, v = [jnp.pad(a, padw) for a in (q, logf, kk, v)]
    nb = (T + pad) // HG_BLOCK

    def blocks(a):
        return a.reshape(B, nb, HG_BLOCK, H, a.shape[-1]).transpose(1, 0, 3, 2, 4)

    causal = jnp.tril(jnp.ones((HG_BLOCK, HG_BLOCK), bool))[:, :, None]

    def step(s, xs):
        qb, fb, kb, vb = xs
        b = jnp.cumsum(fb, axis=2)
        diff = b[:, :, :, None, :] - b[:, :, None, :, :]
        decay = jnp.where(causal, jnp.exp(jnp.where(causal, diff, 0.0)), 0.0)
        scores = jnp.einsum('bhtc,bhsc,bhtsc->bhts', qb, kb, decay)
        o = jnp.einsum('bhts,bhsv->bhtv', scores, vb) + jnp.einsum('bhtc,bhcv->bhtv', qb * jnp.exp(b), s)
        b_last = b[:, :, -1:, :]
        s_new = jnp.exp(b_last[:, :, 0, :])[..., None] * s + jnp.einsum('bhsc,bhsv->bhcv', kb * jnp.exp(b_last - b), vb)
        return s_new, o

    s_fin, o = lax.scan(step, s0, (blocks(q), blocks(logf), blocks(kk), blocks(v)))
    o = o.transpose(1, 0, 3, 2, 4).reshape(B, nb * HG_BLOCK, H, -1)[:, :T]
    return o, s_fin

def route(h2, w_router, router_bias):
    T = h2.shape[0]
    s = jax.nn.sigmoid(jnp.einsum('td,de->te', h2, w_router).astype(F32))
    sb = s + router_bias.astype(F32)
    grp = sb.reshape(T, N_GROUPS, N_EXPERTS // N_GROUPS)
    grp_score = jnp.sum(lax.top_k(grp, 2)[0], -1)
    _, gidx = lax.top_k(grp_score, TOPK_GROUPS)
    gmask = jnp.any(gidx[..., None] == jnp.arange(N_GROUPS), axis=-2)
    emask = jnp.repeat(gmask, N_EXPERTS // N_GROUPS, axis=-1)
    _, idx = lax.top_k(jnp.where(emask, sb, NEG_BIG), TOP_K)
    w = jnp.take_along_axis(s, idx, axis=-1)
    w = w / jnp.sum(w, -1, keepdims=True) * ROUTE_SCALE
    return idx, w

def routed_experts(h2, idx, wts, w_gate, w_up, w_down):
    T = h2.shape[0]
    A = T * TOP_K
    flat_e = idx.reshape(A)
    order = jnp.argsort(flat_e)
    sorted_e = flat_e[order]
    tok_sorted = (order // TOP_K).astype(jnp.int32)
    w_sorted = wts.reshape(A)[order].astype(h2.dtype)
    counts = jnp.zeros((N_EXPERTS,), jnp.int32).at[flat_e].add(1)
    padded = (counts + EXPERT_BLOCK - 1) // EXPERT_BLOCK * EXPERT_BLOCK
    pad_end = jnp.cumsum(padded)
    pad_start = pad_end - padded
    grp_start = jnp.cumsum(counts) - counts
    dest = pad_start[sorted_e] + jnp.arange(A, dtype=jnp.int32) - grp_start[sorted_e]
    n_blocks = -(-(A + N_EXPERTS * (EXPERT_BLOCK - 1)) // EXPERT_BLOCK)
    P = n_blocks * EXPERT_BLOCK
    row_tok = jnp.zeros((P,), jnp.int32).at[dest].set(tok_sorted)
    row_w = jnp.zeros((P,), h2.dtype).at[dest].set(w_sorted)
    block_e = jnp.minimum(jnp.searchsorted(pad_end, jnp.arange(n_blocks, dtype=jnp.int32) * EXPERT_BLOCK, side='right'), N_EXPERTS - 1)

    def step(y, xs):
        toks, ws, e = xs
        xb = h2[toks]
        hb = jax.nn.silu(xb @ w_gate[e]) * (xb @ w_up[e])
        return y.at[toks].add((hb @ w_down[e]) * ws[:, None]), None

    y, _ = lax.scan(step, jnp.zeros_like(h2), (row_tok.reshape(n_blocks, EXPERT_BLOCK), row_w.reshape(n_blocks, EXPERT_BLOCK), block_e))
    return y

def trunk_layer(x, past_k, past_v, s0, lb, w_in, w_out, hg_norm, ln1_g, ln1_b, w_router, router_bias,
                w_eg, w_eu, w_ed, w_sg, w_su, w_sd, ln2_g, ln2_b):
    B, T, _ = x.shape
    split_pts = tuple(int(c) for c in np.cumsum(IN_SPLITS)[:-1])
    sb_q, sb_k, sb_v, hg_q, hg_f, hg_i, hg_g, gate_sb, gate_hg = jnp.split(
        jnp.einsum('btd,de->bte', x, w_in), split_pts, axis=-1)
    q = sb_q.reshape(B, T, SB_HEADS, SB_HEAD_DIM)
    k = sb_k.reshape(B, T, SB_HEADS, SB_HEAD_DIM)
    v = sb_v.reshape(B, T, SB_HEADS, SB_HEAD_DIM)
    if past_k is None:
        o_sb = stick_breaking_prompt(q, k, v)
    else:
        P = past_k.shape[1]
        o_sb = stick_breaking_block(q, jnp.concatenate([past_k.astype(k.dtype), k], 1),
                                    jnp.concatenate([past_v.astype(v.dtype), v], 1),
                                    P + jnp.arange(T), jnp.arange(P + T))
    qh = jax.nn.silu(hg_q.astype(F32)).reshape(B, T, HG_HEADS, HG_KEY_DIM)
    a = hg_f.astype(F32)
    logf = jnp.logaddexp(jax.nn.log_sigmoid(a),
                         jax.nn.log_sigmoid(-a) + jnp.log(jnp.maximum(lb, LB_FLOOR)))
    logf = jnp.minimum(logf, 0.0).reshape(B, T, HG_HEADS, HG_KEY_DIM)
    kh = -jnp.expm1(logf)
    vh = hg_i.astype(F32).reshape(B, T, HG_HEADS, HG_VAL_DIM)
    o_hg, s_fin = hgrn2_chunked(qh, logf, kh, vh, s0.astype(F32))
    o_hg = rms_norm(o_hg, hg_norm) * jax.nn.silu(hg_g.astype(F32)).reshape(B, T, HG_HEADS, HG_VAL_DIM)
    merged = (jax.nn.sigmoid(gate_sb) * o_sb.reshape(B, T, SB_WIDTH)
              + jax.nn.sigmoid(gate_hg) * o_hg.reshape(B, T, HG_VAL_WIDTH).astype(x.dtype))
    x = layer_norm(ALPHA * x + jnp.einsum('bte,ed->btd', merged, w_out), ln1_g, ln1_b)
    h2 = x.reshape(B * T, D_MODEL)
    idx, wts = route(h2, w_router, router_bias)
    shared = (jax.nn.silu(h2 @ w_sg) * (h2 @ w_su)) @ w_sd
    ffn = routed_experts(h2, idx, wts, w_eg, w_eu, w_ed) + shared
    x = layer_norm(ALPHA * x + ffn.reshape(B, T, D_MODEL), ln2_g, ln2_b)
    return x, k, v, s_fin.astype(x.dtype)

def setup_inputs(seed: int = 0) -> dict:
    key = jax.random.key(seed)
    ks = jax.random.split(key, 24)

    def nrm(k, shape, scale):
        return jax.random.normal(k, shape, F32) * scale

    col_scale = jnp.asarray(np.concatenate(
        [np.full((s,), BETA if i in (2, 5) else 1.0, np.float32) for i, s in enumerate(IN_SPLITS)]))
    return {
        "x_prompt": nrm(ks[0], (BATCH, SEQ, D_MODEL), 1.0),
        "x_sample": nrm(ks[1], (DEC_BATCH, DEC_SEQ, D_MODEL), 1.0),
        "cache_sb_k": nrm(ks[2], (DEPTH, DEC_BATCH, PAST_LEN, SB_HEADS, SB_HEAD_DIM), 1.0),
        "cache_sb_v": nrm(ks[3], (DEPTH, DEC_BATCH, PAST_LEN, SB_HEADS, SB_HEAD_DIM), BETA),
        "state_hgrn": nrm(ks[4], (DEPTH, DEC_BATCH, HG_HEADS, HG_KEY_DIM, HG_VAL_DIM), 0.5),
        "ln_in_g": 1.0 + nrm(ks[5], (D_MODEL,), 0.02),
        "ln_in_b": nrm(ks[6], (D_MODEL,), 0.02),
        "w_in": nrm(ks[7], (DEPTH, D_MODEL, IN_WIDTH), D_MODEL ** -0.5) * col_scale,
        "w_out": nrm(ks[8], (DEPTH, SB_WIDTH, D_MODEL), SB_WIDTH ** -0.5 * BETA),
        "hg_norm": 1.0 + nrm(ks[9], (DEPTH, HG_VAL_DIM), 0.02),
        "hg_lb_logits": nrm(ks[10], (DEPTH, HG_KEY_WIDTH), 0.1),
        "ln1_g": 1.0 + nrm(ks[11], (DEPTH, D_MODEL), 0.02),
        "ln1_b": nrm(ks[12], (DEPTH, D_MODEL), 0.02),
        "w_router": nrm(ks[13], (DEPTH, D_MODEL, N_EXPERTS), D_MODEL ** -0.5),
        "router_bias": nrm(ks[14], (DEPTH, N_EXPERTS), 0.01),
        "w_exp_gate": nrm(ks[15], (DEPTH, N_EXPERTS, D_MODEL, D_EXPERT), D_MODEL ** -0.5),
        "w_exp_up": nrm(ks[16], (DEPTH, N_EXPERTS, D_MODEL, D_EXPERT), D_MODEL ** -0.5),
        "w_exp_down": nrm(ks[17], (DEPTH, N_EXPERTS, D_EXPERT, D_MODEL), D_EXPERT ** -0.5 * BETA),
        "w_sh_gate": nrm(ks[18], (DEPTH, D_MODEL, D_SHARED), D_MODEL ** -0.5),
        "w_sh_up": nrm(ks[19], (DEPTH, D_MODEL, D_SHARED), D_MODEL ** -0.5),
        "w_sh_down": nrm(ks[20], (DEPTH, D_SHARED, D_MODEL), D_SHARED ** -0.5 * BETA),
        "ln2_g": 1.0 + nrm(ks[21], (DEPTH, D_MODEL), 0.02),
        "ln2_b": nrm(ks[22], (DEPTH, D_MODEL), 0.02),
    }

def reference(x_prompt, x_sample, cache_sb_k, cache_sb_v, state_hgrn, ln_in_g, ln_in_b, w_in, w_out,
              hg_norm, hg_lb_logits, ln1_g, ln1_b, w_router, router_bias, w_exp_gate, w_exp_up,
              w_exp_down, w_sh_gate, w_sh_up, w_sh_down, ln2_g, ln2_b):
    lb_soft = jax.nn.softmax(hg_lb_logits.astype(F32), axis=0)
    lower_bounds = jnp.cumsum(lb_soft, axis=0) - lb_soft[0]
    xp = layer_norm(x_prompt, ln_in_g, ln_in_b)
    xs = layer_norm(x_sample, ln_in_g, ln_in_b)
    s0_prompt = jnp.zeros((x_prompt.shape[0], HG_HEADS, HG_KEY_DIM, HG_VAL_DIM), F32)
    kp, vp, sp, kd, vd, sd = [], [], [], [], [], []
    for l in range(DEPTH):
        w = (w_in[l], w_out[l], hg_norm[l], ln1_g[l], ln1_b[l], w_router[l], router_bias[l],
             w_exp_gate[l], w_exp_up[l], w_exp_down[l], w_sh_gate[l], w_sh_up[l], w_sh_down[l],
             ln2_g[l], ln2_b[l])
        xp, k1, v1, s1 = trunk_layer(xp, None, None, s0_prompt, lower_bounds[l], *w)
        xs, k2, v2, s2 = trunk_layer(xs, cache_sb_k[l], cache_sb_v[l], state_hgrn[l], lower_bounds[l], *w)
        kp.append(k1); vp.append(v1); sp.append(s1)
        kd.append(k2); vd.append(v2); sd.append(s2)
    return (xp, xs, jnp.stack(kp), jnp.stack(vp), jnp.stack(sp), jnp.stack(kd), jnp.stack(vd), jnp.stack(sd))


_drawn_inputs = setup_inputs


def setup_inputs(seed=0):
    import zlib

    import numpy as np

    out = dict(_drawn_inputs(seed))
    spreads = {}
    factors = {'cache_sb_k': 3.578, 'state_hgrn': 8.0, 'hg_norm': 3.02, 'ln2_g': 2.749, 'ln2_b': 2.828}
    for name, (base, spread) in spreads.items():
        noise = np.random.default_rng([zlib.crc32(name.encode()), seed]).standard_normal(out[name].shape)
        drawn = base * np.exp(spread * noise) if base else spread * noise
        out[name] = __import__('jax').numpy.asarray(drawn.astype(out[name].dtype))
    for name, factor in factors.items():
        out[name] = (out[name] * factor).astype(out[name].dtype)
    return out
```

```python
from contextlib import ExitStack

import concourse.bass as bass
import numpy as np
from concourse import mybir

F32 = mybir.dt.float32
I32 = mybir.dt.int32
U32 = mybir.dt.uint32
ACT = mybir.ActivationFunctionType
ALU = mybir.AluOpType
AX = mybir.AxisListType

P = 128
D = 1024
KT = D // P
SEQ, DEC, PAST = 1024, 64, 128
T = SEQ + DEC
NT = (T + P - 1) // P
HEADS = 8
HH = 4
HALVES = HEADS // HH
W512 = HH * P
NE, NGRP, TOPG, TOPK = 64, 8, 4, 8
EPG = NE // NGRP
FE = 256
ROUTE_SCALE = 2.5
NEG_BIG = -1e9
ALPHA = 2.0 ** 0.25
LN_EPS, RMS_EPS = 1e-5, 1e-6
LB_FLOOR = 1e-30
SCALE = P ** -0.5
LN_SHIFT = 50
LN2 = float(np.log(2.0))
LEVELS = [1, 2, 4, 8, 16, 32, 64]
NL = len(LEVELS)
CHUNKS = [(0, 512), (512, 512), (1024, DEC)]
(C_SQ, C_SK, C_SV, C_HQ, C_HF, C_HI, C_HG, C_GS, C_GH) = range(0, 9 * D, D)


def rows(t):
    return P if t < NT - 1 else T - P * (NT - 1)


def absolute(dve, out, x):
    return dve.scalar_tensor_tensor(out=out, in0=x, scalar=-1.0, in1=x, op0=ALU.mult, op1=ALU.max)


class Chain:

    def __init__(self, eng, sem):
        self.eng, self.sem, self.n = eng, sem, 0

    def __call__(self, ins):
        self.n += 1
        ins.then_inc(self.sem, 1)
        self.eng.wait_ge(self.sem, self.n)


class Phase:

    def __init__(self, nc, names):
        self.nc, self.stack = nc, ExitStack()
        self.sems = [self.stack.enter_context(nc.semaphore(n)) for n in names.split()]

    def __enter__(self):
        self.block_ctx = self.nc.Block()
        return self.block_ctx.__enter__(), self.sems

    def __exit__(self, *a):
        self.block_ctx.__exit__(*a)
        self.nc.all_engine_barrier()
        for s in self.sems:
            self.nc.sync.sem_clear(s)
        self.nc.all_engine_barrier()
        self.stack.close()


def layer_norm_rows(eng, ch, m, x, out, st, gg, sqrt_req, sqrt_done, n):
    for c in range(2):
        ch(eng.bn_stats(st[:m, 6 * c:6 * c + 6], x[:m, 512 * c:512 * c + 512]))
    ch(eng.bn_aggr(st[:m, 12:14], st[:m, 0:12]))
    eng.tensor_scalar(st[:m, 14:15], st[:m, 13:14], LN_EPS, None, ALU.add).then_inc(sqrt_req, 1)
    eng.wait_ge(sqrt_done, n + 1)
    ch(eng.reciprocal(st[:m, 16:17], st[:m, 15:16]))
    ch(eng.tensor_scalar(out[:m, :], x[:m, :], st[:m, 12:13], st[:m, 16:17], ALU.subtract, ALU.mult))
    ch(eng.tensor_tensor(out[:m, :], out[:m, :], gg[:m, :], ALU.mult))


def build(nc, a, o):
    ctx = ExitStack()
    with ctx:
        def sb(name, shape, dt=F32):
            return ctx.enter_context(nc.sbuf_tensor(name, shape, dt))

        def dram(name, shape, dt=F32):
            return nc.dram_tensor(name, shape, dt, kind="Internal").ap()

        xn_d = dram("xn_d", [NT * P, D])
        h2_d = dram("h2_d", [NT * P, D])
        osb_d = dram("osb_d", [HALVES, NT * P, W512])
        ohg_d = dram("ohg_d", [HALVES, NT * P, W512])

        ps = ctx.enter_context(nc.psum_tensor("ps", [P, 8, 512], F32))
        ident = sb("ident", [P, P])
        ones = sb("ones", [P, P])
        gcol = sb("gcol", [P, D])
        bcol = sb("bcol", [P, D])
        bigT = sb("bigT", [P, KT, T])
        st = sb("st", [P, 2, 20])

        constants(nc, ident, ones)
        input_norm(nc, a, xn_d, ps, ident, gcol, bcol, bigT, st)
        with ExitStack() as mix_ctx:
            def msb(name, shape, dt=F32):
                return mix_ctx.enter_context(nc.sbuf_tensor(name, shape, dt))
            mT = msb("mT", [P, HEADS, T])
            wbuf = msb("wbuf", [P, NL + 2, T])
            tri = msb("tri", [P, 3, P])
            masks = msb("masks", [P, NL + 1, P])
            lbc = msb("lbc", [P, 3, HEADS])
            w = [wbuf[:, :, :].rearrange("p a b -> p (a b)")[:, i * KT * W512:(i + 1) * KT * W512]
                 .rearrange("p (k n) -> p k n", k=KT) for i in range(2)]
            mixer_constants(nc, a, tri, masks, lbc)
            with nc.Fori(0, HALVES) as half:
                with ExitStack() as c2:
                    qT = c2.enter_context(nc.sbuf_tensor("qT", [P, HH, T], F32))
                    kT = c2.enter_context(nc.sbuf_tensor("kT", [P, HH, T], F32))
                    v = c2.enter_context(nc.sbuf_tensor("v", [P, NT, W512], F32))
                    project_qkv(nc, a, o, half, w, bigT, ps, ident, qT, kT, v)
                    attention(nc, a, half, ps, ident, tri, qT, kT, v, osb_d)
                with ExitStack() as c2:
                    qT = c2.enter_context(nc.sbuf_tensor("hqT", [P, HH, T], F32))
                    kT = c2.enter_context(nc.sbuf_tensor("hkT", [P, HH, T], F32))
                    bT = c2.enter_context(nc.sbuf_tensor("hbT", [P, HH, T], F32))
                    v = c2.enter_context(nc.sbuf_tensor("hv", [P, NT, W512], F32))
                    project_hgrn(nc, a, half, w, bigT, ps, lbc, qT, kT, bT, v)
                    hgrn(nc, a, o, half, ps, ident, masks, wbuf, qT, kT, bT, v, ohg_d)
                with ExitStack() as c2:
                    g1 = c2.enter_context(nc.sbuf_tensor("g1", [P, NT, W512], F32))
                    merge(nc, a, half, w, bigT, ps, ident, g1, osb_d, ohg_d, mT)
            output_projection(nc, a, wbuf, ps, ident, gcol, bcol, st, mT, bigT, xn_d, h2_d)
        experts_dense(nc, a, o, ps, ident, gcol, bcol, st, bigT, h2_d)


def constants(nc, ident, ones):
    with Phase(nc, "set_up") as (block, (set_up,)):
        @block.gpsimd
        def _(pool):
            pool.memset(ident[:, :], 0.0).then_inc(set_up, 1)
            pool.memset(ones[:, :], 1.0).then_inc(set_up, 1)
            pool.wait_ge(set_up, 2)
            pool.affine_select(out=ident[:, :], in_=ident[:, :], compare_op=ALU.not_equal, fill=1.0, base=0,
                               pattern=[[-1, P]], channel_multiplier=1).then_inc(set_up, 1)
            pool.wait_ge(set_up, 3)


def mixer_constants(nc, a, tri, masks, lbc):
    with Phase(nc, "memo pooled loaded dve act") as (block, (memo, pooled, loaded, dve_s, act_s)):
        @block.vector
        def _(dve):
            ch = Chain(dve, dve_s)
            dve.memset(tri[:, :, :], 1.0).then_inc(memo, 1)
            dve.memset(masks[:, :, :], 1.0).then_inc(memo, 1)
            dve.wait_ge(loaded, 16)
            lg = lbc[:, 0, :]
            ch(dve.tensor_tensor(lbc[:, 1, :], lg, lg, ALU.subtract))
            dve.wait_ge(act_s, 1)
            ch(dve.reciprocal(lbc[:, 0, :], lbc[:, 2, :]))
            ch(dve.tensor_tensor(lbc[:, 0, :], lbc[:, 0, :], lbc[:, 2, :], ALU.mult))
            ch(dve.tensor_tensor(lbc[:, 0, :], lbc[:, 0, :], lbc[:, 0, :], ALU.subtract))
            ch(dve.tensor_scalar(lbc[:, 0, :], lbc[:, 0, :], LB_FLOOR, None, ALU.max))
            ch(dve.tensor_scalar(lbc[:, 1, :], lbc[:, 0, :], -1.0, 1.0, ALU.mult, ALU.add))
            dve.wait_ge(act_s, 2)
            ch(dve.tensor_scalar(lbc[:, 0, :], lbc[:, 2, :], -LN_SHIFT * LN2, None, ALU.add))
            ch(dve.tensor_scalar(lbc[:, 2, :], lbc[:, 0, :], -1.0, None, ALU.mult))

        @block.scalar
        def _(act):
            act.wait_ge(dve_s, 1)
            act.activation(lbc[:, 2, :], lbc[:, 1, :], ACT.Exp).then_inc(act_s, 1)
            act.wait_ge(dve_s, 5)
            act.activation(lbc[:, 2, :], lbc[:, 0, :], ACT.Ln, scale=2.0 ** LN_SHIFT).then_inc(act_s, 1)

        @block.sync
        def _(sp):
            with nc.allow_non_contiguous_dma(reason="1024 numbers, once"):
                sp.dma_start(lbc[:, 0, :], a["hg_lb_logits"].rearrange("a (h c) -> c (a h)", c=P)).then_inc(loaded, 16)
            sp.wait_ge(loaded, 16)

        @block.gpsimd
        def _(pool):
            pool.wait_ge(memo, 2)
            n = 0

            def keep(ap, base, pattern, cm):
                nonlocal n
                pool.affine_select(out=ap, in_=ap, compare_op=ALU.is_ge, fill=0.0, base=base, pattern=pattern,
                                   channel_multiplier=cm).then_inc(pooled, 1)
                n += 1
                pool.wait_ge(pooled, n)

            keep(tri[:, 0, :], -1, [[1, P]], -1)
            keep(tri[:, 1, :], 0, [[-1, P]], 1)
            keep(tri[:, 2, :], -1, [[1, P]], -1)
            for i, h in enumerate(LEVELS):
                v = masks[:, i + 1, :].rearrange("p (g u) -> p g u", u=2 * h)
                keep(v, 0, [[-2 * h, P // (2 * h)], [0, 2 * h]], 1)
                keep(v, h - 1, [[2 * h, P // (2 * h)], [0, 2 * h]], -1)
                keep(v, -h, [[0, P // (2 * h)], [1, 2 * h]], 0)
            keep(masks[:, 0, :], 0, [[1, P]], -1)
            keep(masks[:, 0, :], 0, [[-1, P]], 1)


def input_norm(nc, a, xn_d, ps, ident, gcol, bcol, xT, st):
    with ExitStack() as c:
        xin = c.enter_context(nc.sbuf_tensor("xin", [P, 2, D], F32))
        y = c.enter_context(nc.sbuf_tensor("y", [P, 2, D], F32))
        with Phase(nc, "par_in x_in0 x_in1 dve_s var_ready root_ready y_ready t_done t_act stored0 stored1") as (block, (
                par_in, x_in0, x_in1, dve_s, var_ready, root_ready, y_ready, t_done, t_act, stored0, stored1)):
            x_in, stored = (x_in0, x_in1), (stored0, stored1)

            @block.sync
            def _(sp):
                sp.dma_start(gcol[:, :], a["ln_in_g"].partition_broadcast(P)).then_inc(par_in, 16)
                sp.dma_start(bcol[:, :], a["ln_in_b"].partition_broadcast(P)).then_inc(par_in, 16)
                for t in range(NT):
                    m = rows(t)
                    if t >= 2:
                        sp.wait_ge(y_ready, t - 1)
                    src = a["x_prompt"][0, t * P:t * P + m, :] if t < NT - 1 else a["x_sample"][0, :, :]
                    sp.dma_start(xin[:m, t % 2, :], src).then_inc(x_in[t % 2], 16)

            @block.vector
            def _(dve):
                ch = Chain(dve, dve_s)
                dve.wait_ge(par_in, 32)
                for t in range(NT):
                    m = rows(t)
                    dve.wait_ge(x_in[t % 2], 16 * (t // 2 + 1))
                    if t >= 2:
                        dve.wait_ge(stored[t % 2], 16 * (t // 2))
                        dve.wait_ge(t_done, t - 1)
                    layer_norm_rows(dve, ch, m, xin[:, t % 2, :], y[:, t % 2, :], st[:, t % 2, :], gcol, var_ready, root_ready, t)
                    dve.tensor_tensor(y[:m, t % 2, :], y[:m, t % 2, :], bcol[:m, :], ALU.add).then_inc(y_ready, 1)

            @block.scalar
            def _(act):
                for t in range(NT):
                    m = rows(t)
                    act.wait_ge(var_ready, t + 1)
                    act.activation(st[:m, t % 2, 15:16], st[:m, t % 2, 14:15], ACT.Sqrt).then_inc(root_ready, 1)
                    act.wait_ge(y_ready, t + 1)
                    act.dma_start(xn_d[t * P:t * P + m, :], y[:m, t % 2, :]).then_inc(stored[t % 2], 16)
                    act.wait_ge(t_done, t + 1)
                    for b in range(2):
                        act.activation(xT[:, 4 * b:4 * b + 4, t * P:t * P + m],
                                       ps[:, 2 * (t % 2) + b, :].rearrange("p (k n) -> p k n", k=4)[:, :, 0:m],
                                       ACT.Copy).then_inc(t_act, 1)
                act.wait_ge(stored[0], 16 * 5)
                act.wait_ge(stored[1], 16 * 4)

            @block.tensor
            def _(pe):
                for t in range(NT):
                    m = rows(t)
                    pe.wait_ge(y_ready, t + 1)
                    if t >= 2:
                        pe.wait_ge(t_act, 2 * (t - 1))
                    for k in range(KT):
                        mm = pe.transpose(ps[:, 2 * (t % 2) + k // 4, (k % 4) * P:(k % 4) * P + m],
                                          y[:m, t % 2, k * P:(k + 1) * P], ident[:m, :m])
                    mm.then_inc(t_done, 1)


def load_weights(eng, nc, a, w, half, cols, w_in, mm_done, freed):
    for g, c0 in enumerate(cols):
        if g >= 2:
            eng.wait_ge(mm_done, freed[g - 2])
        src = a["w_in"][0].rearrange("(k p) n -> p k n", p=P)[:, :, bass.ds(half * W512 + c0, W512)]
        eng.dma_start(w[g % 2], src).then_inc(w_in[g % 2], 16)


class Steps:

    def __init__(self, forms):
        self.list = []
        self.last = []
        for g, f in enumerate(forms):
            if f == "T":
                self.list += [(g, f, (e, c)) for e in range(HH) for c in range(3)]
            else:
                self.list += [(g, f, t) for t in range(NT)]
            self.last.append(len(self.list))


def products(pe, steps, w, xT, ps, banks, w_in, mm_done, read_done):
    seen = set()
    for n, (g, f, i) in enumerate(steps.list):
        if g not in seen:
            seen.add(g)
            pe.wait_ge(w_in[g % 2], 16 * (g // 2 + 1))
        if n >= banks:
            e = n - banks
            pe.wait_ge(read_done[e % 2], e // 2 + 1)
        for k in range(KT):
            if f == "T":
                c0, cw = CHUNKS[i[1]]
                mm = pe.matmul(ps[:, n % banks, 0:cw], w[g % 2][:, k, i[0] * P:(i[0] + 1) * P],
                               xT[:, k, c0:c0 + cw], start=k == 0, stop=k == KT - 1)
            else:
                m = rows(i)
                mm = pe.matmul(ps[:m, n % banks, :], xT[:, k, i * P:i * P + m], w[g % 2][:, k, :],
                               start=k == 0, stop=k == KT - 1)
        mm.then_inc(mm_done, 1)


def project_qkv(nc, a, o, half, w, xT, ps, ident, qT, kT, v):
    cols = (C_SQ, C_SK, C_SV)
    steps = Steps("TTR")
    BANKS = 6
    with ExitStack() as c:
        krow = c.enter_context(nc.sbuf_tensor("krow", [P, 2, W512], F32))
        with Phase(nc, "w_in0 w_in1 mm_done act_read dve_read k_done k_copied v_out kout0 kout1") as (block, (
                w_in0, w_in1, mm_done, act_read, dve_read, k_done, k_copied, v_out, kout0, kout1)):
            w_in, read, kout = (w_in0, w_in1), (act_read, dve_read), (kout0, kout1)

            @block.sync
            def _(sp):
                load_weights(sp, nc, a, w, half, cols, w_in, mm_done, steps.last)
                hs = bass.ds(half * HH, HH)
                for t in range(NT):
                    m = rows(t)
                    sp.wait_ge(k_copied, t + 1)
                    dst = o[2][0, 0, t * P:t * P + m, hs, :] if t < NT - 1 else o[5][0, 0, :, hs, :]
                    sp.dma_start(dst, krow[:m, t % 2, :].rearrange("p (h c) -> p h c", h=HH)).then_inc(kout[t % 2], 16)
                sp.wait_ge(act_read, (len(steps.list) + 1) // 2)
                sp.wait_ge(dve_read, len(steps.list) // 2)
                for t in range(NT):
                    m = rows(t)
                    dst = o[3][0, 0, t * P:t * P + m, hs, :] if t < NT - 1 else o[6][0, 0, :, hs, :]
                    sp.dma_start(dst, v[:m, t, :].rearrange("p (h c) -> p h c", h=HH)).then_inc(v_out, 16)
                sp.wait_ge(v_out, 16 * NT)
                sp.wait_ge(kout[0], 16 * 5)
                sp.wait_ge(kout[1], 16 * 4)

            @block.tensor
            def _(pe):
                products(pe, steps, w, xT, ps, BANKS, w_in, mm_done, read)
                pe.wait_ge(act_read, (steps.last[1] + 1) // 2)
                pe.wait_ge(dve_read, steps.last[1] // 2)
                for t in range(NT):
                    m = rows(t)
                    if t >= 2:
                        pe.wait_ge(k_copied, t - 1)
                    for h in range(HH):
                        mm = pe.transpose(ps[:m, BANKS + t % 2, h * P:(h + 1) * P], kT[:, h, t * P:t * P + m], ident[:, :])
                    mm.then_inc(k_done, 1)

            def copy_out(eng, copy, me):
                for n, (g, f, i) in enumerate(steps.list):
                    if n % 2 != me:
                        continue
                    eng.wait_ge(mm_done, n + 1)
                    if f == "T":
                        c0, cw = CHUNKS[i[1]]
                        dst = (qT, kT)[g][:, i[0], c0:c0 + cw]
                        src = ps[:, n % BANKS, 0:cw]
                    else:
                        m = rows(i)
                        dst, src = v[:m, i, :], ps[:m, n % BANKS, :]
                    copy(dst, src).then_inc(read[me], 1)

            @block.scalar
            def _(act):
                copy_out(act, lambda d, s: act.activation(d, s, ACT.Copy), 0)

            @block.vector
            def _(dve):
                copy_out(dve, dve.tensor_copy, 1)
                for t in range(NT):
                    m = rows(t)
                    dve.wait_ge(k_done, t + 1)
                    if t >= 2:
                        dve.wait_ge(kout[t % 2], 16 * (t // 2))
                    dve.tensor_copy(krow[:m, t % 2, :], ps[:m, BANKS + t % 2, :]).then_inc(k_copied, 1)


def attention_units():
    def tile(i):
        js = list(range(i, -1, -1)) if i < NT - 1 else [i, -1]
        return [(i, j, j == js[0], j == js[-1]) for j in js]
    streams = [sum((tile(i) for i in s), []) for s in ((7, 5, 4), (6, 3, 2, 1, 0, 8))]
    out = []
    assert len(streams[0]) == len(streams[1])
    for n in range(len(streams[0])):
        for s in range(2):
            out.append((s, *streams[s][n]))
    return out


def attention(nc, a, half, ps, ident, tri, qT, kT, v, osb_d):
    units = attention_units()
    NU = len(units)
    tiles = {}
    for s in range(2):
        for n, i in enumerate([u[1] for u in units if u[0] == s and u[4]]):
            tiles[s, i] = n
    seq = {}
    done_before = [0, 0]
    for u in units:
        seq[u] = done_before[u[0]]
        done_before[u[0]] += 1

    with ExitStack() as c:
        def sb(name, shape):
            return c.enter_context(nc.sbuf_tensor(name, shape, F32))
        ckr = sb("ckr", [PAST, W512])
        ckT = sb("ckT", [P, HH, PAST])
        cv = sb("cv", [PAST, W512])
        z = sb("z", [P, 2, W512])
        sp_ = sb("sp_", [P, 2, W512])
        arg = sb("arg", [P, 2, W512])
        ob = sb("ob", [P, 2, W512])
        Z, C, O, X = (0, 1), (2, 3), (4, 5), 6
        with Phase(nc, "cache_in ct_done ct_copied z_done z_copied abs_done e_done l_done sp_done sp_masked c_done "
                       "arg_done w_done w_masked c_next o_done o_copied out0 out1 dve_s") as (block, (
                cache_in, ct_done, ct_copied, z_done, z_copied, abs_done, e_done, l_done, sp_done, sp_masked, c_done,
                arg_done, w_done, w_masked, c_next, o_done, o_copied, out0, out1, dve_s)):
            outs = (out0, out1)
            diag = [n for n, u in enumerate(units) if u[3]]
            finals = [n for n, u in enumerate(units) if u[4]]

            def shape(u):
                m = rows(u[1])
                return m, (m if u[1] == NT - 1 and u[2] >= 0 else P)

            def view(ap, m):
                return ap[:, 0:HH * m].rearrange("p (h t) -> p h t", h=HH)

            @block.sync
            def _(sp):
                hs = bass.ds(half * HH, HH)
                sp.dma_start(ckr[:, :].rearrange("p (h c) -> p h c", h=HH), a["cache_sb_k"][0, 0, :, hs, :]).then_inc(cache_in, 16)
                sp.dma_start(cv[:, :].rearrange("p (h c) -> p h c", h=HH), a["cache_sb_v"][0, 0, :, hs, :]).then_inc(cache_in, 16)
                for n, f in enumerate(finals):
                    s, i = units[f][:2]
                    m = rows(i)
                    sp.wait_ge(o_copied, n + 1)
                    sp.dma_start(osb_d[bass.ds(half, 1), i * P:i * P + m, :].rearrange("a p n -> (a p) n"),
                                 ob[:m, n % 2, :]).then_inc(outs[n % 2], 16)
                sp.wait_ge(out0, 16 * 5)
                sp.wait_ge(out1, 16 * 4)

            @block.tensor
            def _(pe):
                pe.wait_ge(cache_in, 32)
                for h in range(HH):
                    mm = pe.transpose(ps[:, X, h * P:(h + 1) * P], ckr[:, h * P:(h + 1) * P], ident[:, :])
                mm.then_inc(ct_done, 1)
                pe.wait_ge(ct_copied, 1)

                def scores(n):
                    u = units[n]
                    m, kr = shape(u)
                    if n >= 2:
                        pe.wait_ge(z_copied, n - 1)
                    for h in range(HH):
                        keys = ckT[:, h, :] if u[2] < 0 else kT[:, h, u[2] * P:u[2] * P + kr]
                        mm = pe.matmul(ps[:kr, Z[n % 2], h * m:(h + 1) * m], keys, qT[:, h, u[1] * P:u[1] * P + m],
                                       start=True, stop=True)
                    mm.then_inc(z_done, 1)

                def sums(n):
                    u = units[n]
                    m, kr = shape(u)
                    pe.wait_ge(sp_done, n + 1)
                    if u[3]:
                        pe.wait_ge(sp_masked, diag.index(n) + 1)
                        before = [k for k in range(n) if units[k][0] == u[0]]
                        if before:
                            pe.wait_ge(arg_done, before[-1] + 1)
                    pe.matmul(ps[:, C[u[0]], 0:HH * m], tri[:kr, 1, :], sp_[:kr, n % 2, 0:HH * m], start=u[3], stop=True,
                              skip_group_check=True).then_inc(c_done, 1)

                def carry(n):
                    u = units[n]
                    m, kr = shape(u)
                    pe.wait_ge(arg_done, n + 1)
                    mm = None
                    if not u[4]:
                        mm = pe.matmul(ps[:, C[u[0]], 0:HH * m], tri[:kr, 2, :], sp_[:kr, n % 2, 0:HH * m], start=False,
                                       stop=True, skip_group_check=True)
                        mm.then_inc(c_next, 1)
                    else:
                        pe.sem_inc(c_next, 1)

                def values(n):
                    u = units[n]
                    m, kr = shape(u)
                    pe.wait_ge(w_done, n + 1)
                    if u[3]:
                        pe.wait_ge(w_masked, diag.index(n) + 1)
                        k = tiles[u[0], u[1]]
                        if k:
                            f = [x for x in finals if x < n and units[x][0] == u[0]]
                            pe.wait_ge(o_copied, finals.index(f[-1]) + 1)
                    for h in range(HH):
                        vals = cv[:, h * P:(h + 1) * P] if u[2] < 0 else v[:kr, u[2], h * P:(h + 1) * P]
                        mm = pe.matmul(ps[:m, O[u[0]], h * P:(h + 1) * P], arg[:kr, n % 2, h * m:(h + 1) * m], vals,
                                       start=u[3] and h == 0, stop=u[4], skip_group_check=True)
                    mm.then_inc(o_done, 1)

                scores(0)
                for n in range(NU + 1):
                    if n + 1 < NU:
                        scores(n + 1)
                    if n < NU:
                        sums(n)
                    if n >= 1:
                        carry(n - 1)
                        values(n - 1)

            @block.scalar
            def _(act):
                act.wait_ge(ct_done, 1)
                act.activation(ckT[:, :, :], ps[:, X, :].rearrange("p (h c) -> p h c", h=HH), ACT.Copy).then_inc(ct_copied, 1)

                def front(n):
                    u = units[n]
                    m, kr = shape(u)
                    w_ = HH * m
                    act.wait_ge(z_done, n + 1)
                    if n >= 2:
                        act.wait_ge(arg_done, n - 1)
                    act.activation(z[:kr, n % 2, 0:w_], ps[:kr, Z[n % 2], 0:w_], ACT.Copy, scale=SCALE).then_inc(z_copied, 1)
                    if n >= 2:
                        act.wait_ge(c_next, n - 1)
                    act.wait_ge(abs_done, n + 1)
                    act.activation(sp_[:kr, n % 2, 0:w_], sp_[:kr, n % 2, 0:w_], ACT.Exp, scale=-1.0).then_inc(e_done, 1)
                    act.wait_ge(e_done, n + 1)
                    act.activation(sp_[:kr, n % 2, 0:w_], sp_[:kr, n % 2, 0:w_], ACT.Ln, bias=1.0).then_inc(l_done, 1)

                def back(n):
                    u = units[n]
                    m, kr = shape(u)
                    w_ = HH * m
                    act.wait_ge(arg_done, n + 1)
                    act.activation(arg[:kr, n % 2, 0:w_], arg[:kr, n % 2, 0:w_], ACT.Exp).then_inc(w_done, 1)

                for n in range(NU + 1):
                    if n < NU:
                        front(n)
                    if n >= 1:
                        back(n - 1)

            @block.vector
            def _(dve):
                ch = Chain(dve, dve_s)

                def front(n):
                    u = units[n]
                    m, kr = shape(u)
                    w_ = HH * m
                    dve.wait_ge(z_copied, n + 1)
                    if n >= 2:
                        dve.wait_ge(c_next, n - 1)
                    absolute(dve, sp_[:kr, n % 2, 0:w_], z[:kr, n % 2, 0:w_]).then_inc(abs_done, 1)

                def middle(n):
                    u = units[n]
                    m, kr = shape(u)
                    w_ = HH * m
                    dve.wait_ge(l_done, n + 1)
                    dve.scalar_tensor_tensor(out=sp_[:kr, n % 2, 0:w_], in0=z[:kr, n % 2, 0:w_], scalar=0.0,
                                             in1=sp_[:kr, n % 2, 0:w_], op0=ALU.max, op1=ALU.add).then_inc(sp_done, 1)

                def back(n):
                    u = units[n]
                    m, kr = shape(u)
                    w_ = HH * m
                    dve.wait_ge(c_done, n + 1)
                    if n >= 2:
                        dve.wait_ge(o_done, n - 1)
                    if u[3]:
                        ch(dve.tensor_tensor(arg[:kr, n % 2, 0:w_], z[:kr, n % 2, 0:w_], ps[:kr, C[u[0]], 0:w_], ALU.subtract))
                        dve.tensor_scalar(arg[:kr, n % 2, 0:w_], arg[:kr, n % 2, 0:w_], 0.0, None, ALU.min).then_inc(arg_done, 1)
                    else:
                        dve.tensor_tensor(arg[:kr, n % 2, 0:w_], z[:kr, n % 2, 0:w_], ps[:kr, C[u[0]], 0:w_],
                                          ALU.subtract).then_inc(arg_done, 1)

                def outputs(n):
                    if n < 0 or not units[n][4]:
                        return
                    k = finals.index(n)
                    m = rows(units[n][1])
                    dve.wait_ge(o_done, n + 1)
                    if k >= 2:
                        dve.wait_ge(outs[k % 2], 16 * (k // 2))
                    dve.tensor_copy(ob[:m, k % 2, :], ps[:m, O[units[n][0]], :]).then_inc(o_copied, 1)

                front(0)
                for n in range(NU):
                    middle(n)
                    if n + 1 < NU:
                        front(n + 1)
                    back(n)
                    outputs(n - 1)
                outputs(NU - 1)

            @block.gpsimd
            def _(pool):
                for k, n in enumerate(diag):
                    u = units[n]
                    m, kr = shape(u)
                    below = tri[:kr, 0:1, 0:m].to_broadcast([kr, HH, m])
                    pool.wait_ge(sp_done, n + 1)
                    s_ = view(sp_[:kr, n % 2, :], m)
                    pool.tensor_tensor(s_, s_, below, ALU.mult).then_inc(sp_masked, 1)
                    pool.wait_ge(w_done, n + 1)
                    w_ = view(arg[:kr, n % 2, :], m)
                    pool.tensor_tensor(w_, w_, below, ALU.mult).then_inc(w_masked, 1)


def project_hgrn(nc, a, half, w, xT, ps, lbc, qT, kT, bT, v):
    cols = (C_HF, C_HQ, C_HI)
    steps = Steps("TTR")
    BANKS = 8
    with ExitStack() as c:
        tmp = c.enter_context(nc.sbuf_tensor("ptmp", [P, T], F32))
        keep = c.enter_context(nc.sbuf_tensor("pkeep", [P, T], F32))
        low = c.enter_context(nc.sbuf_tensor("plow", [P, T], F32))
        with Phase(nc, "w_in0 w_in1 mm_done act_read dve_read dve_s act_s") as (block, (
                w_in0, w_in1, mm_done, act_read, dve_read, dve_s, act_s)):
            w_in, read = (w_in0, w_in1), (act_read, dve_read)
            NS = len(steps.list)

            @block.sync
            def _(sp):
                load_weights(sp, nc, a, w, half, cols, w_in, mm_done, steps.last)

            @block.tensor
            def _(pe):
                products(pe, steps, w, xT, ps, BANKS, w_in, mm_done, read)

            def copy_out(eng, copy, me, lo, hi):
                for n, (g, f, i) in enumerate(steps.list):
                    if n % 2 != me or not lo <= n < hi:
                        continue
                    eng.wait_ge(mm_done, n + 1)
                    if f == "T":
                        c0, cw = CHUNKS[i[1]]
                        dst = (bT, qT)[g][:, i[0], c0:c0 + cw]
                        src = ps[:, n % BANKS, 0:cw]
                    else:
                        m = rows(i)
                        dst, src = v[:m, i, :], ps[:m, n % BANKS, :]
                    copy(dst, src).then_inc(read[me], 1)

            TURNS = 14

            @block.scalar
            def _(act):
                copy_out(act, lambda d, s: act.activation(d, s, ACT.Copy), 0, 0, NS)
                n = 0

                def turn(*args, **kw):
                    nonlocal n
                    act.activation(*args, **kw).then_inc(act_s, 1)
                    n += 1
                    act.wait_ge(act_s, n)

                for h in range(HH):
                    base = TURNS * h
                    act.wait_ge(dve_s, base + 2)
                    turn(tmp[:, :], tmp[:, :], ACT.Exp, scale=-1.0)
                    turn(tmp[:, :], tmp[:, :], ACT.Ln, bias=1.0)
                    act.wait_ge(dve_s, base + 4)
                    turn(kT[:, h, :], kT[:, h, :], ACT.Exp)
                    act.wait_ge(dve_s, base + 7)
                    turn(tmp[:, :], tmp[:, :], ACT.Exp, scale=-1.0)
                    turn(tmp[:, :], tmp[:, :], ACT.Ln, bias=1.0)
                    act.wait_ge(dve_s, base + 11)
                    turn(tmp[:, :], qT[:, h, :], ACT.Exp, scale=-1.0)

            @block.vector
            def _(dve):
                ch = Chain(dve, dve_s)
                copy_out(dve, dve.tensor_copy, 1, 0, NS)
                dve.wait_ge(act_read, (NS + 1) // 2)
                dve.memset(keep[:, :], 1.0).then_inc(dve_read, 1)
                dve.wait_ge(dve_read, NS // 2 + 1)
                dve.memset(keep[:, 0:T:P], 0.0).then_inc(dve_read, 1)
                dve.wait_ge(dve_read, NS // 2 + 2)
                for h in range(HH):
                    A = bT[:, h, :]
                    L = lbc[:, 0, bass.ds(half * HH + h, 1)]
                    NLb = lbc[:, 2, bass.ds(half * HH + h, 1)]
                    om = lbc[:, 1, bass.ds(half * HH + h, 1)]
                    na = 6 * h
                    ch(absolute(dve, tmp[:, :], A))
                    ch(dve.tensor_scalar(kT[:, h, :], A, 0.0, None, ALU.min))
                    dve.wait_ge(act_s, na + 2)
                    ch(dve.tensor_tensor(tmp[:, :], kT[:, h, :], tmp[:, :], ALU.subtract))
                    ch(dve.tensor_tensor(kT[:, h, :], tmp[:, :], A, ALU.subtract))
                    ch(dve.tensor_scalar(A, A, NLb, None, ALU.add))
                    ch(dve.scalar_tensor_tensor(out=low[:, :], in0=A, scalar=0.0, in1=tmp[:, :], op0=ALU.min,
                                                op1=ALU.subtract))
                    ch(absolute(dve, tmp[:, :], A))
                    dve.wait_ge(act_s, na + 5)
                    ch(dve.tensor_tensor(tmp[:, :], tmp[:, :], low[:, :], ALU.subtract))
                    ch(dve.tensor_scalar(tmp[:, :], tmp[:, :], 0.0, None, ALU.min))
                    ch(dve.tensor_tensor_scan(A, keep[:, :], tmp[:, :], 0.0, ALU.mult, ALU.add))
                    ch(dve.tensor_scalar(kT[:, h, :], kT[:, h, :], om, None, ALU.mult))
                    dve.wait_ge(act_s, na + 6)
                    ch(dve.tensor_scalar(tmp[:, :], tmp[:, :], 1.0, None, ALU.add))
                    ch(dve.reciprocal(tmp[:, :], tmp[:, :]))
                    ch(dve.tensor_tensor(qT[:, h, :], qT[:, h, :], tmp[:, :], ALU.mult))


def hgrn(nc, a, o, half, ps, ident, masks, x, qT, kT, bT, v, ohg_d):
    PARTS = [(0, 512), (512, T - 512)]
    parts = [(h, *p) for h in range(HH) for p in PARTS]
    chunks = []
    for n, (h, c0, cw) in enumerate(parts):
        for c in range(c0, c0 + cw, P):
            chunks.append((n, h, c, min(P, T - c), c // P))
    NC = len(chunks)
    last_of = {n: max(i for i, k in enumerate(chunks) if k[0] == n) for n in range(len(parts))}
    first_of = {n: min(i for i, k in enumerate(chunks) if k[0] == n) for n in range(len(parts))}
    PER = 2 * NL + 2
    with ExitStack() as c:
        def sb(name, shape):
            return c.enter_context(nc.sbuf_tensor(name, shape, F32))
        pm = sb("pm", [P, 2, NL + 1, P])
        aT = sb("aT", [P, 2, P])
        ke = sb("ke", [P, 2, P])
        orow = sb("orow", [P, 2, P])
        eb = sb("eb", [P, HH, NT])
        S = sb("S", [P, 4, P])
        O, KE, SU = (4, 5), 6, 7
        with Phase(nc, "zeroed s_in diff_done exp_done eb_done x_done p_done masked a_done o_done o_copied o_out0 o_out1 "
                       "ke_done ke_copied su_done s_done s_out") as (block, (
                zeroed, s_in, diff_done, exp_done, eb_done, x_done, p_done, masked, a_done, o_done, o_copied, o_out0, o_out1,
                ke_done, ke_copied, su_done, s_done, s_out)):
            o_out = (o_out0, o_out1)

            def src_state(k):
                return 2 if k[4] == NT - 1 else k[4] % 2

            def dst_state(k):
                return 3 if k[4] == NT - 1 else (k[4] + 1) % 2

            def halves(n):
                h, c0, cw = parts[n]
                out = []
                for i, hw in enumerate(LEVELS):
                    w_ = cw // (2 * hw) * (2 * hw)
                    for side in range(2):
                        out.append((i, side, hw, c0, w_))
                return out

            def seg(ap, c0, w_, hw, side):
                return ap[:, c0:c0 + w_].rearrange("p (g u) -> p g u", u=2 * hw)[:, :, side * hw:side * hw + hw]

            def ends(c0, cw):
                out = [(c0, cw // P * P, P)]
                if cw % P:
                    out.append((c0 + cw // P * P, cw % P, cw % P))
                return out

            @block.sync
            def _(sp):
                for h in range(HH):
                    if h >= 1:
                        sp.wait_ge(s_done, NT * h)
                    sp.dma_start(S[:, 2, :], a["state_hgrn"][0, 0, bass.ds(half * HH + h, 1), :, :]
                                 .rearrange("a c v -> (a c) v")).then_inc(s_in, 16)

            @block.gpsimd
            def _(pool):
                for n, (h, c0, cw) in enumerate(parts):
                    base = n * (NL + 2)
                    for i, side, hw, b0, w_ in halves(n):
                        if side == 0:
                            pool.wait_ge(exp_done, base + i + 1)
                        q = (kT, qT)[side][:, h, :]
                        xs = seg(x[:, i, :], b0, w_, hw, side)
                        pool.tensor_tensor(xs, xs, seg(q, b0, w_, hw, side), ALU.mult).then_inc(x_done, 1)
                    for i, q in ((NL, qT), (NL + 1, kT)):
                        pool.wait_ge(exp_done, base + i + 1)
                        xs = x[:, i, c0:c0 + cw]
                        pool.tensor_tensor(xs, xs, q[:, h, c0:c0 + cw], ALU.mult).then_inc(x_done, 1)

            @block.scalar
            def _(act):
                for h in range(HH):
                    act.activation(eb[:, h, 0:NT - 1], bT[:, h, P - 1:SEQ:P], ACT.Exp).then_inc(eb_done, 1)
                    act.activation(eb[:, h, NT - 1:NT], bT[:, h, T - 1:T], ACT.Exp).then_inc(eb_done, 1)

                def exps(n):
                    h, c0, cw = parts[n]
                    for i in range(NL + 2):
                        w_ = cw // (2 * LEVELS[i]) * (2 * LEVELS[i]) if i < NL else cw
                        act.wait_ge(diff_done, 2 * (NL + 2) * n + 2 * (i + 1))
                        act.activation(x[:, i, c0:c0 + w_], x[:, i, c0:c0 + w_], ACT.Exp).then_inc(exp_done, 1)

                def copies(j):
                    k = chunks[j]
                    m = k[3]
                    act.wait_ge(ke_done, j + 1)
                    if j >= 2:
                        act.wait_ge(su_done, j - 1)
                    act.activation(ke[:m, j % 2, :], ps[:m, KE, 0:P], ACT.Copy).then_inc(ke_copied, 1)
                    act.wait_ge(o_done, j + 1)
                    if j >= 2:
                        act.wait_ge(o_out[j % 2], 16 * (j // 2))
                    act.activation(orow[:m, j % 2, :], ps[:m, O[j % 2], 0:P], ACT.Copy).then_inc(o_copied, 1)
                    act.wait_ge(o_copied, j + 1)
                    act.dma_start(ohg_d[bass.ds(half, 1), k[4] * P:k[4] * P + m, k[1] * P:(k[1] + 1) * P]
                                  .rearrange("a p n -> (a p) n"), orow[:m, j % 2, :]).then_inc(o_out[j % 2], 16)

                exps(0)
                for n in range(len(parts)):
                    if n + 1 < len(parts):
                        exps(n + 1)
                    for j in range(first_of[n], last_of[n] + 1):
                        copies(j)
                    if n % 2:
                        h = parts[n][0]
                        act.wait_ge(s_done, NT * (h + 1))
                        hd = bass.ds(half * HH + h, 1)
                        act.dma_start(o[4][0, 0, hd, :, :].rearrange("a c v -> (a c) v"), S[:, 0, :]).then_inc(s_out, 16)
                        act.dma_start(o[7][0, 0, hd, :, :].rearrange("a c v -> (a c) v"), S[:, 3, :]).then_inc(s_out, 16)
                act.wait_ge(s_out, 32 * HH)
                act.wait_ge(o_out0, 16 * (NC // 2))
                act.wait_ge(o_out1, 16 * (NC // 2))

            @block.vector
            def _(dve):
                def diffs(n):
                    h, c0, cw = parts[n]
                    b = bT[:, h, :]
                    if n >= 2:
                        dve.wait_ge(o_done, last_of[n - 2] + 1)
                        dve.wait_ge(ke_done, last_of[n - 2] + 1)
                        dve.wait_ge(p_done, last_of[n - 2] + 1)
                    for i, side, hw, b0, w_ in halves(n):
                        mid = b[:, b0:b0 + w_].rearrange("p (g u) -> p g u", u=2 * hw)[:, :, hw - 1:hw] \
                            .to_broadcast([P, w_ // (2 * hw), hw])
                        bs, xs = seg(b, b0, w_, hw, side), seg(x[:, i, :], b0, w_, hw, side)
                        dve.tensor_tensor(xs, *((mid, bs) if side == 0 else (bs, mid)), ALU.subtract).then_inc(diff_done, 1)
                    dve.tensor_copy(x[:, NL, c0:c0 + cw], b[:, c0:c0 + cw]).then_inc(diff_done, 2)
                    es = ends(c0, cw)
                    for e0, ew, u in es:
                        g = ew // u
                        bs = b[:, e0:e0 + ew].rearrange("p (g u) -> p g u", u=u)
                        xs = x[:, NL + 1, e0:e0 + ew].rearrange("p (g u) -> p g u", u=u)
                        dve.tensor_tensor(xs, bs[:, :, u - 1:u].to_broadcast([P, g, u]), bs, ALU.subtract) \
                            .then_inc(diff_done, 2 // len(es))

                def scores(j):
                    n, h, c0, m, t = chunks[j]
                    s = NL + 1 if m == P else NL
                    dve.wait_ge(p_done, j + 1)
                    if j >= 2:
                        dve.wait_ge(a_done, j - 1)
                    pp = ps[:m, 2 * (j % 2):2 * (j % 2) + 2, :].rearrange("p b (l t) -> p (b l) t", l=4)[:, 0:s, 0:m]
                    dve.tensor_tensor(pm[:m, j % 2, 0:s, 0:m], pp, masks[:m, 0:s, 0:m], ALU.mult).then_inc(masked, 1)
                    dve.wait_ge(masked, j + 1)
                    if j >= 2:
                        dve.wait_ge(o_done, j - 1)
                    dve.tensor_reduce(aT[:m, j % 2, 0:m], pm[:m, j % 2, 0:s, 0:m].rearrange("p l t -> p t l"), AX.X,
                                      ALU.add).then_inc(a_done, 1)

                def state(j):
                    k = chunks[j]
                    dve.wait_ge(su_done, j + 1)
                    dve.wait_ge(o_done, max(j - 1, 1))
                    if j >= 1:
                        dve.wait_ge(s_done, j)
                    if k[4] == 0:
                        dve.wait_ge(eb_done, 2 * HH)
                    if k[4] == NT - 1:
                        dve.wait_ge(s_in, 16 * (k[1] + 1))
                    dve.scalar_tensor_tensor(out=S[:, dst_state(k), :], in0=S[:, src_state(k), :],
                                             scalar=eb[:, k[1], k[4]:k[4] + 1], in1=ps[:, SU, 0:P], op0=ALU.mult,
                                             op1=ALU.add).then_inc(s_done, 1)

                diffs(0)
                for n in range(len(parts)):
                    if n + 1 < len(parts):
                        diffs(n + 1)
                    for j in range(first_of[n], last_of[n] + 1):
                        if chunks[j][4] == 0:
                            if chunks[j][1]:
                                dve.wait_ge(s_out, 32 * chunks[j][1])
                            dve.memset(S[:, 0, :], 0.0).then_inc(zeroed, 1)
                            dve.wait_ge(zeroed, chunks[j][1] + 1)
                        scores(j)
                        state(j)

            @block.tensor
            def _(pe):
                def products(j):
                    n, h, c0, m, t = chunks[j]
                    if j == first_of[n]:
                        pe.wait_ge(x_done, PER * (n + 1))
                    if j >= 2:
                        pe.wait_ge(masked, j - 1)
                    b0 = 2 * (j % 2)
                    pe.matmul(ps[:m, b0, 0:m], kT[:, h, c0:c0 + m], qT[:, h, c0:c0 + m], start=True, stop=True)
                    for i in range(NL if m == P else NL - 1):
                        xs = x[:, i, c0:c0 + m]
                        mm = pe.matmul(ps[:m, b0 + (i + 1) // 4, (i + 1) % 4 * P:(i + 1) % 4 * P + m], xs, xs,
                                       start=True, stop=True)
                    mm.then_inc(p_done, 1)
                    if j >= 1:
                        pe.wait_ge(ke_copied, j)
                    pe.transpose(ps[:m, KE, 0:P], x[:, NL + 1, c0:c0 + m], ident[:, :]).then_inc(ke_done, 1)

                def outputs(j):
                    k = chunks[j]
                    n, h, c0, m, t = k
                    vals = v[:m, t, h * P:(h + 1) * P]
                    pe.wait_ge(a_done, j + 1)
                    if j >= 2:
                        pe.wait_ge(o_copied, j - 1)
                    pe.matmul(ps[:m, O[j % 2], 0:P], aT[:m, j % 2, 0:m], vals, start=True, stop=False)
                    if t == 0:
                        pe.wait_ge(zeroed, h + 1)
                    if t == NT - 1:
                        pe.wait_ge(s_in, 16 * (h + 1))
                    elif j >= 1:
                        pe.wait_ge(s_done, j)
                    pe.matmul(ps[:m, O[j % 2], 0:P], x[:, NL, c0:c0 + m], S[:, src_state(k), :], start=False,
                              stop=True).then_inc(o_done, 1)
                    pe.wait_ge(ke_copied, j + 1)
                    if j >= 1:
                        pe.wait_ge(s_done, j)
                    pe.matmul(ps[:, SU, 0:P], ke[:m, j % 2, :], vals, start=True, stop=True).then_inc(su_done, 1)

                products(0)
                for j in range(NC):
                    if j + 1 < NC and chunks[j + 1][0] == chunks[j][0]:
                        products(j + 1)
                        outputs(j)
                    else:
                        outputs(j)
                        if j + 1 < NC:
                            products(j + 1)


def merge(nc, a, half, w, xT, ps, ident, g1, osb_d, ohg_d, mT):
    cols = (C_HG, C_GH, C_GS)
    steps = Steps("RRR")
    BANKS = 6
    with ExitStack() as c:
        def sb(name, shape):
            return c.enter_context(nc.sbuf_tensor(name, shape, F32))
        og = sb("og", [P, NT, W512])
        oa = sb("oa", [P, NT, W512])
        s = sb("sg", [P, 2, W512])
        sq = sb("sq", [P, P])
        rs = sb("rs", [P, NT, 8])
        hn = sb("hn", [P, P])
        with Phase(nc, "w_in0 w_in1 mm_done act_read loads squares var roots rstd s_done g0 g0n on prod m_done t_done t_copied dve_s") as (
                block, (w_in0, w_in1, mm_done, act_read, loads, squares, var, roots, rstd, s_done, g0, g0n, on, prod, m_done,
                        t_done, t_copied, dve_s)):
            w_in = (w_in0, w_in1)

            @block.sync
            def _(sp):
                load_weights(sp, nc, a, w, half, cols[:2], w_in, mm_done, steps.last)
                sp.dma_start(hn[:, :], a["hg_norm"][0].partition_broadcast(P)).then_inc(loads, 16)
                for buf, d in ((og, ohg_d), (oa, osb_d)):
                    sp.dma_start(buf[:, 0:NT - 1, :], d[bass.ds(half, 1), 0:SEQ, :].rearrange("a (t p) n -> p (a t) n", p=P)).then_inc(loads, 16)
                    sp.dma_start(buf[:DEC, NT - 1, :], d[bass.ds(half, 1), SEQ:T, :].rearrange("a p n -> (a p) n")).then_inc(loads, 16)
                sp.wait_ge(mm_done, steps.last[0])
                src = a["w_in"][0].rearrange("(k p) n -> p k n", p=P)[:, :, bass.ds(half * W512 + cols[2], W512)]
                sp.dma_start(w[0], src).then_inc(w_in[0], 16)
                sp.wait_ge(loads, 80)

            def turn(pe, t):
                m = rows(t)
                pe.wait_ge(m_done, t + 1)
                if t >= 2:
                    pe.wait_ge(t_copied, t - 1)
                for h in range(HH):
                    mm = pe.transpose(ps[:, BANKS + t % 2, h * P:h * P + m], g1[:m, t, h * P:(h + 1) * P], ident[:m, :m])
                mm.then_inc(t_done, 1)

            @block.tensor
            def _(pe):
                seen = set()
                for n, (g, f, t) in enumerate(steps.list):
                    m = rows(t)
                    if g not in seen:
                        seen.add(g)
                        pe.wait_ge(w_in[g % 2], 16 * (g // 2 + 1))
                    if n >= BANKS:
                        pe.wait_ge(s_done, n - BANKS + 1)
                        e = n - BANKS
                        if e < NT:
                            pe.wait_ge(g0, e + 1)
                    for k in range(KT):
                        mm = pe.matmul(ps[:m, n % BANKS, :], xT[:, k, t * P:t * P + m], w[g % 2][:, k, :],
                                       start=k == 0, stop=k == KT - 1)
                    mm.then_inc(mm_done, 1)
                    if g == 2 and t >= 2:
                        turn(pe, t - 2)
                for t in (NT - 2, NT - 1):
                    turn(pe, t)

            @block.scalar
            def _(act):
                act.wait_ge(loads, 80)
                for t in range(NT):
                    m = rows(t)
                    for h in range(HH):
                        act.activation(sq[:m, :], og[:m, t, h * P:(h + 1) * P], ACT.Square,
                                       accum_out=rs[:m, t, h:h + 1]).then_inc(squares, 1)
                        act.wait_ge(squares, HH * t + h + 1)
                for t in range(NT):
                    m = rows(t)
                    act.wait_ge(var, t + 1)
                    act.activation(rs[:m, t, 4:8], rs[:m, t, 4:8], ACT.Sqrt).then_inc(roots, 1)

                def copy(t):
                    m = rows(t)
                    act.wait_ge(t_done, t + 1)
                    act.activation(mT[:, bass.ds(half * HH, HH), t * P:t * P + m],
                                   ps[:, BANKS + t % 2, :].rearrange("p (h n) -> p h n", h=HH)[:, :, 0:m], ACT.Copy).then_inc(t_copied, 1)

                for n, (g, f, t) in enumerate(steps.list):
                    m = rows(t)
                    act.wait_ge(mm_done, n + 1)
                    if n >= 2:
                        e = n - 2
                        if e < NT:
                            act.wait_ge(g0, e + 1)
                        elif e < 2 * NT:
                            act.wait_ge(prod, e - NT + 1)
                        else:
                            act.wait_ge(m_done, e - 2 * NT + 1)
                    act.activation(s[:m, n % 2, :], ps[:m, n % BANKS, :], ACT.Sigmoid).then_inc(s_done, 1)
                    if g == 2 and t >= 3:
                        copy(t - 3)
                for t in (NT - 3, NT - 2, NT - 1):
                    copy(t)

            @block.vector
            def _(dve):
                ch = Chain(dve, dve_s)
                for t in range(NT):
                    m = rows(t)
                    dve.wait_ge(squares, HH * (t + 1))
                    dve.tensor_scalar(rs[:m, t, 4:8], rs[:m, t, 0:4], 1.0 / P, RMS_EPS, ALU.mult, ALU.add).then_inc(var, 1)
                for t in range(NT):
                    m = rows(t)
                    dve.wait_ge(roots, t + 1)
                    ch(dve.reciprocal(rs[:m, t, 0:4], rs[:m, t, 4:8]))
                for t in range(NT):
                    m = rows(t)
                    dve.wait_ge(s_done, t + 1)
                    dve.tensor_tensor(g1[:m, t, :], s[:m, t % 2, :], ps[:m, t % BANKS, :], ALU.mult).then_inc(g0, 1)
                    dve.wait_ge(g0, t + 1)
                    for h in range(HH):
                        hs = slice(h * P, (h + 1) * P)
                        dve.scalar_tensor_tensor(out=g1[:m, t, hs], in0=og[:m, t, hs], scalar=rs[:m, t, h:h + 1],
                                                 in1=g1[:m, t, hs], op0=ALU.mult, op1=ALU.mult).then_inc(g0n, 1)
                for t in range(NT):
                    m = rows(t)
                    dve.wait_ge(on, t + 1)
                    dve.wait_ge(s_done, NT + t + 1)
                    dve.tensor_tensor(g1[:m, t, :], g1[:m, t, :], s[:m, (NT + t) % 2, :], ALU.mult).then_inc(prod, 1)
                for t in range(NT):
                    m = rows(t)
                    n = 2 * NT + t
                    dve.wait_ge(s_done, n + 1)
                    ch(dve.tensor_tensor(oa[:m, t, :], oa[:m, t, :], s[:m, n % 2, :], ALU.mult))
                    dve.wait_ge(prod, t + 1)
                    dve.tensor_tensor(g1[:m, t, :], g1[:m, t, :], oa[:m, t, :], ALU.add).then_inc(m_done, 1)

            @block.gpsimd
            def _(pool):
                pool.wait_ge(loads, 80)
                for t in range(NT):
                    m = rows(t)
                    pool.wait_ge(g0n, HH * (t + 1))
                    gv = g1[:m, t, :].rearrange("p (h c) -> p h c", h=HH)
                    pool.tensor_tensor(gv, gv, hn[:m, :].unsqueeze(1).to_broadcast([m, HH, P]), ALU.mult).then_inc(on, 1)


def output_projection(nc, a, wbuf, ps, ident, gcol, bcol, st, mT, xT, xn_d, h2_d):
    wo = wbuf[:, :, :].rearrange("p a b -> p (a b)")[:, 0:HEADS * D].rearrange("p (k n) -> p k n", k=HEADS)
    with ExitStack() as c:
        xr = c.enter_context(nc.sbuf_tensor("xr", [P, 2, D], F32))
        y = c.enter_context(nc.sbuf_tensor("y1", [P, 2, D], F32))
        with Phase(nc, "par_in x_in0 x_in1 mm_done sum_done dve_s var_ready root_ready y_ready t_done t_act stored0 stored1") as (block, (
                par_in, x_in0, x_in1, mm_done, sum_done, dve_s, var_ready, root_ready, y_ready, t_done, t_act, stored0, stored1)):
            x_in, stored = (x_in0, x_in1), (stored0, stored1)

            @block.sync
            def _(sp):
                sp.dma_start(wo, a["w_out"][0].rearrange("(k p) n -> p k n", p=P)).then_inc(par_in, 16)
                sp.dma_start(gcol[:, :], a["ln1_g"][0].partition_broadcast(P)).then_inc(par_in, 16)
                sp.dma_start(bcol[:, :], a["ln1_b"][0].partition_broadcast(P)).then_inc(par_in, 16)
                for t in range(NT):
                    m = rows(t)
                    if t >= 2:
                        sp.wait_ge(sum_done, t - 1)
                    sp.dma_start(xr[:m, t % 2, :], xn_d[t * P:t * P + m, :]).then_inc(x_in[t % 2], 16)
                sp.wait_ge(par_in, 48)

            @block.tensor
            def _(pe):
                pe.wait_ge(par_in, 48)

                def turn(t):
                    m = rows(t)
                    pe.wait_ge(y_ready, t + 1)
                    if t >= 2:
                        pe.wait_ge(t_act, 2 * (t - 1))
                    for k in range(KT):
                        mm = pe.transpose(ps[:, 4 + 2 * (t % 2) + k // 4, (k % 4) * P:(k % 4) * P + m],
                                          y[:m, t % 2, k * P:(k + 1) * P], ident[:m, :m])
                    mm.then_inc(t_done, 1)

                for t in range(NT):
                    m = rows(t)
                    if t >= 2:
                        pe.wait_ge(sum_done, t - 1)
                    for b in range(2):
                        for k in range(HEADS):
                            mm = pe.matmul(ps[:m, 2 * (t % 2) + b, :], mT[:, k, t * P:t * P + m], wo[:, k, b * 512:(b + 1) * 512],
                                           start=k == 0, stop=k == HEADS - 1)
                    mm.then_inc(mm_done, 1)
                    if t >= 1:
                        turn(t - 1)
                turn(NT - 1)

            @block.vector
            def _(dve):
                ch = Chain(dve, dve_s)
                for t in range(NT):
                    m = rows(t)
                    dve.wait_ge(mm_done, t + 1)
                    dve.wait_ge(x_in[t % 2], 16 * (t // 2 + 1))
                    if t >= 2:
                        dve.wait_ge(stored[t % 2], 16 * (t // 2))
                        dve.wait_ge(t_done, t - 1)
                    pp = ps[:m, 2 * (t % 2):2 * (t % 2) + 2, :].rearrange("p b n -> p (b n)")
                    dve.scalar_tensor_tensor(out=y[:m, t % 2, :], in0=xr[:m, t % 2, :], scalar=ALPHA, in1=pp, op0=ALU.mult,
                                             op1=ALU.add).then_inc(sum_done, 1)
                    dve.wait_ge(sum_done, t + 1)
                    layer_norm_rows(dve, ch, m, y[:, t % 2, :], y[:, t % 2, :], st[:, t % 2, :], gcol, var_ready, root_ready, t)
                    dve.tensor_tensor(y[:m, t % 2, :], y[:m, t % 2, :], bcol[:m, :], ALU.add).then_inc(y_ready, 1)

            @block.scalar
            def _(act):
                for t in range(NT):
                    m = rows(t)
                    act.wait_ge(var_ready, t + 1)
                    act.activation(st[:m, t % 2, 15:16], st[:m, t % 2, 14:15], ACT.Sqrt).then_inc(root_ready, 1)
                    act.wait_ge(y_ready, t + 1)
                    act.dma_start(h2_d[t * P:t * P + m, :], y[:m, t % 2, :]).then_inc(stored[t % 2], 16)
                    act.wait_ge(t_done, t + 1)
                    for b in range(2):
                        act.activation(xT[:, 4 * b:4 * b + 4, t * P:t * P + m],
                                       ps[:, 4 + 2 * (t % 2) + b, :].rearrange("p (k n) -> p k n", k=4)[:, :, 0:m],
                                       ACT.Copy).then_inc(t_act, 1)
                act.wait_ge(stored[0], 16 * 5)
                act.wait_ge(stored[1], 16 * 4)


def router(nc, a, ps, xT, gates):
    with ExitStack() as c:
        def sb(name, shape):
            return c.enter_context(nc.sbuf_tensor(name, shape, F32))
        wr = sb("wr", [P, KT, NE])
        rb = sb("rb", [P, NE])
        s = sb("rs_", [P, 2, NE])
        sbm = sb("sbm", [P, NE])
        rep = sb("rep", [P, NE])
        g8 = sb("g8", [P, NGRP, 8])
        gs = sb("gs", [P, NGRP])
        cmp_ = sb("cmp_", [P, 2, NGRP, NGRP])
        earlier = sb("earlier", [P, NGRP, NGRP])
        rank = sb("rank", [P, 3, NGRP])
        top = sb("top", [P, 8])
        tot = sb("tot", [P, 2])
        with Phase(nc, "r_in pooled memo mm_done s_done dve_s") as (block, (r_in, pooled, memo, mm_done, s_done, dve_s)):
            @block.sync
            def _(sp):
                sp.dma_start(wr[:, :, :], a["w_router"][0].rearrange("(k p) n -> p k n", p=P)).then_inc(r_in, 16)
                sp.dma_start(rb[:, :], a["router_bias"][0].partition_broadcast(P)).then_inc(r_in, 16)
                sp.wait_ge(r_in, 32)

            @block.gpsimd
            def _(pool):
                pool.memset(earlier[:, :, :], 1.0).then_inc(memo, 1)
                pool.wait_ge(memo, 1)
                pool.affine_select(out=earlier[:, :, :], in_=earlier[:, :, :], compare_op=ALU.is_ge, fill=0.0, base=-1,
                                   pattern=[[1, NGRP], [-1, NGRP]], channel_multiplier=0).then_inc(pooled, 1)

            @block.tensor
            def _(pe):
                pe.wait_ge(r_in, 32)
                for t in range(NT):
                    m = rows(t)
                    if t >= 2:
                        pe.wait_ge(s_done, t - 1)
                    for k in range(KT):
                        mm = pe.matmul(ps[:m, t % 2, 0:NE], xT[:, k, t * P:t * P + m], wr[:, k, :], start=k == 0, stop=k == KT - 1)
                    mm.then_inc(mm_done, 1)

            STEPS = 27

            @block.scalar
            def _(act):
                for t in range(NT):
                    m = rows(t)
                    act.wait_ge(mm_done, t + 1)
                    if t >= 2:
                        act.wait_ge(dve_s, STEPS * (t - 1))
                    act.activation(s[:m, t % 2, :], ps[:m, t % 2, 0:NE], ACT.Sigmoid).then_inc(s_done, 1)

            @block.vector
            def _(dve):
                ch = Chain(dve, dve_s)
                dve.wait_ge(pooled, 1)
                dve.wait_ge(r_in, 32)
                for t in range(NT):
                    m = rows(t)
                    sc = s[:m, t % 2, :]
                    B = [m, NGRP, NGRP]
                    dve.wait_ge(s_done, t + 1)
                    ch(dve.tensor_tensor(sbm[:m, :], sc, rb[:m, :], ALU.add))
                    for g in range(NGRP):
                        ch(dve.max(g8[:m, g, :], sbm[:m, g * EPG:(g + 1) * EPG]))
                    ch(dve.tensor_tensor(gs[:m, :], g8[:m, :, 0], g8[:m, :, 1], ALU.add))
                    own, other = gs[:m, :].unsqueeze(2).to_broadcast(B), gs[:m, :].unsqueeze(1).to_broadcast(B)
                    ch(dve.tensor_tensor(cmp_[:m, 0, :, :], other, own, ALU.is_gt))
                    ch(dve.tensor_tensor(cmp_[:m, 1, :, :], other, own, ALU.is_equal))
                    ch(dve.tensor_tensor(cmp_[:m, 1, :, :], cmp_[:m, 1, :, :], earlier[:m, :, :], ALU.mult))
                    ch(dve.tensor_tensor(cmp_[:m, 0, :, :], cmp_[:m, 0, :, :], cmp_[:m, 1, :, :], ALU.add))
                    ch(dve.tensor_reduce(rank[:m, 0, :], cmp_[:m, 0, :, :], AX.X, ALU.add))
                    ch(dve.tensor_scalar(rank[:m, 1, :], rank[:m, 0, :], float(TOPG), None, ALU.is_lt))
                    ch(dve.tensor_scalar(rank[:m, 2, :], rank[:m, 1, :], -1.0, -NEG_BIG, ALU.add, ALU.mult))
                    v3 = sbm[:m, :].rearrange("p (g e) -> p g e", g=NGRP)
                    ch(dve.tensor_tensor(v3, v3, rank[:m, 1, :].unsqueeze(2).to_broadcast([m, NGRP, EPG]), ALU.mult))
                    ch(dve.tensor_tensor(v3, v3, rank[:m, 2, :].unsqueeze(2).to_broadcast([m, NGRP, EPG]), ALU.add))
                    ch(dve.max(top[:m, :], sbm[:m, :]))
                    ch(dve.match_replace(rep[:m, :], top[:m, :], sbm[:m, :], 4 * NEG_BIG))
                    ch(dve.tensor_scalar(rep[:m, :], rep[:m, :], 2 * NEG_BIG, None, ALU.is_lt))
                    ch(dve.tensor_tensor(gates[:m, t, :], rep[:m, :], sc, ALU.mult))
                    ch(dve.tensor_reduce(tot[:m, 0:1], gates[:m, t, :], AX.X, ALU.add))
                    ch(dve.reciprocal(tot[:m, 1:2], tot[:m, 0:1]))
                    ch(dve.tensor_scalar(gates[:m, t, :], gates[:m, t, :], tot[:m, 1:2], ROUTE_SCALE, ALU.mult, ALU.mult))
                    ch(dve.memset(tot[:m, 0:1], 0.0))
                    assert ch.n == STEPS * (t + 1), ch.n


def experts_dense(nc, a, o, ps, ident, gcol, bcol, st, xT, h2_d):
    with ExitStack() as c:
        def sb(name, shape):
            return c.enter_context(nc.sbuf_tensor(name, shape, F32))
        gates = sb("gates", [P, NT, NE])
        router(nc, a, ps, xT, gates)
        y = sb("yacc", [P, NT, D])
        wg = sb("wg", [P, 2, KT, FE])
        wu = sb("wu", [P, 2, KT, FE])
        wd = sb("wd", [P, 2, 2, D])
        hT = sb("hT", [P, 2, T])
        sl = sb("sl", [P, 2, 512])
        xr = sb("xr2", [P, 2, D])
        with Phase(nc, "primed wu0 wu1 wd0 wd1 gu_done s_done h_done d_done acc par_in x_in0 x_in1 dve_s var_ready root_ready y_ready y_out") as (block, (
                primed, wu0, wu1, wd0, wd1, gu_done, s_done, h_done, d_done, acc, par_in, x_in0, x_in1, dve_s, var_ready, root_ready, y_ready, y_out)):
            wu_in, wd_in, x_in = (wu0, wu1), (wd0, wd1), (x_in0, x_in1)
            steps = [(f, ci) for f in range(2) for ci in range(3)]
            dsteps = [(t, b) for t in range(NT) for b in range(2)]
            G, DN = len(steps), len(dsteps)

            def load(sp, b, G_, U_, D_):
                sp.dma_start(wg[:, b, :, :], G_.rearrange("(k p) n -> p k n", p=P)).then_inc(wu_in[b], 16)
                sp.dma_start(wu[:, b, :, :], U_.rearrange("(k p) n -> p k n", p=P)).then_inc(wu_in[b], 16)
                sp.dma_start(wd[:, b, :, :], D_.rearrange("(k p) n -> p k n", p=P)).then_inc(wd_in[b], 16)

            def expert(e):
                return [a[n][0, bass.ds(e, 1), :, :].rearrange("a d f -> (a d) f") for n in ("w_exp_gate", "w_exp_up", "w_exp_down")]

            @block.sync
            def _(sp):
                sp.dma_start(gcol[:, :], a["ln2_g"][0].partition_broadcast(P)).then_inc(par_in, 16)
                sp.dma_start(bcol[:, :], a["ln2_b"][0].partition_broadcast(P)).then_inc(par_in, 16)
                for b in range(2):
                    load(sp, b, *expert(b))
                with sp.Fori(1, NE // 2) as i:
                    for b in range(2):
                        sp.wait_ge(d_done, (2 * i + b - 1) * DN)
                        load(sp, b, *expert(2 * i + b))
                sp.wait_ge(d_done, (NE - 1) * DN)
                load(sp, 0, a["w_sh_gate"][0], a["w_sh_up"][0], a["w_sh_down"][0])
                for t in range(NT):
                    m = rows(t)
                    if t >= 2:
                        sp.wait_ge(y_ready, t - 1)
                    sp.dma_start(xr[:m, t % 2, :], h2_d[t * P:t * P + m, :]).then_inc(x_in[t % 2], 16)
                sp.wait_ge(par_in, 32)

            def up(pe, b, wait_w, base, prime):
                pe.wait_ge(wu_in[b], wait_w)
                for n, (f, ci) in enumerate(steps):
                    c0, cw = CHUNKS[ci]
                    if prime or n >= 2:
                        pe.wait_ge(h_done, base + n - 1)
                    for wt, bank in ((wg, n % 2), (wu, 2 + n % 2)):
                        for k in range(KT):
                            mm = pe.matmul(ps[:, bank, 0:cw], wt[:, b, k, f * P:(f + 1) * P], xT[:, k, c0:c0 + cw],
                                           start=k == 0, stop=k == KT - 1)
                    mm.then_inc(gu_done, 1)

            def down(pe, b, wait_w, hbase, base, prime):
                pe.wait_ge(wd_in[b], wait_w)
                pe.wait_ge(h_done, hbase + G)
                for n, (t, q) in enumerate(dsteps):
                    m = rows(t)
                    if n >= 4:
                        pe.wait_ge(acc, base + n - 3)
                    elif n == 0 and prime:
                        pe.wait_ge(acc, base)
                    for f in range(2):
                        mm = pe.matmul(ps[:m, 4 + n % 4, :], hT[:, f, t * P:t * P + m], wd[:, b, f, q * 512:(q + 1) * 512],
                                       start=f == 0, stop=f == 1)
                    mm.then_inc(d_done, 1)

            @block.tensor
            def _(pe):
                def one(i, b, prime):
                    up(pe, b, 32 * i + 32, (2 * i + b) * G, prime)
                    down(pe, b, 16 * i + 16, (2 * i + b) * G, (2 * i + b) * DN, prime)
                one(0, 0, False)
                one(0, 1, True)
                with pe.Fori(1, NE // 2) as i:
                    for b in range(2):
                        one(i, b, True)
                one(NE // 2, 0, True)

            @block.scalar
            def _(act):
                def one(base, prime):
                    for n, (f, ci) in enumerate(steps):
                        c0, cw = CHUNKS[ci]
                        act.wait_ge(gu_done, base + n + 1)
                        if prime or n >= 2:
                            act.wait_ge(h_done, base + n - 1)
                        act.activation(sl[:, n % 2, 0:cw], ps[:, n % 2, 0:cw], ACT.Silu).then_inc(s_done, 1)
                one(0, False)
                with act.Fori(1, NE + 1) as e:
                    one(e * G, True)
                for t in range(NT):
                    m = rows(t)
                    act.wait_ge(var_ready, t + 1)
                    act.activation(st[:m, t % 2, 15:16], st[:m, t % 2, 14:15], ACT.Sqrt).then_inc(root_ready, 1)
                for t in range(NT):
                    m = rows(t)
                    act.wait_ge(y_ready, t + 1)
                    dst = o[0][0, t * P:t * P + m, :] if t < NT - 1 else o[1][0, :, :]
                    act.dma_start(dst, y[:m, t, :]).then_inc(y_out, 16)
                act.wait_ge(y_out, 16 * NT)

            @block.vector
            def _(dve):
                ch = Chain(dve, dve_s)

                def hidden(base):
                    for n, (f, ci) in enumerate(steps):
                        c0, cw = CHUNKS[ci]
                        dve.wait_ge(s_done, base + n + 1)
                        dve.tensor_tensor(hT[:, f, c0:c0 + cw], sl[:, n % 2, 0:cw], ps[:, 2 + n % 2, 0:cw], ALU.mult).then_inc(h_done, 1)

                def accumulate(base, e, first):
                    for n, (t, b) in enumerate(dsteps):
                        m = rows(t)
                        ys = y[:m, t, b * 512:(b + 1) * 512]
                        dve.wait_ge(d_done, base + n + 1)
                        if first:
                            dve.tensor_scalar(ys, ps[:m, 4 + n % 4, :], gates[:m, t, e:e + 1], None, ALU.mult).then_inc(acc, 1)
                        else:
                            dve.wait_ge(acc, base + n + 1 - DN)
                            sc = 1.0 if e is None else gates[:m, t, bass.ds(e, 1)]
                            dve.scalar_tensor_tensor(out=ys, in0=ps[:m, 4 + n % 4, :], scalar=sc, in1=ys,
                                                     op0=ALU.mult, op1=ALU.add).then_inc(acc, 1)

                hidden(0)
                accumulate(0, 0, True)
                with dve.Fori(1, NE) as e:
                    hidden(e * G)
                    accumulate(e * DN, e, False)
                hidden(NE * G)
                accumulate(NE * DN, None, False)
                dve.wait_ge(par_in, 32)
                dve.wait_ge(acc, (NE + 1) * DN)
                for t in range(NT):
                    m = rows(t)
                    dve.wait_ge(x_in[t % 2], 16 * (t // 2 + 1))
                    ch(dve.scalar_tensor_tensor(out=y[:m, t, :], in0=xr[:m, t % 2, :], scalar=ALPHA, in1=y[:m, t, :],
                                                op0=ALU.mult, op1=ALU.add))
                    layer_norm_rows(dve, ch, m, y[:, t, :], y[:, t, :], st[:, t % 2, :], gcol,
                                    var_ready, root_ready, t)
                    dve.tensor_tensor(y[:m, t, :], y[:m, t, :], bcol[:m, :], ALU.add).then_inc(y_ready, 1)


_INS = ["x_prompt", "x_sample", "cache_sb_k", "cache_sb_v", "state_hgrn", "ln_in_g", "ln_in_b", "w_in", "w_out", "hg_norm",
        "hg_lb_logits", "ln1_g", "ln1_b", "w_router", "router_bias", "w_exp_gate", "w_exp_up", "w_exp_down", "w_sh_gate",
        "w_sh_up", "w_sh_down", "ln2_g", "ln2_b"]
_OUTS = [(1, SEQ, D), (1, DEC, D), (1, 1, SEQ, HEADS, P), (1, 1, SEQ, HEADS, P), (1, 1, HEADS, P, P),
         (1, 1, DEC, HEADS, P), (1, 1, DEC, HEADS, P), (1, 1, HEADS, P, P)]


def kernel(**inputs):
    import concourse.bacc as bacc
    from concourse.bass_utils import run_bass_kernel_spmd

    nc = bacc.Bacc("TRN2", target_bir_lowering=False, num_devices=1)
    arrays, args = {}, {}
    for name in _INS:
        x = np.ascontiguousarray(inputs[name])
        arrays[f"in_{name}"] = x
        args[name] = nc.dram_tensor(f"in_{name}", x.shape, mybir.dt.from_np(x.dtype), kind="ExternalInput").ap()
    outs = [nc.dram_tensor(f"out_{i}", s, F32, kind="ExternalOutput").ap() for i, s in enumerate(_OUTS)]
    build(nc, args, outs)
    r = run_bass_kernel_spmd(nc, [arrays], core_ids=[0])
    return tuple(r.results[0][f"out_{i}"] for i in range(len(_OUTS)))
```

```python
from contextlib import ExitStack

import concourse.bass as bass
import numpy as np
from concourse import mybir

F32 = mybir.dt.float32
I32 = mybir.dt.int32
U32 = mybir.dt.uint32
F32R = mybir.dt.float32r
ACT = mybir.ActivationFunctionType
ALU = mybir.AluOpType
AX = mybir.AxisListType

P = 128
D = 1024
KT = D // P
SEQ, DEC, PAST = 1024, 64, 128
T = SEQ + DEC
NT = (T + P - 1) // P
HEADS = 8
HH = 4
HALVES = HEADS // HH
W512 = HH * P
NE, NGRP, TOPG, TOPK = 64, 8, 4, 8
EPG = NE // NGRP
FE = 256
ROUTE_SCALE = 2.5
NEG_BIG = -1e9
ALPHA = 2.0 ** 0.25
LN_EPS, RMS_EPS = 1e-5, 1e-6
LB_FLOOR = 1e-30
SCALE = P ** -0.5
LN_SHIFT = 50
LN2 = float(np.log(2.0))
CAP = 192
NOBODY = 4 * T
OVB = max(min(n * -(-(T - CAP) // P), (T * TOPK - n * (CAP + 1)) // P + n) for n in range(1, NE + 1) if n * (CAP + 1) <= T * TOPK)
SLOTS = NE * CAP + OVB * P
LEVELS = [1, 2, 4, 8, 16, 32, 64]
NL = len(LEVELS)
CHUNKS = [(0, 512), (512, 512), (1024, DEC)]
(C_SQ, C_SK, C_SV, C_HQ, C_HF, C_HI, C_HG, C_GS, C_GH) = range(0, 9 * D, D)


def rows(t):
    return P if t < NT - 1 else T - P * (NT - 1)


def absolute(dve, out, x):
    return dve.scalar_tensor_tensor(out=out, in0=x, scalar=-1.0, in1=x, op0=ALU.mult, op1=ALU.max)


class Chain:

    def __init__(self, eng, sem):
        self.eng, self.sem, self.n = eng, sem, 0

    def __call__(self, ins):
        self.n += 1
        ins.then_inc(self.sem, 1)
        self.eng.wait_ge(self.sem, self.n)


class Phase:

    def __init__(self, nc, names, software_dma=()):
        self.nc, self.stack = nc, ExitStack()
        self.sems = [self.stack.enter_context(nc.semaphore(n)) for n in names.split()]
        self.queued = [self.sems[names.split().index(n)] for n in software_dma]

    def __enter__(self):
        self.block_ctx = self.nc.Block()
        return self.block_ctx.__enter__(), self.sems

    def __exit__(self, *a):
        self.block_ctx.__exit__(*a)
        self.nc.all_engine_barrier()
        for s in self.queued:
            self.nc.gpsimd.dma_reset(range(s.num, s.num + 1))
            self.nc.gpsimd.sem_clear(s)
        for s in self.sems:
            self.nc.sync.sem_clear(s)
        self.nc.all_engine_barrier()
        self.stack.close()


def layer_norm_rows(eng, ch, m, x, out, st, gg, sqrt_req, sqrt_done, n):
    for c in range(2):
        ch(eng.bn_stats(st[:m, 6 * c:6 * c + 6], x[:m, 512 * c:512 * c + 512]))
    ch(eng.bn_aggr(st[:m, 12:14], st[:m, 0:12]))
    eng.tensor_scalar(st[:m, 14:15], st[:m, 13:14], LN_EPS, None, ALU.add).then_inc(sqrt_req, 1)
    eng.wait_ge(sqrt_done, n + 1)
    ch(eng.reciprocal(st[:m, 16:17], st[:m, 15:16]))
    ch(eng.tensor_scalar(out[:m, :], x[:m, :], st[:m, 12:13], st[:m, 16:17], ALU.subtract, ALU.mult))
    ch(eng.tensor_tensor(out[:m, :], out[:m, :], gg[:m, :], ALU.mult))


def build(nc, a, o):
    ctx = ExitStack()
    with ctx:
        def sb(name, shape, dt=F32):
            return ctx.enter_context(nc.sbuf_tensor(name, shape, dt))

        def dram(name, shape, dt=F32):
            return nc.dram_tensor(name, shape, dt, kind="Internal").ap()

        xn_d = dram("xn_d", [NT * P, D])
        h2_d = dram("h2_d", [T, D])
        osb_d = dram("osb_d", [HALVES, NT * P, W512])
        ohg_d = dram("ohg_d", [HALVES, NT * P, W512])

        ps = ctx.enter_context(nc.psum_tensor("ps", [P, 8, 512], F32))
        ident = sb("ident", [P, P])
        ones = sb("ones", [P, P])
        gcol = sb("gcol", [P, D])
        bcol = sb("bcol", [P, D])
        bigT = sb("bigT", [P, KT, T])
        st = sb("st", [P, 2, 20])
        before = sb("before", [P, P])
        tok_d = dram("tok_d", [SLOTS, 1], U32)
        plan_d = dram("plan_d", [OVB + 1, 1], I32)
        gates_d = dram("gates_d", [T, NE])
        only_d = dram("only_d", [OVB, NE])
        ys_d = dram("ys_d", [T, D])
        ye_d = dram("ye_d", [NE * CAP, D])

        constants(nc, ident, ones, before)
        input_norm(nc, a, xn_d, ps, ident, gcol, bcol, bigT, st)
        with ExitStack() as mix_ctx:
            def msb(name, shape, dt=F32):
                return mix_ctx.enter_context(nc.sbuf_tensor(name, shape, dt))
            mT = msb("mT", [P, HEADS, T])
            wbuf = msb("wbuf", [P, NL + 2, T])
            tri = msb("tri", [P, 3, P])
            masks = msb("masks", [P, NL + 1, P])
            lbc = msb("lbc", [P, 3, HEADS])
            w = [wbuf[:, :, :].rearrange("p a b -> p (a b)")[:, i * KT * W512:(i + 1) * KT * W512]
                 .rearrange("p (k n) -> p k n", k=KT) for i in range(2)]
            mixer_constants(nc, a, tri, masks, lbc)
            with nc.Fori(0, HALVES) as half:
                with ExitStack() as c2:
                    qT = c2.enter_context(nc.sbuf_tensor("qT", [P, HH, T], F32))
                    kT = c2.enter_context(nc.sbuf_tensor("kT", [P, HH, T], F32))
                    v = c2.enter_context(nc.sbuf_tensor("v", [P, NT, W512], F32))
                    project_qkv(nc, a, o, half, w, bigT, ps, ident, qT, kT, v)
                    attention(nc, a, half, ps, ident, tri, qT, kT, v, osb_d)
                with ExitStack() as c2:
                    qT = c2.enter_context(nc.sbuf_tensor("hqT", [P, HH, T], F32))
                    kT = c2.enter_context(nc.sbuf_tensor("hkT", [P, HH, T], F32))
                    bT = c2.enter_context(nc.sbuf_tensor("hbT", [P, HH, T], F32))
                    v = c2.enter_context(nc.sbuf_tensor("hv", [P, NT, W512], F32))
                    project_hgrn(nc, a, half, w, bigT, ps, lbc, qT, kT, bT, v)
                    hgrn(nc, a, o, half, ps, ident, masks, wbuf, qT, kT, bT, v, ohg_d)
                with ExitStack() as c2:
                    g1 = c2.enter_context(nc.sbuf_tensor("g1", [P, NT, W512], F32))
                    merge(nc, a, half, w, bigT, ps, ident, g1, osb_d, ohg_d, mT)
            output_projection(nc, a, wbuf, ps, ident, gcol, bcol, st, mT, bigT, xn_d, h2_d)
        mixture(nc, a, o, ps, ident, ones, gcol, bcol, st, bigT, before, h2_d, tok_d, plan_d, gates_d, only_d, ys_d, ye_d)


def constants(nc, ident, ones, before):
    with Phase(nc, "set_up") as (block, (set_up,)):
        @block.gpsimd
        def _(pool):
            pool.memset(ident[:, :], 0.0).then_inc(set_up, 1)
            pool.memset(ones[:, :], 1.0).then_inc(set_up, 1)
            pool.memset(before[:, :], 1.0).then_inc(set_up, 1)
            pool.wait_ge(set_up, 3)
            pool.affine_select(out=before[:, :], in_=before[:, :], compare_op=ALU.is_ge, fill=0.0, base=-1,
                               pattern=[[1, P]], channel_multiplier=-1).then_inc(set_up, 1)
            pool.affine_select(out=ident[:, :], in_=ident[:, :], compare_op=ALU.not_equal, fill=1.0, base=0,
                               pattern=[[-1, P]], channel_multiplier=1).then_inc(set_up, 1)
            pool.wait_ge(set_up, 5)


def mixer_constants(nc, a, tri, masks, lbc):
    with Phase(nc, "memo pooled loaded dve act") as (block, (memo, pooled, loaded, dve_s, act_s)):
        @block.vector
        def _(dve):
            ch = Chain(dve, dve_s)
            dve.memset(tri[:, :, :], 1.0).then_inc(memo, 1)
            dve.memset(masks[:, :, :], 1.0).then_inc(memo, 1)
            dve.wait_ge(loaded, 16)
            lg = lbc[:, 0, :]
            ch(dve.tensor_tensor(lbc[:, 1, :], lg, lg, ALU.subtract))
            dve.wait_ge(act_s, 1)
            ch(dve.reciprocal(lbc[:, 0, :], lbc[:, 2, :]))
            ch(dve.tensor_tensor(lbc[:, 0, :], lbc[:, 0, :], lbc[:, 2, :], ALU.mult))
            ch(dve.tensor_tensor(lbc[:, 0, :], lbc[:, 0, :], lbc[:, 0, :], ALU.subtract))
            ch(dve.tensor_scalar(lbc[:, 0, :], lbc[:, 0, :], LB_FLOOR, None, ALU.max))
            ch(dve.tensor_scalar(lbc[:, 1, :], lbc[:, 0, :], -1.0, 1.0, ALU.mult, ALU.add))
            dve.wait_ge(act_s, 2)
            ch(dve.tensor_scalar(lbc[:, 0, :], lbc[:, 2, :], -LN_SHIFT * LN2, None, ALU.add))
            ch(dve.tensor_scalar(lbc[:, 2, :], lbc[:, 0, :], -1.0, None, ALU.mult))

        @block.scalar
        def _(act):
            act.wait_ge(dve_s, 1)
            act.activation(lbc[:, 2, :], lbc[:, 1, :], ACT.Exp).then_inc(act_s, 1)
            act.wait_ge(dve_s, 5)
            act.activation(lbc[:, 2, :], lbc[:, 0, :], ACT.Ln, scale=2.0 ** LN_SHIFT).then_inc(act_s, 1)

        @block.sync
        def _(sp):
            with nc.allow_non_contiguous_dma(reason="1024 numbers, once"):
                sp.dma_start(lbc[:, 0, :], a["hg_lb_logits"].rearrange("a (h c) -> c (a h)", c=P)).then_inc(loaded, 16)
            sp.wait_ge(loaded, 16)

        @block.gpsimd
        def _(pool):
            pool.wait_ge(memo, 2)
            n = 0

            def keep(ap, base, pattern, cm):
                nonlocal n
                pool.affine_select(out=ap, in_=ap, compare_op=ALU.is_ge, fill=0.0, base=base, pattern=pattern,
                                   channel_multiplier=cm).then_inc(pooled, 1)
                n += 1
                pool.wait_ge(pooled, n)

            keep(tri[:, 0, :], -1, [[1, P]], -1)
            keep(tri[:, 1, :], 0, [[-1, P]], 1)
            keep(tri[:, 2, :], -1, [[1, P]], -1)
            for i, h in enumerate(LEVELS):
                v = masks[:, i + 1, :].rearrange("p (g u) -> p g u", u=2 * h)
                keep(v, 0, [[-2 * h, P // (2 * h)], [0, 2 * h]], 1)
                keep(v, h - 1, [[2 * h, P // (2 * h)], [0, 2 * h]], -1)
                keep(v, -h, [[0, P // (2 * h)], [1, 2 * h]], 0)
            keep(masks[:, 0, :], 0, [[1, P]], -1)
            keep(masks[:, 0, :], 0, [[-1, P]], 1)


def input_norm(nc, a, xn_d, ps, ident, gcol, bcol, xT, st):
    with ExitStack() as c:
        xin = c.enter_context(nc.sbuf_tensor("xin", [P, 2, D], F32))
        y = c.enter_context(nc.sbuf_tensor("y", [P, 2, D], F32))
        with Phase(nc, "par_in x_in0 x_in1 dve_s var_ready root_ready y_ready t_done t_act stored0 stored1") as (block, (
                par_in, x_in0, x_in1, dve_s, var_ready, root_ready, y_ready, t_done, t_act, stored0, stored1)):
            x_in, stored = (x_in0, x_in1), (stored0, stored1)

            @block.sync
            def _(sp):
                sp.dma_start(gcol[:, :], a["ln_in_g"].partition_broadcast(P)).then_inc(par_in, 16)
                sp.dma_start(bcol[:, :], a["ln_in_b"].partition_broadcast(P)).then_inc(par_in, 16)
                for t in range(NT):
                    m = rows(t)
                    if t >= 2:
                        sp.wait_ge(y_ready, t - 1)
                    src = a["x_prompt"][0, t * P:t * P + m, :] if t < NT - 1 else a["x_sample"][0, :, :]
                    sp.dma_start(xin[:m, t % 2, :], src).then_inc(x_in[t % 2], 16)

            @block.vector
            def _(dve):
                ch = Chain(dve, dve_s)
                dve.wait_ge(par_in, 32)
                for t in range(NT):
                    m = rows(t)
                    dve.wait_ge(x_in[t % 2], 16 * (t // 2 + 1))
                    if t >= 2:
                        dve.wait_ge(stored[t % 2], 16 * (t // 2))
                        dve.wait_ge(t_done, t - 1)
                    layer_norm_rows(dve, ch, m, xin[:, t % 2, :], y[:, t % 2, :], st[:, t % 2, :], gcol, var_ready, root_ready, t)
                    dve.tensor_tensor(y[:m, t % 2, :], y[:m, t % 2, :], bcol[:m, :], ALU.add).then_inc(y_ready, 1)

            @block.scalar
            def _(act):
                for t in range(NT):
                    m = rows(t)
                    act.wait_ge(var_ready, t + 1)
                    act.activation(st[:m, t % 2, 15:16], st[:m, t % 2, 14:15], ACT.Sqrt).then_inc(root_ready, 1)
                    act.wait_ge(y_ready, t + 1)
                    act.dma_start(xn_d[t * P:t * P + m, :], y[:m, t % 2, :]).then_inc(stored[t % 2], 16)
                    act.wait_ge(t_done, t + 1)
                    for b in range(2):
                        act.activation(xT[:, 4 * b:4 * b + 4, t * P:t * P + m],
                                       ps[:, 2 * (t % 2) + b, :].rearrange("p (k n) -> p k n", k=4)[:, :, 0:m],
                                       ACT.Copy).then_inc(t_act, 1)
                act.wait_ge(stored[0], 16 * 5)
                act.wait_ge(stored[1], 16 * 4)

            @block.tensor
            def _(pe):
                for t in range(NT):
                    m = rows(t)
                    pe.wait_ge(y_ready, t + 1)
                    if t >= 2:
                        pe.wait_ge(t_act, 2 * (t - 1))
                    for k in range(KT):
                        mm = pe.transpose(ps[:, 2 * (t % 2) + k // 4, (k % 4) * P:(k % 4) * P + m],
                                          y[:m, t % 2, k * P:(k + 1) * P], ident[:m, :m])
                    mm.then_inc(t_done, 1)


def load_weights(eng, nc, a, w, half, cols, w_in, mm_done, freed):
    for g, c0 in enumerate(cols):
        if g >= 2:
            eng.wait_ge(mm_done, freed[g - 2])
        src = a["w_in"][0].rearrange("(k p) n -> p k n", p=P)[:, :, bass.ds(half * W512 + c0, W512)]
        eng.dma_start(w[g % 2], src).then_inc(w_in[g % 2], 16)


class Steps:

    def __init__(self, forms):
        self.list = []
        self.last = []
        for g, f in enumerate(forms):
            if f == "T":
                self.list += [(g, f, (e, c)) for e in range(HH) for c in range(3)]
            else:
                self.list += [(g, f, t) for t in range(NT)]
            self.last.append(len(self.list))


def products(pe, steps, w, xT, ps, banks, w_in, mm_done, read_done):
    seen = set()
    for n, (g, f, i) in enumerate(steps.list):
        if g not in seen:
            seen.add(g)
            pe.wait_ge(w_in[g % 2], 16 * (g // 2 + 1))
        if n >= banks:
            e = n - banks
            pe.wait_ge(read_done[e % len(read_done)], e // len(read_done) + 1)
        for k in range(KT):
            if f == "T":
                c0, cw = CHUNKS[i[1]]
                mm = pe.matmul(ps[:, n % banks, 0:cw], w[g % 2][:, k, i[0] * P:(i[0] + 1) * P],
                               xT[:, k, c0:c0 + cw], start=k == 0, stop=k == KT - 1)
            else:
                m = rows(i)
                mm = pe.matmul(ps[:m, n % banks, :], xT[:, k, i * P:i * P + m], w[g % 2][:, k, :],
                               start=k == 0, stop=k == KT - 1)
        mm.then_inc(mm_done, 1)


def project_qkv(nc, a, o, half, w, xT, ps, ident, qT, kT, v):
    cols = (C_SQ, C_SK, C_SV)
    steps = Steps("TTR")
    BANKS = 6
    with ExitStack() as c:
        krow = c.enter_context(nc.sbuf_tensor("krow", [P, 2, W512], F32))
        with Phase(nc, "w_in0 w_in1 mm_done act_read dve_read k_done k_copied v_out kout0 kout1") as (block, (
                w_in0, w_in1, mm_done, act_read, dve_read, k_done, k_copied, v_out, kout0, kout1)):
            w_in, read, kout = (w_in0, w_in1), (act_read, dve_read), (kout0, kout1)

            @block.sync
            def _(sp):
                load_weights(sp, nc, a, w, half, cols, w_in, mm_done, steps.last)
                hs = bass.ds(half * HH, HH)
                for t in range(NT):
                    m = rows(t)
                    sp.wait_ge(k_copied, t + 1)
                    dst = o[2][0, 0, t * P:t * P + m, hs, :] if t < NT - 1 else o[5][0, 0, :, hs, :]
                    sp.dma_start(dst, krow[:m, t % 2, :].rearrange("p (h c) -> p h c", h=HH)).then_inc(kout[t % 2], 16)
                sp.wait_ge(act_read, (len(steps.list) + 1) // 2)
                sp.wait_ge(dve_read, len(steps.list) // 2)
                for t in range(NT):
                    m = rows(t)
                    dst = o[3][0, 0, t * P:t * P + m, hs, :] if t < NT - 1 else o[6][0, 0, :, hs, :]
                    sp.dma_start(dst, v[:m, t, :].rearrange("p (h c) -> p h c", h=HH)).then_inc(v_out, 16)
                sp.wait_ge(v_out, 16 * NT)
                sp.wait_ge(kout[0], 16 * 5)
                sp.wait_ge(kout[1], 16 * 4)

            @block.tensor
            def _(pe):
                products(pe, steps, w, xT, ps, BANKS, w_in, mm_done, read)
                pe.wait_ge(act_read, (steps.last[1] + 1) // 2)
                pe.wait_ge(dve_read, steps.last[1] // 2)
                for t in range(NT):
                    m = rows(t)
                    if t >= 2:
                        pe.wait_ge(k_copied, t - 1)
                    for h in range(HH):
                        mm = pe.transpose(ps[:m, BANKS + t % 2, h * P:(h + 1) * P], kT[:, h, t * P:t * P + m], ident[:, :])
                    mm.then_inc(k_done, 1)

            def copy_out(eng, copy, me):
                for n, (g, f, i) in enumerate(steps.list):
                    if n % 2 != me:
                        continue
                    eng.wait_ge(mm_done, n + 1)
                    if f == "T":
                        c0, cw = CHUNKS[i[1]]
                        dst = (qT, kT)[g][:, i[0], c0:c0 + cw]
                        src = ps[:, n % BANKS, 0:cw]
                    else:
                        m = rows(i)
                        dst, src = v[:m, i, :], ps[:m, n % BANKS, :]
                    copy(dst, src).then_inc(read[me], 1)

            @block.scalar
            def _(act):
                copy_out(act, lambda d, s: act.activation(d, s, ACT.Copy), 0)

            @block.vector
            def _(dve):
                copy_out(dve, dve.tensor_copy, 1)
                for t in range(NT):
                    m = rows(t)
                    dve.wait_ge(k_done, t + 1)
                    if t >= 2:
                        dve.wait_ge(kout[t % 2], 16 * (t // 2))
                    dve.tensor_copy(krow[:m, t % 2, :], ps[:m, BANKS + t % 2, :]).then_inc(k_copied, 1)


def attention_units():
    def tile(i):
        js = list(range(i, -1, -1)) if i < NT - 1 else [i, -1]
        return [(i, j, j == js[0], j == js[-1]) for j in js]
    streams = [sum((tile(i) for i in s), []) for s in ((7, 5, 4), (6, 3, 2, 1, 0, 8))]
    out = []
    assert len(streams[0]) == len(streams[1])
    for n in range(len(streams[0])):
        for s in range(2):
            out.append((s, *streams[s][n]))
    return out


def attention(nc, a, half, ps, ident, tri, qT, kT, v, osb_d):
    units = attention_units()
    NU = len(units)
    tiles = {}
    for s in range(2):
        for n, i in enumerate([u[1] for u in units if u[0] == s and u[4]]):
            tiles[s, i] = n
    seq = {}
    done_before = [0, 0]
    for u in units:
        seq[u] = done_before[u[0]]
        done_before[u[0]] += 1

    with ExitStack() as c:
        def sb(name, shape):
            return c.enter_context(nc.sbuf_tensor(name, shape, F32))
        ckr = sb("ckr", [PAST, W512])
        ckT = sb("ckT", [P, HH, PAST])
        cv = sb("cv", [PAST, W512])
        z = sb("z", [P, 2, W512])
        sp_ = sb("sp_", [P, 2, W512])
        arg = sb("arg", [P, 2, W512])
        ob = sb("ob", [P, 2, W512])
        Z, C, O, X = (0, 1), (2, 3), (4, 5), 6
        with Phase(nc, "cache_in ct_done ct_copied z_done z_copied abs_done e_done l_done sp_done sp_masked c_done "
                       "arg_done w_done w_masked c_next o_done o_copied out0 out1 dve_s") as (block, (
                cache_in, ct_done, ct_copied, z_done, z_copied, abs_done, e_done, l_done, sp_done, sp_masked, c_done,
                arg_done, w_done, w_masked, c_next, o_done, o_copied, out0, out1, dve_s)):
            outs = (out0, out1)
            diag = [n for n, u in enumerate(units) if u[3]]
            finals = [n for n, u in enumerate(units) if u[4]]

            def shape(u):
                m = rows(u[1])
                return m, (m if u[1] == NT - 1 and u[2] >= 0 else P)

            def view(ap, m):
                return ap[:, 0:HH * m].rearrange("p (h t) -> p h t", h=HH)

            @block.sync
            def _(sp):
                hs = bass.ds(half * HH, HH)
                sp.dma_start(ckr[:, :].rearrange("p (h c) -> p h c", h=HH), a["cache_sb_k"][0, 0, :, hs, :]).then_inc(cache_in, 16)
                sp.dma_start(cv[:, :].rearrange("p (h c) -> p h c", h=HH), a["cache_sb_v"][0, 0, :, hs, :]).then_inc(cache_in, 16)
                for n, f in enumerate(finals):
                    s, i = units[f][:2]
                    m = rows(i)
                    sp.wait_ge(o_copied, n + 1)
                    sp.dma_start(osb_d[bass.ds(half, 1), i * P:i * P + m, :].rearrange("a p n -> (a p) n"),
                                 ob[:m, n % 2, :]).then_inc(outs[n % 2], 16)
                sp.wait_ge(out0, 16 * 5)
                sp.wait_ge(out1, 16 * 4)

            @block.tensor
            def _(pe):
                pe.wait_ge(cache_in, 32)
                for h in range(HH):
                    mm = pe.transpose(ps[:, X, h * P:(h + 1) * P], ckr[:, h * P:(h + 1) * P], ident[:, :])
                mm.then_inc(ct_done, 1)
                pe.wait_ge(ct_copied, 1)

                def scores(n):
                    u = units[n]
                    m, kr = shape(u)
                    if n >= 2:
                        pe.wait_ge(z_copied, n - 1)
                    for h in range(HH):
                        keys = ckT[:, h, :] if u[2] < 0 else kT[:, h, u[2] * P:u[2] * P + kr]
                        mm = pe.matmul(ps[:kr, Z[n % 2], h * m:(h + 1) * m], keys, qT[:, h, u[1] * P:u[1] * P + m],
                                       start=True, stop=True)
                    mm.then_inc(z_done, 1)

                def sums(n):
                    u = units[n]
                    m, kr = shape(u)
                    pe.wait_ge(sp_done, n + 1)
                    if u[3]:
                        pe.wait_ge(sp_masked, diag.index(n) + 1)
                        before = [k for k in range(n) if units[k][0] == u[0]]
                        if before:
                            pe.wait_ge(arg_done, before[-1] + 1)
                    pe.matmul(ps[:, C[u[0]], 0:HH * m], tri[:kr, 1, :], sp_[:kr, n % 2, 0:HH * m], start=u[3], stop=True,
                              skip_group_check=True).then_inc(c_done, 1)

                def carry(n):
                    u = units[n]
                    m, kr = shape(u)
                    pe.wait_ge(arg_done, n + 1)
                    mm = None
                    if not u[4]:
                        mm = pe.matmul(ps[:, C[u[0]], 0:HH * m], tri[:kr, 2, :], sp_[:kr, n % 2, 0:HH * m], start=False,
                                       stop=True, skip_group_check=True)
                        mm.then_inc(c_next, 1)
                    else:
                        pe.sem_inc(c_next, 1)

                def values(n):
                    u = units[n]
                    m, kr = shape(u)
                    pe.wait_ge(w_done, n + 1)
                    if u[3]:
                        pe.wait_ge(w_masked, diag.index(n) + 1)
                        k = tiles[u[0], u[1]]
                        if k:
                            f = [x for x in finals if x < n and units[x][0] == u[0]]
                            pe.wait_ge(o_copied, finals.index(f[-1]) + 1)
                    for h in range(HH):
                        vals = cv[:, h * P:(h + 1) * P] if u[2] < 0 else v[:kr, u[2], h * P:(h + 1) * P]
                        mm = pe.matmul(ps[:m, O[u[0]], h * P:(h + 1) * P], arg[:kr, n % 2, h * m:(h + 1) * m], vals,
                                       start=u[3] and h == 0, stop=u[4], skip_group_check=True)
                    mm.then_inc(o_done, 1)

                scores(0)
                for n in range(NU + 1):
                    if n + 1 < NU:
                        scores(n + 1)
                    if n < NU:
                        sums(n)
                    if n >= 1:
                        carry(n - 1)
                        values(n - 1)

            @block.scalar
            def _(act):
                act.wait_ge(ct_done, 1)
                act.activation(ckT[:, :, :], ps[:, X, :].rearrange("p (h c) -> p h c", h=HH), ACT.Copy).then_inc(ct_copied, 1)

                def front(n):
                    u = units[n]
                    m, kr = shape(u)
                    w_ = HH * m
                    act.wait_ge(z_done, n + 1)
                    if n >= 2:
                        act.wait_ge(arg_done, n - 1)
                    act.activation(z[:kr, n % 2, 0:w_], ps[:kr, Z[n % 2], 0:w_], ACT.Copy, scale=SCALE).then_inc(z_copied, 1)
                    if n >= 2:
                        act.wait_ge(c_next, n - 1)
                    act.wait_ge(abs_done, n + 1)
                    act.activation(sp_[:kr, n % 2, 0:w_], sp_[:kr, n % 2, 0:w_], ACT.Exp, scale=-1.0).then_inc(e_done, 1)
                    act.wait_ge(e_done, n + 1)
                    act.activation(sp_[:kr, n % 2, 0:w_], sp_[:kr, n % 2, 0:w_], ACT.Ln, bias=1.0).then_inc(l_done, 1)

                def back(n):
                    u = units[n]
                    m, kr = shape(u)
                    w_ = HH * m
                    act.wait_ge(arg_done, n + 1)
                    act.activation(arg[:kr, n % 2, 0:w_], arg[:kr, n % 2, 0:w_], ACT.Exp).then_inc(w_done, 1)

                for n in range(NU + 1):
                    if n < NU:
                        front(n)
                    if n >= 1:
                        back(n - 1)

            @block.vector
            def _(dve):
                ch = Chain(dve, dve_s)

                def front(n):
                    u = units[n]
                    m, kr = shape(u)
                    w_ = HH * m
                    dve.wait_ge(z_copied, n + 1)
                    if n >= 2:
                        dve.wait_ge(c_next, n - 1)
                    absolute(dve, sp_[:kr, n % 2, 0:w_], z[:kr, n % 2, 0:w_]).then_inc(abs_done, 1)

                def middle(n):
                    u = units[n]
                    m, kr = shape(u)
                    w_ = HH * m
                    dve.wait_ge(l_done, n + 1)
                    dve.scalar_tensor_tensor(out=sp_[:kr, n % 2, 0:w_], in0=z[:kr, n % 2, 0:w_], scalar=0.0,
                                             in1=sp_[:kr, n % 2, 0:w_], op0=ALU.max, op1=ALU.add).then_inc(sp_done, 1)

                def back(n):
                    u = units[n]
                    m, kr = shape(u)
                    w_ = HH * m
                    dve.wait_ge(c_done, n + 1)
                    if n >= 2:
                        dve.wait_ge(o_done, n - 1)
                    if u[3]:
                        ch(dve.tensor_tensor(arg[:kr, n % 2, 0:w_], z[:kr, n % 2, 0:w_], ps[:kr, C[u[0]], 0:w_], ALU.subtract))
                        dve.tensor_scalar(arg[:kr, n % 2, 0:w_], arg[:kr, n % 2, 0:w_], 0.0, None, ALU.min).then_inc(arg_done, 1)
                    else:
                        dve.tensor_tensor(arg[:kr, n % 2, 0:w_], z[:kr, n % 2, 0:w_], ps[:kr, C[u[0]], 0:w_],
                                          ALU.subtract).then_inc(arg_done, 1)

                def outputs(n):
                    if n < 0 or not units[n][4]:
                        return
                    k = finals.index(n)
                    m = rows(units[n][1])
                    dve.wait_ge(o_done, n + 1)
                    if k >= 2:
                        dve.wait_ge(outs[k % 2], 16 * (k // 2))
                    dve.tensor_copy(ob[:m, k % 2, :], ps[:m, O[units[n][0]], :]).then_inc(o_copied, 1)

                front(0)
                for n in range(NU):
                    middle(n)
                    if n + 1 < NU:
                        front(n + 1)
                    back(n)
                    outputs(n - 1)
                outputs(NU - 1)

            @block.gpsimd
            def _(pool):
                for k, n in enumerate(diag):
                    u = units[n]
                    m, kr = shape(u)
                    below = tri[:kr, 0:1, 0:m].to_broadcast([kr, HH, m])
                    pool.wait_ge(sp_done, n + 1)
                    s_ = view(sp_[:kr, n % 2, :], m)
                    pool.tensor_tensor(s_, s_, below, ALU.mult).then_inc(sp_masked, 1)
                    pool.wait_ge(w_done, n + 1)
                    w_ = view(arg[:kr, n % 2, :], m)
                    pool.tensor_tensor(w_, w_, below, ALU.mult).then_inc(w_masked, 1)


def project_hgrn(nc, a, half, w, xT, ps, lbc, qT, kT, bT, v):
    cols = (C_HF, C_HQ, C_HI)
    steps = Steps("TTR")
    BANKS = 8
    with ExitStack() as c:
        tmp = c.enter_context(nc.sbuf_tensor("ptmp", [P, T], F32))
        keep = c.enter_context(nc.sbuf_tensor("pkeep", [P, T], F32))
        low = c.enter_context(nc.sbuf_tensor("plow", [P, T], F32))
        with Phase(nc, "w_in0 w_in1 mm_done act_read dve_s act_s") as (block, (
                w_in0, w_in1, mm_done, act_read, dve_s, act_s)):
            w_in = (w_in0, w_in1)
            NS = len(steps.list)
            TURNS = 11
            SETUP = 2

            @block.sync
            def _(sp):
                load_weights(sp, nc, a, w, half, cols, w_in, mm_done, steps.last)

            @block.tensor
            def _(pe):
                products(pe, steps, w, xT, ps, BANKS, w_in, mm_done, (act_read,))

            @block.scalar
            def _(act):
                n = 0

                def copy_out(lo, hi):
                    for n in range(lo, hi):
                        g, f, i = steps.list[n]
                        act.wait_ge(mm_done, n + 1)
                        if f == "T":
                            c0, cw = CHUNKS[i[1]]
                            act.activation((bT, qT)[g][:, i[0], c0:c0 + cw], ps[:, n % BANKS, 0:cw],
                                           (ACT.Copy, ACT.Silu)[g]).then_inc(act_read, 1)
                        else:
                            m = rows(i)
                            act.activation(v[:m, i, :], ps[:m, n % BANKS, :], ACT.Copy).then_inc(act_read, 1)

                def turn(*args, **kw):
                    nonlocal n
                    act.activation(*args, **kw).then_inc(act_s, 1)
                    n += 1
                    act.wait_ge(act_s, n)

                copied = 3
                copy_out(0, copied)
                for h in range(HH):
                    base = SETUP + TURNS * h
                    act.wait_ge(dve_s, base + 2)
                    turn(tmp[:, :], tmp[:, :], ACT.Exp, scale=-1.0)
                    turn(tmp[:, :], tmp[:, :], ACT.Ln, bias=1.0)
                    act.wait_ge(dve_s, base + 4)
                    turn(kT[:, h, :], kT[:, h, :], ACT.Exp)
                    act.wait_ge(dve_s, base + 7)
                    turn(tmp[:, :], tmp[:, :], ACT.Exp, scale=-1.0)
                    turn(tmp[:, :], tmp[:, :], ACT.Ln, bias=1.0)
                    copy_out(copied, copied + 5)
                    copied += 5
                copy_out(copied, NS)

            @block.vector
            def _(dve):
                ch = Chain(dve, dve_s)
                ch(dve.memset(keep[:, :], 1.0))
                ch(dve.memset(keep[:, 0:T:P], 0.0))
                for h in range(HH):
                    A = bT[:, h, :]
                    NLb = lbc[:, 2, bass.ds(half * HH + h, 1)]
                    om = lbc[:, 1, bass.ds(half * HH + h, 1)]
                    na = 5 * h
                    dve.wait_ge(act_read, 3 * h + 3)
                    ch(absolute(dve, tmp[:, :], A))
                    ch(dve.tensor_scalar(kT[:, h, :], A, 0.0, None, ALU.min))
                    dve.wait_ge(act_s, na + 2)
                    ch(dve.tensor_tensor(tmp[:, :], kT[:, h, :], tmp[:, :], ALU.subtract))
                    ch(dve.tensor_tensor(kT[:, h, :], tmp[:, :], A, ALU.subtract))
                    ch(dve.tensor_scalar(A, A, NLb, None, ALU.add))
                    ch(dve.scalar_tensor_tensor(out=low[:, :], in0=A, scalar=0.0, in1=tmp[:, :], op0=ALU.min,
                                                op1=ALU.subtract))
                    ch(absolute(dve, tmp[:, :], A))
                    dve.wait_ge(act_s, na + 5)
                    ch(dve.tensor_tensor(tmp[:, :], tmp[:, :], low[:, :], ALU.subtract))
                    ch(dve.tensor_scalar(tmp[:, :], tmp[:, :], 0.0, None, ALU.min))
                    ch(dve.tensor_tensor_scan(A, keep[:, :], tmp[:, :], 0.0, ALU.mult, ALU.add))
                    ch(dve.tensor_scalar(kT[:, h, :], kT[:, h, :], om, None, ALU.mult))


def hgrn(nc, a, o, half, ps, ident, masks, x, qT, kT, bT, v, ohg_d):
    PARTS = [(0, 512), (512, T - 512)]
    parts = [(h, *p) for h in range(HH) for p in PARTS]
    chunks = []
    for n, (h, c0, cw) in enumerate(parts):
        for c in range(c0, c0 + cw, P):
            chunks.append((n, h, c, min(P, T - c), c // P))
    NC = len(chunks)
    last_of = {n: max(i for i, k in enumerate(chunks) if k[0] == n) for n in range(len(parts))}
    first_of = {n: min(i for i, k in enumerate(chunks) if k[0] == n) for n in range(len(parts))}
    PER = 2 * NL + 2
    with ExitStack() as c:
        def sb(name, shape):
            return c.enter_context(nc.sbuf_tensor(name, shape, F32))
        pm = sb("pm", [P, 2, NL + 1, P])
        aT = sb("aT", [P, 2, P])
        ke = sb("ke", [P, 2, P])
        orow = sb("orow", [P, 2, P])
        eb = sb("eb", [P, HH, NT])
        S = sb("S", [P, 4, P])
        O, KE, SU = (4, 5), 6, 7
        with Phase(nc, "zeroed s_in diff_done exp_done eb_done x_done p_done masked a_done o_done o_copied o_out0 o_out1 "
                       "ke_done ke_copied su_done s_done s_out") as (block, (
                zeroed, s_in, diff_done, exp_done, eb_done, x_done, p_done, masked, a_done, o_done, o_copied, o_out0, o_out1,
                ke_done, ke_copied, su_done, s_done, s_out)):
            o_out = (o_out0, o_out1)

            def src_state(k):
                return 2 if k[4] == NT - 1 else k[4] % 2

            def dst_state(k):
                return 3 if k[4] == NT - 1 else (k[4] + 1) % 2

            def halves(n):
                h, c0, cw = parts[n]
                out = []
                for i, hw in enumerate(LEVELS):
                    w_ = cw // (2 * hw) * (2 * hw)
                    for side in range(2):
                        out.append((i, side, hw, c0, w_))
                return out

            def seg(ap, c0, w_, hw, side):
                return ap[:, c0:c0 + w_].rearrange("p (g u) -> p g u", u=2 * hw)[:, :, side * hw:side * hw + hw]

            def ends(c0, cw):
                out = [(c0, cw // P * P, P)]
                if cw % P:
                    out.append((c0 + cw // P * P, cw % P, cw % P))
                return out

            @block.sync
            def _(sp):
                for h in range(HH):
                    if h >= 1:
                        sp.wait_ge(s_done, NT * h)
                    sp.dma_start(S[:, 2, :], a["state_hgrn"][0, 0, bass.ds(half * HH + h, 1), :, :]
                                 .rearrange("a c v -> (a c) v")).then_inc(s_in, 16)

            @block.gpsimd
            def _(pool):
                for n, (h, c0, cw) in enumerate(parts):
                    base = n * (NL + 2)
                    for i, side, hw, b0, w_ in halves(n):
                        if side == 0:
                            pool.wait_ge(exp_done, base + i + 1)
                        q = (kT, qT)[side][:, h, :]
                        xs = seg(x[:, i, :], b0, w_, hw, side)
                        pool.tensor_tensor(xs, xs, seg(q, b0, w_, hw, side), ALU.mult).then_inc(x_done, 1)
                    for i, q in ((NL, qT), (NL + 1, kT)):
                        pool.wait_ge(exp_done, base + i + 1)
                        xs = x[:, i, c0:c0 + cw]
                        pool.tensor_tensor(xs, xs, q[:, h, c0:c0 + cw], ALU.mult).then_inc(x_done, 1)

            @block.scalar
            def _(act):
                for h in range(HH):
                    act.activation(eb[:, h, 0:NT - 1], bT[:, h, P - 1:SEQ:P], ACT.Exp).then_inc(eb_done, 1)
                    act.activation(eb[:, h, NT - 1:NT], bT[:, h, T - 1:T], ACT.Exp).then_inc(eb_done, 1)

                def exps(n):
                    h, c0, cw = parts[n]
                    for i in range(NL + 2):
                        w_ = cw // (2 * LEVELS[i]) * (2 * LEVELS[i]) if i < NL else cw
                        act.wait_ge(diff_done, 2 * (NL + 2) * n + 2 * (i + 1))
                        act.activation(x[:, i, c0:c0 + w_], x[:, i, c0:c0 + w_], ACT.Exp).then_inc(exp_done, 1)

                def copies(j):
                    k = chunks[j]
                    m = k[3]
                    act.wait_ge(ke_done, j + 1)
                    if j >= 2:
                        act.wait_ge(su_done, j - 1)
                    act.activation(ke[:m, j % 2, :], ps[:m, KE, 0:P], ACT.Copy).then_inc(ke_copied, 1)
                    act.wait_ge(o_done, j + 1)
                    if j >= 2:
                        act.wait_ge(o_out[j % 2], 16 * (j // 2))
                    act.activation(orow[:m, j % 2, :], ps[:m, O[j % 2], 0:P], ACT.Copy).then_inc(o_copied, 1)
                    act.wait_ge(o_copied, j + 1)
                    act.dma_start(ohg_d[bass.ds(half, 1), k[4] * P:k[4] * P + m, k[1] * P:(k[1] + 1) * P]
                                  .rearrange("a p n -> (a p) n"), orow[:m, j % 2, :]).then_inc(o_out[j % 2], 16)

                exps(0)
                for n in range(len(parts)):
                    if n + 1 < len(parts):
                        exps(n + 1)
                    for j in range(first_of[n], last_of[n] + 1):
                        copies(j)
                    if n % 2:
                        h = parts[n][0]
                        act.wait_ge(s_done, NT * (h + 1))
                        hd = bass.ds(half * HH + h, 1)
                        act.dma_start(o[4][0, 0, hd, :, :].rearrange("a c v -> (a c) v"), S[:, 0, :]).then_inc(s_out, 16)
                        act.dma_start(o[7][0, 0, hd, :, :].rearrange("a c v -> (a c) v"), S[:, 3, :]).then_inc(s_out, 16)
                act.wait_ge(s_out, 32 * HH)
                act.wait_ge(o_out0, 16 * (NC // 2))
                act.wait_ge(o_out1, 16 * (NC // 2))

            @block.vector
            def _(dve):
                def diffs(n):
                    h, c0, cw = parts[n]
                    b = bT[:, h, :]
                    if n >= 2:
                        dve.wait_ge(o_done, last_of[n - 2] + 1)
                        dve.wait_ge(ke_done, last_of[n - 2] + 1)
                        dve.wait_ge(p_done, last_of[n - 2] + 1)
                    for i, side, hw, b0, w_ in halves(n):
                        mid = b[:, b0:b0 + w_].rearrange("p (g u) -> p g u", u=2 * hw)[:, :, hw - 1:hw] \
                            .to_broadcast([P, w_ // (2 * hw), hw])
                        bs, xs = seg(b, b0, w_, hw, side), seg(x[:, i, :], b0, w_, hw, side)
                        dve.tensor_tensor(xs, *((mid, bs) if side == 0 else (bs, mid)), ALU.subtract).then_inc(diff_done, 1)
                    dve.tensor_copy(x[:, NL, c0:c0 + cw], b[:, c0:c0 + cw]).then_inc(diff_done, 2)
                    es = ends(c0, cw)
                    for e0, ew, u in es:
                        g = ew // u
                        bs = b[:, e0:e0 + ew].rearrange("p (g u) -> p g u", u=u)
                        xs = x[:, NL + 1, e0:e0 + ew].rearrange("p (g u) -> p g u", u=u)
                        dve.tensor_tensor(xs, bs[:, :, u - 1:u].to_broadcast([P, g, u]), bs, ALU.subtract) \
                            .then_inc(diff_done, 2 // len(es))

                def scores(j):
                    n, h, c0, m, t = chunks[j]
                    s = NL + 1 if m == P else NL
                    dve.wait_ge(p_done, j + 1)
                    if j >= 2:
                        dve.wait_ge(a_done, j - 1)
                    pp = ps[:m, 2 * (j % 2):2 * (j % 2) + 2, :].rearrange("p b (l t) -> p (b l) t", l=4)[:, 0:s, 0:m]
                    dve.tensor_tensor(pm[:m, j % 2, 0:s, 0:m], pp, masks[:m, 0:s, 0:m], ALU.mult).then_inc(masked, 1)
                    dve.wait_ge(masked, j + 1)
                    if j >= 2:
                        dve.wait_ge(o_done, j - 1)
                    dve.tensor_reduce(aT[:m, j % 2, 0:m], pm[:m, j % 2, 0:s, 0:m].rearrange("p l t -> p t l"), AX.X,
                                      ALU.add).then_inc(a_done, 1)

                def state(j):
                    k = chunks[j]
                    dve.wait_ge(su_done, j + 1)
                    dve.wait_ge(o_done, max(j - 1, 1))
                    if j >= 1:
                        dve.wait_ge(s_done, j)
                    if k[4] == 0:
                        dve.wait_ge(eb_done, 2 * HH)
                    if k[4] == NT - 1:
                        dve.wait_ge(s_in, 16 * (k[1] + 1))
                    dve.scalar_tensor_tensor(out=S[:, dst_state(k), :], in0=S[:, src_state(k), :],
                                             scalar=eb[:, k[1], k[4]:k[4] + 1], in1=ps[:, SU, 0:P], op0=ALU.mult,
                                             op1=ALU.add).then_inc(s_done, 1)

                diffs(0)
                for n in range(len(parts)):
                    if n + 1 < len(parts):
                        diffs(n + 1)
                    for j in range(first_of[n], last_of[n] + 1):
                        if chunks[j][4] == 0:
                            if chunks[j][1]:
                                dve.wait_ge(s_out, 32 * chunks[j][1])
                            dve.memset(S[:, 0, :], 0.0).then_inc(zeroed, 1)
                            dve.wait_ge(zeroed, chunks[j][1] + 1)
                        scores(j)
                        state(j)

            @block.tensor
            def _(pe):
                def products(j):
                    n, h, c0, m, t = chunks[j]
                    if j == first_of[n]:
                        pe.wait_ge(x_done, PER * (n + 1))
                    if j >= 2:
                        pe.wait_ge(masked, j - 1)
                    b0 = 2 * (j % 2)
                    pe.matmul(ps[:m, b0, 0:m], kT[:, h, c0:c0 + m], qT[:, h, c0:c0 + m], start=True, stop=True)
                    for i in range(NL if m == P else NL - 1):
                        xs = x[:, i, c0:c0 + m]
                        mm = pe.matmul(ps[:m, b0 + (i + 1) // 4, (i + 1) % 4 * P:(i + 1) % 4 * P + m], xs, xs,
                                       start=True, stop=True)
                    mm.then_inc(p_done, 1)
                    if j >= 1:
                        pe.wait_ge(ke_copied, j)
                    pe.transpose(ps[:m, KE, 0:P], x[:, NL + 1, c0:c0 + m], ident[:, :]).then_inc(ke_done, 1)

                def outputs(j):
                    k = chunks[j]
                    n, h, c0, m, t = k
                    vals = v[:m, t, h * P:(h + 1) * P]
                    pe.wait_ge(a_done, j + 1)
                    if j >= 2:
                        pe.wait_ge(o_copied, j - 1)
                    pe.matmul(ps[:m, O[j % 2], 0:P], aT[:m, j % 2, 0:m], vals, start=True, stop=False)
                    if t == 0:
                        pe.wait_ge(zeroed, h + 1)
                    if t == NT - 1:
                        pe.wait_ge(s_in, 16 * (h + 1))
                    elif j >= 1:
                        pe.wait_ge(s_done, j)
                    pe.matmul(ps[:m, O[j % 2], 0:P], x[:, NL, c0:c0 + m], S[:, src_state(k), :], start=False,
                              stop=True).then_inc(o_done, 1)
                    pe.wait_ge(ke_copied, j + 1)
                    if j >= 1:
                        pe.wait_ge(s_done, j)
                    pe.matmul(ps[:, SU, 0:P], ke[:m, j % 2, :], vals, start=True, stop=True).then_inc(su_done, 1)

                products(0)
                for j in range(NC):
                    if j + 1 < NC and chunks[j + 1][0] == chunks[j][0]:
                        products(j + 1)
                        outputs(j)
                    else:
                        outputs(j)
                        if j + 1 < NC:
                            products(j + 1)


def merge(nc, a, half, w, xT, ps, ident, g1, osb_d, ohg_d, mT):
    cols = (C_HG, C_GH, C_GS)
    steps = Steps("RRR")
    BANKS = 6
    with ExitStack() as c:
        def sb(name, shape):
            return c.enter_context(nc.sbuf_tensor(name, shape, F32))
        og = sb("og", [P, NT, W512])
        oa = sb("oa", [P, NT, W512])
        s = sb("sg", [P, 2, W512])
        sq = sb("sq", [P, P])
        rs = sb("rs", [P, NT, 8])
        hn = sb("hn", [P, P])
        with Phase(nc, "w_in0 w_in1 mm_done act_read loads squares var roots rstd s_done g0 g0n on prod m_done t_done t_copied dve_s") as (
                block, (w_in0, w_in1, mm_done, act_read, loads, squares, var, roots, rstd, s_done, g0, g0n, on, prod, m_done,
                        t_done, t_copied, dve_s)):
            w_in = (w_in0, w_in1)

            @block.sync
            def _(sp):
                load_weights(sp, nc, a, w, half, cols[:2], w_in, mm_done, steps.last)
                sp.dma_start(hn[:, :], a["hg_norm"][0].partition_broadcast(P)).then_inc(loads, 16)
                for buf, d in ((og, ohg_d), (oa, osb_d)):
                    sp.dma_start(buf[:, 0:NT - 1, :], d[bass.ds(half, 1), 0:SEQ, :].rearrange("a (t p) n -> p (a t) n", p=P)).then_inc(loads, 16)
                    sp.dma_start(buf[:DEC, NT - 1, :], d[bass.ds(half, 1), SEQ:T, :].rearrange("a p n -> (a p) n")).then_inc(loads, 16)
                sp.wait_ge(mm_done, steps.last[0])
                src = a["w_in"][0].rearrange("(k p) n -> p k n", p=P)[:, :, bass.ds(half * W512 + cols[2], W512)]
                sp.dma_start(w[0], src).then_inc(w_in[0], 16)
                sp.wait_ge(loads, 80)

            def turn(pe, t):
                m = rows(t)
                pe.wait_ge(m_done, t + 1)
                if t >= 2:
                    pe.wait_ge(t_copied, t - 1)
                for h in range(HH):
                    mm = pe.transpose(ps[:, BANKS + t % 2, h * P:h * P + m], g1[:m, t, h * P:(h + 1) * P], ident[:m, :m])
                mm.then_inc(t_done, 1)

            @block.tensor
            def _(pe):
                seen = set()
                for n, (g, f, t) in enumerate(steps.list):
                    m = rows(t)
                    if g not in seen:
                        seen.add(g)
                        pe.wait_ge(w_in[g % 2], 16 * (g // 2 + 1))
                    if n >= BANKS:
                        pe.wait_ge(s_done, n - BANKS + 1)
                        e = n - BANKS
                        if e < NT:
                            pe.wait_ge(g0, e + 1)
                    for k in range(KT):
                        mm = pe.matmul(ps[:m, n % BANKS, :], xT[:, k, t * P:t * P + m], w[g % 2][:, k, :],
                                       start=k == 0, stop=k == KT - 1)
                    mm.then_inc(mm_done, 1)
                    if g == 2 and t >= 2:
                        turn(pe, t - 2)
                for t in (NT - 2, NT - 1):
                    turn(pe, t)

            @block.scalar
            def _(act):
                act.wait_ge(loads, 80)
                for t in range(NT):
                    m = rows(t)
                    for h in range(HH):
                        act.activation(sq[:m, :], og[:m, t, h * P:(h + 1) * P], ACT.Square,
                                       accum_out=rs[:m, t, h:h + 1]).then_inc(squares, 1)
                        act.wait_ge(squares, HH * t + h + 1)
                for t in range(NT):
                    m = rows(t)
                    act.wait_ge(var, t + 1)
                    act.activation(rs[:m, t, 4:8], rs[:m, t, 4:8], ACT.Sqrt).then_inc(roots, 1)

                def copy(t):
                    m = rows(t)
                    act.wait_ge(t_done, t + 1)
                    act.activation(mT[:, bass.ds(half * HH, HH), t * P:t * P + m],
                                   ps[:, BANKS + t % 2, :].rearrange("p (h n) -> p h n", h=HH)[:, :, 0:m], ACT.Copy).then_inc(t_copied, 1)

                for n, (g, f, t) in enumerate(steps.list):
                    m = rows(t)
                    act.wait_ge(mm_done, n + 1)
                    if n >= 2:
                        e = n - 2
                        if e < NT:
                            act.wait_ge(g0, e + 1)
                        elif e < 2 * NT:
                            act.wait_ge(prod, e - NT + 1)
                        else:
                            act.wait_ge(m_done, e - 2 * NT + 1)
                    act.activation(s[:m, n % 2, :], ps[:m, n % BANKS, :], ACT.Sigmoid).then_inc(s_done, 1)
                    if g == 2 and t >= 3:
                        copy(t - 3)
                for t in (NT - 3, NT - 2, NT - 1):
                    copy(t)

            @block.vector
            def _(dve):
                ch = Chain(dve, dve_s)
                for t in range(NT):
                    m = rows(t)
                    dve.wait_ge(squares, HH * (t + 1))
                    dve.tensor_scalar(rs[:m, t, 4:8], rs[:m, t, 0:4], 1.0 / P, RMS_EPS, ALU.mult, ALU.add).then_inc(var, 1)
                for t in range(NT):
                    m = rows(t)
                    dve.wait_ge(roots, t + 1)
                    ch(dve.reciprocal(rs[:m, t, 0:4], rs[:m, t, 4:8]))
                for t in range(NT):
                    m = rows(t)
                    dve.wait_ge(s_done, t + 1)
                    dve.tensor_tensor(g1[:m, t, :], s[:m, t % 2, :], ps[:m, t % BANKS, :], ALU.mult).then_inc(g0, 1)
                    dve.wait_ge(g0, t + 1)
                    for h in range(HH):
                        hs = slice(h * P, (h + 1) * P)
                        dve.scalar_tensor_tensor(out=g1[:m, t, hs], in0=og[:m, t, hs], scalar=rs[:m, t, h:h + 1],
                                                 in1=g1[:m, t, hs], op0=ALU.mult, op1=ALU.mult).then_inc(g0n, 1)
                for t in range(NT):
                    m = rows(t)
                    dve.wait_ge(on, t + 1)
                    dve.wait_ge(s_done, NT + t + 1)
                    dve.tensor_tensor(g1[:m, t, :], g1[:m, t, :], s[:m, (NT + t) % 2, :], ALU.mult).then_inc(prod, 1)
                for t in range(NT):
                    m = rows(t)
                    n = 2 * NT + t
                    dve.wait_ge(s_done, n + 1)
                    ch(dve.tensor_tensor(oa[:m, t, :], oa[:m, t, :], s[:m, n % 2, :], ALU.mult))
                    dve.wait_ge(prod, t + 1)
                    dve.tensor_tensor(g1[:m, t, :], g1[:m, t, :], oa[:m, t, :], ALU.add).then_inc(m_done, 1)

            @block.gpsimd
            def _(pool):
                pool.wait_ge(loads, 80)
                for t in range(NT):
                    m = rows(t)
                    pool.wait_ge(g0n, HH * (t + 1))
                    gv = g1[:m, t, :].rearrange("p (h c) -> p h c", h=HH)
                    pool.tensor_tensor(gv, gv, hn[:m, :].unsqueeze(1).to_broadcast([m, HH, P]), ALU.mult).then_inc(on, 1)


def output_projection(nc, a, wbuf, ps, ident, gcol, bcol, st, mT, xT, xn_d, h2_d):
    wo = wbuf[:, :, :].rearrange("p a b -> p (a b)")[:, 0:HEADS * D].rearrange("p (k n) -> p k n", k=HEADS)
    with ExitStack() as c:
        xr = c.enter_context(nc.sbuf_tensor("xr", [P, 2, D], F32))
        y = c.enter_context(nc.sbuf_tensor("y1", [P, 2, D], F32))
        with Phase(nc, "par_in x_in0 x_in1 mm_done sum_done dve_s var_ready root_ready y_ready t_done t_act stored0 stored1") as (block, (
                par_in, x_in0, x_in1, mm_done, sum_done, dve_s, var_ready, root_ready, y_ready, t_done, t_act, stored0, stored1)):
            x_in, stored = (x_in0, x_in1), (stored0, stored1)

            @block.sync
            def _(sp):
                sp.dma_start(wo, a["w_out"][0].rearrange("(k p) n -> p k n", p=P)).then_inc(par_in, 16)
                sp.dma_start(gcol[:, :], a["ln1_g"][0].partition_broadcast(P)).then_inc(par_in, 16)
                sp.dma_start(bcol[:, :], a["ln1_b"][0].partition_broadcast(P)).then_inc(par_in, 16)
                for t in range(NT):
                    m = rows(t)
                    if t >= 2:
                        sp.wait_ge(sum_done, t - 1)
                    sp.dma_start(xr[:m, t % 2, :], xn_d[t * P:t * P + m, :]).then_inc(x_in[t % 2], 16)
                sp.wait_ge(par_in, 48)

            @block.tensor
            def _(pe):
                pe.wait_ge(par_in, 48)

                def turn(t):
                    m = rows(t)
                    pe.wait_ge(y_ready, t + 1)
                    if t >= 2:
                        pe.wait_ge(t_act, 2 * (t - 1))
                    for k in range(KT):
                        mm = pe.transpose(ps[:, 4 + 2 * (t % 2) + k // 4, (k % 4) * P:(k % 4) * P + m],
                                          y[:m, t % 2, k * P:(k + 1) * P], ident[:m, :m])
                    mm.then_inc(t_done, 1)

                for t in range(NT):
                    m = rows(t)
                    if t >= 2:
                        pe.wait_ge(sum_done, t - 1)
                    for b in range(2):
                        for k in range(HEADS):
                            mm = pe.matmul(ps[:m, 2 * (t % 2) + b, :], mT[:, k, t * P:t * P + m], wo[:, k, b * 512:(b + 1) * 512],
                                           start=k == 0, stop=k == HEADS - 1)
                    mm.then_inc(mm_done, 1)
                    if t >= 1:
                        turn(t - 1)
                turn(NT - 1)

            @block.vector
            def _(dve):
                ch = Chain(dve, dve_s)
                for t in range(NT):
                    m = rows(t)
                    dve.wait_ge(mm_done, t + 1)
                    dve.wait_ge(x_in[t % 2], 16 * (t // 2 + 1))
                    if t >= 2:
                        dve.wait_ge(stored[t % 2], 16 * (t // 2))
                        dve.wait_ge(t_done, t - 1)
                    pp = ps[:m, 2 * (t % 2):2 * (t % 2) + 2, :].rearrange("p b n -> p (b n)")
                    dve.scalar_tensor_tensor(out=y[:m, t % 2, :], in0=xr[:m, t % 2, :], scalar=ALPHA, in1=pp, op0=ALU.mult,
                                             op1=ALU.add).then_inc(sum_done, 1)
                    dve.wait_ge(sum_done, t + 1)
                    layer_norm_rows(dve, ch, m, y[:, t % 2, :], y[:, t % 2, :], st[:, t % 2, :], gcol, var_ready, root_ready, t)
                    dve.tensor_tensor(y[:m, t % 2, :], y[:m, t % 2, :], bcol[:m, :], ALU.add).then_inc(y_ready, 1)

            @block.scalar
            def _(act):
                for t in range(NT):
                    m = rows(t)
                    act.wait_ge(var_ready, t + 1)
                    act.activation(st[:m, t % 2, 15:16], st[:m, t % 2, 14:15], ACT.Sqrt).then_inc(root_ready, 1)
                    act.wait_ge(y_ready, t + 1)
                    act.dma_start(h2_d[t * P:t * P + m, :], y[:m, t % 2, :]).then_inc(stored[t % 2], 16)
                    act.wait_ge(t_done, t + 1)
                    for b in range(2):
                        act.activation(xT[:, 4 * b:4 * b + 4, t * P:t * P + m],
                                       ps[:, 4 + 2 * (t % 2) + b, :].rearrange("p (k n) -> p k n", k=4)[:, :, 0:m],
                                       ACT.Copy).then_inc(t_act, 1)
                act.wait_ge(stored[0], 16 * 5)
                act.wait_ge(stored[1], 16 * 4)


def router(nc, a, ps, xT, gates, chosen, picks):
    with ExitStack() as c:
        def sb(name, shape):
            return c.enter_context(nc.sbuf_tensor(name, shape, F32))
        wr = sb("wr", [P, KT, NE])
        rb = sb("rb", [P, NE])
        s = sb("rs_", [P, 2, NE])
        sbm = sb("sbm", [P, NE])
        rep = sb("rep", [P, NE])
        g8 = sb("g8", [P, NGRP, 8])
        gs = sb("gs", [P, NGRP])
        cmp_ = sb("cmp_", [P, 2, NGRP, NGRP])
        earlier = sb("earlier", [P, NGRP, NGRP])
        rank = sb("rank", [P, 3, NGRP])
        top = sb("top", [P, 8])
        tot = sb("tot", [P, 2])
        with Phase(nc, "r_in pooled memo mm_done s_done dve_s") as (block, (r_in, pooled, memo, mm_done, s_done, dve_s)):
            @block.sync
            def _(sp):
                sp.dma_start(wr[:, :, :], a["w_router"][0].rearrange("(k p) n -> p k n", p=P)).then_inc(r_in, 16)
                sp.dma_start(rb[:, :], a["router_bias"][0].partition_broadcast(P)).then_inc(r_in, 16)
                sp.wait_ge(r_in, 32)

            @block.gpsimd
            def _(pool):
                pool.memset(earlier[:, :, :], 1.0).then_inc(memo, 1)
                pool.wait_ge(memo, 1)
                pool.affine_select(out=earlier[:, :, :], in_=earlier[:, :, :], compare_op=ALU.is_ge, fill=0.0, base=-1,
                                   pattern=[[1, NGRP], [-1, NGRP]], channel_multiplier=0).then_inc(pooled, 1)

            @block.tensor
            def _(pe):
                pe.wait_ge(r_in, 32)
                for t in range(NT):
                    m = rows(t)
                    if t >= 2:
                        pe.wait_ge(s_done, t - 1)
                    for k in range(KT):
                        mm = pe.matmul(ps[:m, t % 2, 0:NE], xT[:, k, t * P:t * P + m], wr[:, k, :], start=k == 0, stop=k == KT - 1)
                    mm.then_inc(mm_done, 1)

            STEPS = 27

            @block.scalar
            def _(act):
                for t in range(NT):
                    m = rows(t)
                    act.wait_ge(mm_done, t + 1)
                    if t >= 2:
                        act.wait_ge(dve_s, STEPS * (t - 1))
                    act.activation(s[:m, t % 2, :], ps[:m, t % 2, 0:NE], ACT.Sigmoid).then_inc(s_done, 1)

            @block.vector
            def _(dve):
                ch = Chain(dve, dve_s)
                dve.wait_ge(pooled, 1)
                dve.wait_ge(r_in, 32)
                for t in range(NT):
                    m = rows(t)
                    sc = s[:m, t % 2, :]
                    B = [m, NGRP, NGRP]
                    dve.wait_ge(s_done, t + 1)
                    ch(dve.tensor_tensor(sbm[:m, :], sc, rb[:m, :], ALU.add))
                    for g in range(NGRP):
                        ch(dve.max(g8[:m, g, :], sbm[:m, g * EPG:(g + 1) * EPG]))
                    ch(dve.tensor_tensor(gs[:m, :], g8[:m, :, 0], g8[:m, :, 1], ALU.add))
                    own, other = gs[:m, :].unsqueeze(2).to_broadcast(B), gs[:m, :].unsqueeze(1).to_broadcast(B)
                    ch(dve.tensor_tensor(cmp_[:m, 0, :, :], other, own, ALU.is_gt))
                    ch(dve.tensor_tensor(cmp_[:m, 1, :, :], other, own, ALU.is_equal))
                    ch(dve.tensor_tensor(cmp_[:m, 1, :, :], cmp_[:m, 1, :, :], earlier[:m, :, :], ALU.mult))
                    ch(dve.tensor_tensor(cmp_[:m, 0, :, :], cmp_[:m, 0, :, :], cmp_[:m, 1, :, :], ALU.add))
                    ch(dve.tensor_reduce(rank[:m, 0, :], cmp_[:m, 0, :, :], AX.X, ALU.add))
                    ch(dve.tensor_scalar(rank[:m, 1, :], rank[:m, 0, :], float(TOPG), None, ALU.is_lt))
                    ch(dve.tensor_scalar(rank[:m, 2, :], rank[:m, 1, :], -1.0, -NEG_BIG, ALU.add, ALU.mult))
                    v3 = sbm[:m, :].rearrange("p (g e) -> p g e", g=NGRP)
                    ch(dve.tensor_tensor(v3, v3, rank[:m, 1, :].unsqueeze(2).to_broadcast([m, NGRP, EPG]), ALU.mult))
                    ch(dve.tensor_tensor(v3, v3, rank[:m, 2, :].unsqueeze(2).to_broadcast([m, NGRP, EPG]), ALU.add))
                    ch(dve.max(top[:m, :], sbm[:m, :]))
                    ch(dve.max_index(picks[:m, t, :], top[:m, :], sbm[:m, :]))
                    ch(dve.match_replace(rep[:m, :], top[:m, :], sbm[:m, :], 4 * NEG_BIG))
                    ch(dve.tensor_scalar(chosen[:m, t, :], rep[:m, :], 2 * NEG_BIG, None, ALU.is_lt))
                    ch(dve.tensor_tensor(gates[:m, t, :], chosen[:m, t, :], sc, ALU.mult))
                    ch(dve.tensor_reduce(tot[:m, 0:1], gates[:m, t, :], AX.X, ALU.add))
                    ch(dve.reciprocal(tot[:m, 1:2], tot[:m, 0:1]))
                    ch(dve.tensor_scalar(gates[:m, t, :], gates[:m, t, :], tot[:m, 1:2], ROUTE_SCALE, ALU.mult, ALU.mult))
                    assert ch.n == STEPS * (t + 1), ch.n




def dispatch(nc, a, ps, ident, ones, before, xT, gates, chosen, picks, ys_d, dest, w8, tab, tok_d, plan_d,
             gates_d, only_d):
    FILL = SLOTS // P
    assert SLOTS % P == 0
    with ExitStack() as c:
        def sb(name, shape, dt=F32):
            return c.enter_context(nc.sbuf_tensor(name, shape, dt))
        wg, wu, wd = sb("swg", [P, KT, FE]), sb("swu", [P, KT, FE]), sb("swd", [P, 2, D])
        hT, sl, ys = sb("shT", [P, 2, T]), sb("ssl", [P, 2, 512]), sb("ys", [P, 2, D])
        only = sb("only", [P, NE])
        fill = sb("fill", [P, FILL], U32)
        tokens = sb("tokens", [P, NT], U32)
        num = sb("num", [P, 4, NE])
        numi = sb("numi", [P, NE], I32)
        rowi = sb("rowi", [P, 1], I32)
        rowf = sb("rowf", [P, 2])
        cnt = sb("cnt", [P, 4, NE])
        slot = sb("slot", [P, 2, NE])
        hot = sb("hot", [P, TOPK, NE])
        prod = sb("prod_", [P, TOPK, NE])
        pf = sb("pf", [P, TOPK])
        df = sb("df", [P, TOPK])
        one64 = sb("one64", [P, NE])
        plan = sb("plan", [P, 2], I32)
        planf = sb("planf", [P, 2])
        tb = sb("tb", [NE, CAP], U32)
        tbf = sb("tbf", [NE, CAP])
        POS, CNT, TB = 5, 6, 7
        PLAN = 29
        steps = [(f, ci) for f in range(2) for ci in range(3)]
        dsteps = [(t, b) for t in range(NT) for b in range(2)]
        with Phase(nc, "pooled filled w_in pos_done cnt_done dve_s slot_read dest_done sent plan_out tb_in tb_f tbT_done tab_s "
                       "gu_done s_done h_done d_done y_act y_dve yo0 yo1") as (block, (
                pooled, filled, w_in, pos_done, cnt_done, dve_s, slot_read, dest_done, sent, plan_out, tb_in, tb_f, tbT_done,
                tab_s, gu_done, s_done, h_done, d_done, y_act, y_dve, yo0, yo1)):
            y_out = (yo0, yo1)

            @block.gpsimd
            def _(pool):
                pool.memset(fill[:, :], NOBODY).then_inc(pooled, 1)
                pool.iota(tokens[:, :], pattern=[[P, NT]], base=0, channel_multiplier=1).then_inc(pooled, 1)
                pool.iota(numi[:, :], pattern=[[1, NE]], base=0, channel_multiplier=0).then_inc(pooled, 1)
                pool.iota(rowi[:, :], pattern=[[0, 1]], base=0, channel_multiplier=1).then_inc(pooled, 1)
                pool.wait_ge(pooled, 4)
                pool.wait_ge(filled, 16)
                for t in range(NT):
                    m = rows(t)
                    pool.wait_ge(dest_done, t + 1)
                    for k in range(TOPK):
                        pool.indirect_dma_start(out=tok_d[:, :], out_offset=bass.IndirectOffsetOnAxis(ap=dest[:m, t, k:k + 1], axis=0),
                                                in_=tokens[:m, t:t + 1], in_offset=None).then_inc(sent, 16)

            @block.sync
            def _(sp):
                sp.wait_ge(pooled, 4)
                sp.dma_start(tok_d.rearrange("(p n) o -> p (n o)", p=P), fill[:, :]).then_inc(filled, 16)
                for dst, n in ((wg, "w_sh_gate"), (wu, "w_sh_up"), (wd, "w_sh_down")):
                    sp.dma_start(dst[:, :, :], a[n][0].rearrange("(k p) n -> p k n", p=P)).then_inc(w_in, 16)
                sp.wait_ge(dve_s, PLAN)
                sp.dma_start(plan_d[0:OVB, :], plan[0:OVB, 0:1]).then_inc(plan_out, 16)
                sp.dma_start(plan_d[OVB:OVB + 1, :], plan[0:1, 1:2]).then_inc(plan_out, 16)
                sp.dma_start(only_d[:, :], only[0:OVB, :]).then_inc(plan_out, 16)
                sp.dma_start(gates_d[0:SEQ, :].rearrange("(t p) e -> p t e", p=P), gates[:, 0:NT - 1, :]).then_inc(plan_out, 16)
                sp.dma_start(gates_d[SEQ:T, :], gates[:DEC, NT - 1, :]).then_inc(plan_out, 16)
                for t in range(NT):
                    m = rows(t)
                    sp.wait_ge(y_act, t + 1)
                    sp.wait_ge(y_dve, t + 1)
                    sp.dma_start(ys_d[t * P:t * P + m, :], ys[:m, t % 2, :]).then_inc(y_out[t % 2], 16)
                sp.wait_ge(sent, 16 * NT * TOPK)
                sp.dma_start(tb[:, :], tok_d[0:NE * CAP, :].rearrange("(e s) o -> e (s o)", e=NE)).then_inc(tb_in, 16)
                sp.wait_ge(tb_in, 16)
                sp.wait_ge(plan_out, 80)
                sp.wait_ge(y_out[0], 16 * 5)
                sp.wait_ge(y_out[1], 16 * 4)

            @block.vector
            def _(dve):
                ch = Chain(dve, dve_s)
                NUM, BASE, STEP, FREE = (num[:, k, :] for k in range(4))
                dve.wait_ge(pooled, 4)
                ch(dve.tensor_copy(NUM, numi[:, :]))
                ch(dve.tensor_copy(rowf[:, 0:1], rowi[:, :]))
                ch(dve.tensor_scalar(BASE, NUM, float(CAP), None, ALU.mult))
                ch(dve.memset(one64[:, :], 1.0))
                dve.wait_ge(cnt_done, 1)
                ch(dve.tensor_scalar(cnt[:, 0, :], ps[:, CNT, 0:NE], float(CAP), None, ALU.subtract))
                for k in range(7):
                    ch(dve.tensor_scalar(cnt[:, 1, :], cnt[:, 0, :], float(P * k), None, ALU.is_gt))
                    if k == 0:
                        ch(dve.tensor_copy(cnt[:, 2, :], cnt[:, 1, :]))
                    else:
                        ch(dve.tensor_tensor(cnt[:, 2, :], cnt[:, 2, :], cnt[:, 1, :], ALU.add))
                ch(dve.tensor_tensor_scan(cnt[:, 3, :], one64[:, :], cnt[:, 2, :], 0.0, ALU.mult, ALU.add))
                ch(dve.tensor_tensor(cnt[:, 1, :], cnt[:, 3, :], cnt[:, 2, :], ALU.subtract))
                ch(dve.tensor_scalar(STEP, cnt[:, 1, :], float(P), float(NE * CAP - CAP), ALU.mult, ALU.add))
                ch(dve.tensor_tensor(STEP, STEP, BASE, ALU.subtract))
                ch(dve.tensor_scalar(cnt[:, 0, :], cnt[:, 3, :], rowf[:, 0:1], None, ALU.is_le))
                ch(dve.tensor_reduce(planf[:, 0:1], cnt[:, 0, :], AX.X, ALU.add))
                ch(dve.tensor_scalar(planf[:, 0:1], planf[:, 0:1], float(NE - 1), None, ALU.min))
                ch(dve.tensor_copy(planf[:, 1:2], cnt[:, 3, NE - 1:NE]))
                ch(dve.tensor_copy(plan[:, :], planf[:, :]))
                ch(dve.tensor_scalar(only[:, :], NUM, planf[:, 0:1], None, ALU.is_equal))
                assert ch.n == PLAN, ch.n
                for t in range(NT):
                    m = rows(t)
                    if t:
                        dve.wait_ge(slot_read, t)
                    dve.wait_ge(pos_done, t + 1)
                    pos = ps[:m, POS, 0:NE]
                    ch(dve.tensor_scalar(slot[:m, 0, :], pos, float(CAP), None, ALU.is_ge))
                    ch(dve.tensor_tensor(slot[:m, 0, :], slot[:m, 0, :], STEP[:m, :], ALU.mult))
                    dve.tensor_tensor(slot[:m, 0, :], slot[:m, 0, :], pos, ALU.add).then_inc(slot_read, 1)
                    dve.wait_ge(slot_read, t + 1)
                    ch(dve.tensor_tensor(slot[:m, 0, :], slot[:m, 0, :], BASE[:m, :], ALU.add))
                    ch(dve.tensor_copy(pf[:m, :], picks[:m, t, :]))
                    B = [m, TOPK, NE]
                    ch(dve.tensor_tensor(hot[:m, :, :], NUM[:m, :].unsqueeze(1).to_broadcast(B),
                                         pf[:m, :].unsqueeze(2).to_broadcast(B), ALU.is_equal))
                    ch(dve.tensor_tensor(prod[:m, :, :], hot[:m, :, :], slot[:m, 0, :].unsqueeze(1).to_broadcast(B), ALU.mult))
                    ch(dve.tensor_reduce(df[:m, :], prod[:m, :, :], AX.X, ALU.add))
                    dve.tensor_copy(dest[:m, t, :], df[:m, :]).then_inc(dest_done, 1)
                    ch(dve.tensor_tensor(prod[:m, :, :], hot[:m, :, :], gates[:m, t, :].unsqueeze(1).to_broadcast(B), ALU.mult))
                    ch(dve.tensor_reduce(w8[:m, t, :], prod[:m, :, :], AX.X, ALU.add))
                    ch(dve.tensor_scalar(pf[:m, :], df[:m, :], float(NE * CAP), None, ALU.is_lt))
                    ch(dve.tensor_tensor(w8[:m, t, :], w8[:m, t, :], pf[:m, :], ALU.mult))
                for n, (f, ci) in enumerate(steps):
                    c0, cw = CHUNKS[ci]
                    dve.wait_ge(s_done, n + 1)
                    dve.tensor_tensor(hT[:, f, c0:c0 + cw], sl[:, n % 2, 0:cw], ps[:, 1, 0:cw], ALU.mult).then_inc(h_done, 1)
                for n, (t, b) in enumerate(dsteps):
                    if n % 2 == 0:
                        continue
                    m = rows(t)
                    dve.wait_ge(d_done, n + 1)
                    if t >= 2:
                        dve.wait_ge(y_out[t % 2], 16 * (t // 2))
                    dve.tensor_copy(ys[:m, t % 2, b * 512:(b + 1) * 512], ps[:m, 2 + n % 3, :]).then_inc(y_dve, 1)
                dve.wait_ge(tb_in, 16)
                dve.tensor_copy(tbf[:, :], tb[:, :]).then_inc(tb_f, 1)
                dve.wait_ge(tbT_done, 1)
                dve.tensor_copy(tab[:, :, 0], ps[:, TB, 0:NE]).then_inc(tab_s, 1)
                dve.tensor_copy(tab[:CAP - P, :, 1], ps[:CAP - P, TB, NE:2 * NE]).then_inc(tab_s, 1)

            @block.scalar
            def _(act):
                for n, (f, ci) in enumerate(steps):
                    c0, cw = CHUNKS[ci]
                    act.wait_ge(gu_done, n + 1)
                    if n >= 2:
                        act.wait_ge(h_done, n - 1)
                    act.activation(sl[:, n % 2, 0:cw], ps[:, 0, 0:cw], ACT.Silu).then_inc(s_done, 1)
                for n, (t, b) in enumerate(dsteps):
                    if n % 2:
                        continue
                    m = rows(t)
                    act.wait_ge(d_done, n + 1)
                    if t >= 2:
                        act.wait_ge(y_out[t % 2], 16 * (t // 2))
                    act.activation(ys[:m, t % 2, b * 512:(b + 1) * 512], ps[:m, 2 + n % 3, :], ACT.Copy).then_inc(y_act, 1)

            @block.tensor
            def _(pe):
                for t in range(NT):
                    m = rows(t)
                    mm = pe.matmul(ps[:, CNT, 0:NE], ones[:m, :], chosen[:m, t, :], start=t == 0, stop=t == NT - 1)
                mm.then_inc(cnt_done, 1)
                for t in range(NT):
                    m = rows(t)
                    if t:
                        pe.wait_ge(slot_read, t)
                    mm = pe.matmul(ps[:m, POS, 0:NE], before[:m, :m], chosen[:m, t, :], start=True, stop=t == 0)
                    for u in range(t):
                        mm = pe.matmul(ps[:m, POS, 0:NE], ones[:, :m], chosen[:, u, :], start=False, stop=u == t - 1)
                    mm.then_inc(pos_done, 1)
                pe.wait_ge(w_in, 48)
                for n, (f, ci) in enumerate(steps):
                    c0, cw = CHUNKS[ci]
                    if n:
                        pe.wait_ge(h_done, n)
                    for wt, bank in ((wg, 0), (wu, 1)):
                        for k in range(KT):
                            mm = pe.matmul(ps[:, bank, 0:cw], wt[:, k, f * P:(f + 1) * P], xT[:, k, c0:c0 + cw],
                                           start=k == 0, stop=k == KT - 1)
                    mm.then_inc(gu_done, 1)
                pe.wait_ge(h_done, len(steps))
                for n, (t, b) in enumerate(dsteps):
                    m = rows(t)
                    if n >= 3:
                        e = n - 3
                        pe.wait_ge(*((y_dve, e // 2 + 1) if e % 2 else (y_act, e // 2 + 1)))
                    for f in range(2):
                        mm = pe.matmul(ps[:m, 2 + n % 3, :], hT[:, f, t * P:t * P + m], wd[:, f, b * 512:(b + 1) * 512],
                                       start=f == 0, stop=f == 1)
                    mm.then_inc(d_done, 1)
                pe.wait_ge(tb_f, 1)
                pe.transpose(ps[:, TB, 0:NE], tbf[:, 0:P], ident[:NE, :NE])
                pe.transpose(ps[:CAP - P, TB, NE:2 * NE], tbf[:, P:CAP], ident[:NE, :NE]).then_inc(tbT_done, 1)


def split_high(act, hi, x):
    return act.activation(hi, x, ACT.Copy)


def split_low(dve, lo, x, hi):
    return dve.tensor_tensor(lo, x, hi.bitcast(F32), ALU.subtract)


def split_product(pe, out, lh, ll, rh, rl, start, stop):
    pe.matmul(out, ll, rh, start=start, stop=False)
    pe.matmul(out, lh, rl, start=False, stop=False)
    return pe.matmul(out, lh, rh, start=False, stop=stop)


def experts(nc, a, ps, ident, tab, h2_d, ye_d, bufs):
    wg, wu, wd, xg, sl, yo = bufs
    C2 = CAP - P
    GB, UB, TB, DB = 0, 1, 2, (5, 6, 7, 5)
    with ExitStack() as c:
        def sb(name, shape, dt=F32):
            return c.enter_context(nc.sbuf_tensor(name, shape, dt))
        idx = sb("idx", [P, 2, 2], U32)
        wgh, wgl, wuh, wul = (sb(n, [P, KT, FE], F32R) for n in ("wgh", "wgl", "wuh", "wul"))
        wdh, wdl = (sb(n, [P, 2, D], F32R) for n in ("wdh", "wdl"))
        xh, xl = (sb(n, [P, KT, CAP], F32R) for n in ("xgh", "xgl"))
        hT = sb("hT", [P, 2 * CAP])
        hh, hl = (sb(n, [P, 2, 2, CAP], F32R) for n in ("hTh", "hTl"))
        with Phase(nc, "cleared g_in0 g_in1 u_in0 u_in1 d_in0 d_in1 idx_ready x_in0 x_in1 t_done x_high x_low gh gl uh ul dh dl "
                       "g_done u_done s_done h_s h_high h_done d_done y_ready st0 st1") as (block, (
                cleared, gi0, gi1, ui0, ui1, di0, di1, idx_ready, xi0, xi1, t_done, x_high, x_low, gh, gl, uh, ul, dh, dl,
                g_done, u_done, s_done, h_s, h_high, h_done, d_done, y_ready, st0, st1)):
            g_in, u_in, d_in, x_in, stored = (gi0, gi1), (ui0, ui1), (di0, di1), (xi0, xi1), (st0, st1)
            high, low = (gh, uh, dh), (gl, ul, dl)
            GATE, UP, DOWN = range(3)

            def source(n, e):
                return a[n][0, bass.ds(e, 1), :, :].rearrange("o (k p) n -> p (o k) n", p=P)

            def every_expert(eng, body):
                def one(e):
                    body(e, e % 2, lambda d: (e + d) // 2)
                for e in range(3):
                    one(e)
                with eng.Fori(2, NE // 2 - 1) as j:
                    for r in range(2):
                        body(2 * j + r - 1, 1 - r, lambda d: j + (r - 1 + d) // 2)
                for e in range(NE - 3, NE):
                    one(e)

            def at_least(e, n):
                return not isinstance(e, int) or e >= n

            def at_most(e, n):
                return not isinstance(e, int) or e <= n

            def high_part(act, which, e, b, uses):
                arrived, raw, hi = ((g_in, wg, wgh), (u_in, wu, wuh), (d_in, wd, wdh))[which]
                act.wait_ge(arrived[b], 16 * (uses + 1))
                if at_least(e, 1):
                    if which == DOWN:
                        act.wait_ge(d_done, 4 * e)
                    else:
                        act.wait_ge((g_done, u_done)[which], e)
                split_high(act, hi[:, :, :], raw[:, b, :, :]).then_inc(high[which], 1)

            def low_part(dve, which, e, b):
                raw, hi, lo = ((wg, wgh, wgl), (wu, wuh, wul), (wd, wdh, wdl))[which]
                dve.wait_ge(high[which], e + 1)
                split_low(dve, lo[:, :, :], raw[:, b, :, :], hi[:, :, :]).then_inc(low[which], 1)

            def transposed(part):
                return ((part[:, :, 0:P], ps[:, TB:TB + 2, :].rearrange("p b (k n) -> p (b k) n", n=P)),
                        (part[:, :, P:CAP], ps[:, TB + 2, 0:KT * C2].rearrange("p (k n) -> p k n", n=C2)))

            @block.sync
            def _(sp):
                def load(which, e, b):
                    arrived, raw, n = ((g_in, wg, "w_exp_gate"), (u_in, wu, "w_exp_up"), (d_in, wd, "w_exp_down"))[which]
                    sp.dma_start(raw[:, b, :, :], source(n, e)).then_inc(arrived[b], 16)

                def store(e, b):
                    sp.wait_ge(y_ready, 4 * e + 4)
                    sp.dma_start(ye_d[bass.ds(e * CAP, P), :], yo[:, b, 0, :]).then_inc(stored[b], 16)
                    sp.dma_start(ye_d[bass.ds(e * CAP + P, C2), :], yo[:C2, b, 1, :]).then_inc(stored[b], 16)

                for b in range(2):
                    for which in range(3):
                        load(which, b, b)

                def body(e, b, half):
                    if at_most(e, NE - 3):
                        for which in (GATE, UP):
                            sp.wait_ge(low[which], e + 1)
                            load(which, e + 2, b)
                    if at_least(e, 2):
                        store(e - 2, b)
                    if at_least(e, 1) and at_most(e, NE - 2):
                        sp.wait_ge(low[DOWN], e)
                        load(DOWN, e + 1, 1 - b)
                every_expert(sp, body)
                for e in (NE - 2, NE - 1):
                    store(e, e % 2)
                for b in range(2):
                    sp.wait_ge(stored[b], 16 * NE)

            @block.gpsimd
            def _(pool):
                pool.memset(xg[:, 0, :, :], 0.0).then_inc(cleared, 1)
                pool.memset(xg[:, 1, :, :], 0.0).then_inc(cleared, 1)
                pool.wait_ge(cleared, 2)
                last_row = pool.to_reg(T - 1)

                def body(e, b, half):
                    if at_least(e, 2):
                        pool.wait_ge(x_in[b], 32 * half(0))
                        pool.wait_ge(t_done, e - 1)
                    pool.tensor_copy(idx[:, b, 0:1], tab[:, bass.ds(e, 1), 0]).then_inc(idx_ready, 1)
                    pool.tensor_copy(idx[:C2, b, 1:2], tab[:C2, bass.ds(e, 1), 1]).then_inc(idx_ready, 1)
                    pool.wait_ge(idx_ready, 2)
                    pool.sem_clear(idx_ready)
                    for j, m in ((0, P), (1, C2)):
                        pool.indirect_dma_start(out=xg[:m, b, j, :], out_offset=None, in_=h2_d[:, :],
                                                in_offset=bass.IndirectOffsetOnAxis(ap=idx[:m, b, j:j + 1], axis=0),
                                                bounds_check=last_row, oob_is_err=False).then_inc(x_in[b], 16)
                every_expert(pool, body)

            @block.tensor
            def _(pe):
                def turn(e, b, uses):
                    pe.wait_ge(x_in[b], 32 * (uses + 1))
                    if at_least(e, 1):
                        pe.wait_ge(x_low, 2 * e)
                    for k in range(KT):
                        pe.transpose(ps[:, TB + k // 4, k % 4 * P:(k % 4 + 1) * P], xg[:, b, 0, k * P:(k + 1) * P], ident[:, :])
                    for k in range(KT):
                        mm = pe.transpose(ps[:, TB + 2, k * C2:(k + 1) * C2], xg[:C2, b, 1, k * P:(k + 1) * P], ident[:C2, :C2])
                    mm.then_inc(t_done, 1)

                def down(e, b):
                    pe.wait_ge(low[DOWN], e + 1)
                    pe.wait_ge(h_done, e + 1)
                    for n in range(4):
                        j, q = divmod(n, 2)
                        m = (P, C2)[j]
                        if n == 3:
                            pe.wait_ge(y_ready, 4 * e + 1)
                        elif at_least(e, 1):
                            pe.wait_ge(y_ready, 4 * e + (0, -2, -1)[n])
                        for f in range(2):
                            mm = split_product(pe, ps[:m, DB[n], :], hh[:, b, f, j * P:j * P + m], hl[:, b, f, j * P:j * P + m],
                                               wdh[:, f, q * 512:(q + 1) * 512], wdl[:, f, q * 512:(q + 1) * 512], f == 0, f == 1)
                        mm.then_inc(d_done, 1)

                turn(0, 0, 0)

                def body(e, b, half):
                    pe.wait_ge(x_low, 2 * e + 2)
                    if at_least(e, 1):
                        pe.wait_ge(h_s, e)
                    for which, wh, wl, bank, done in ((GATE, wgh, wgl, GB, g_done), (UP, wuh, wul, UB, u_done)):
                        pe.wait_ge(low[which], e + 1)
                        for f in range(2):
                            for k in range(KT):
                                mm = split_product(pe, ps[:, bank, f * CAP:(f + 1) * CAP], wh[:, k, f * P:(f + 1) * P],
                                                   wl[:, k, f * P:(f + 1) * P], xh[:, k, :], xl[:, k, :], k == 0, k == KT - 1)
                        mm.then_inc(done, 1)
                    if at_most(e, NE - 2):
                        turn(e + 1, 1 - b, half(1))
                    if at_least(e, 1):
                        down(e - 1, 1 - b)
                every_expert(pe, body)
                down(NE - 1, 1)

            @block.scalar
            def _(act):
                def x_high_part(e):
                    act.wait_ge(t_done, e + 1)
                    for dst, src in transposed(xh):
                        split_high(act, dst, src).then_inc(x_high, 1)

                def copy_rows(e, b, uses):
                    for n in range(4):
                        j, q = divmod(n, 2)
                        m = (P, C2)[j]
                        act.wait_ge(d_done, 4 * e + n + 1)
                        if n == 0 and at_least(e, 2):
                            act.wait_ge(stored[b], 32 * uses)
                        act.activation(yo[:m, b, j, q * 512:(q + 1) * 512], ps[:m, DB[n], :], ACT.Copy).then_inc(y_ready, 1)

                high_part(act, GATE, 0, 0, 0)
                x_high_part(0)
                high_part(act, UP, 0, 0, 0)

                def body(e, b, half):
                    if at_least(e, 1):
                        high_part(act, DOWN, e - 1, 1 - b, half(-1))
                    if at_most(e, NE - 2):
                        high_part(act, GATE, e + 1, 1 - b, half(1))
                    act.wait_ge(u_done, e + 1)
                    if at_least(e, 1):
                        act.wait_ge(h_s, e)
                    act.activation(sl[:, :], ps[:, GB, 0:2 * CAP], ACT.Silu).then_inc(s_done, 1)
                    if at_most(e, NE - 2):
                        x_high_part(e + 1)
                        high_part(act, UP, e + 1, 1 - b, half(1))
                    if at_least(e, 1):
                        copy_rows(e - 1, 1 - b, half(-1))
                every_expert(act, body)
                high_part(act, DOWN, NE - 1, 1, NE // 2 - 1)
                copy_rows(NE - 1, 1, NE // 2 - 1)

            @block.vector
            def _(dve):
                def x_low_part(e):
                    for n, ((dst, src), (hi, _)) in enumerate(zip(transposed(xl), transposed(xh))):
                        dve.wait_ge(x_high, 2 * e + n + 1)
                        split_low(dve, dst, src, hi).then_inc(x_low, 1)

                low_part(dve, GATE, 0, 0)
                x_low_part(0)
                low_part(dve, UP, 0, 0)

                def body(e, b, half):
                    if at_least(e, 1):
                        low_part(dve, DOWN, e - 1, 1 - b)
                    if at_most(e, NE - 2):
                        low_part(dve, GATE, e + 1, 1 - b)
                    dve.wait_ge(s_done, e + 1)
                    dve.tensor_tensor(hT[:, :], sl[:, :], ps[:, UB, 0:2 * CAP], ALU.mult).then_inc(h_s, 1)
                    dve.wait_ge(h_s, e + 1)
                    if at_least(e, 2):
                        dve.wait_ge(d_done, 4 * e - 4)
                    flat = [t[:, b, :, :].rearrange("p f n -> p (f n)") for t in (hh, hl)]
                    dve.tensor_copy(flat[0], hT[:, :]).then_inc(h_high, 1)
                    dve.wait_ge(h_high, e + 1)
                    split_low(dve, flat[1], hT[:, :], flat[0]).then_inc(h_done, 1)
                    if at_most(e, NE - 2):
                        x_low_part(e + 1)
                        low_part(dve, UP, e + 1, 1 - b)
                every_expert(dve, body)
                low_part(dve, DOWN, NE - 1, 1)


def overflow(nc, a, ps, ident, h2_d, ys_d, tok_d, plan_d, gates_d, only_d, bufs):
    wg, wu, wd, xg, sl, yo = bufs
    with ExitStack() as c:
        idx = c.enter_context(nc.sbuf_tensor("oidx", [P, 1], U32))
        gr, on, pr = (c.enter_context(nc.sbuf_tensor(n, [P, NE], F32)) for n in ("ogr", "oon", "opr"))
        wt_ = c.enter_context(nc.sbuf_tensor("ow", [P, 1], F32))
        xgT = c.enter_context(nc.sbuf_tensor("oxT", [P, 1, KT, P], F32))
        hT = c.enter_context(nc.sbuf_tensor("ohT", [P, 2, P], F32))
        total = nc.values_load(plan_d[OVB:OVB + 1, 0:1], min_val=0, max_val=OVB)
        c.enter_context(nc.If(total > 0))
        with nc.Fori(0, OVB) as i:
            with nc.If(i < total):
                with Phase(nc, "oin ocl ox ot ocp ogu os oh od osc oy oout", ("ox", "oout")) as (block, (
                        oin, cleared, ox, ot, ocp, ogu, os_, oh, od, osc, oy, oout)):
                    first = NE * CAP + i * P

                    @block.sync
                    def _(sp):
                        sp.dma_start(idx[:, :], tok_d[bass.ds(first, P), :]).then_inc(oin, 16)
                        e = sp.value_load(plan_d[bass.ds(i, 1), 0:1], min_val=0, max_val=NE - 1)
                        for dst, n in ((wg, "w_exp_gate"), (wu, "w_exp_up"), (wd, "w_exp_down")):
                            sp.dma_start(dst[:, 0, :, :], a[n][0, bass.ds(e, 1), :, :].rearrange("o (k p) n -> p (o k) n", p=P)) \
                                .then_inc(oin, 16)
                        sp.dma_start(on[:, :], only_d[bass.ds(i, 1), :].rearrange("o e -> (o e)").partition_broadcast(P)).then_inc(oin, 16)

                    @block.gpsimd
                    def _(pool):
                        pool.memset(gr[:, :], 0.0).then_inc(cleared, 1)
                        pool.memset(yo[:, 0, 0, :], 0.0).then_inc(cleared, 1)
                        pool.wait_ge(cleared, 2)
                        pool.wait_ge(oin, 80)
                        at = bass.IndirectOffsetOnAxis(ap=idx[:, :], axis=0)
                        pool.indirect_dma_start(out=gr[:, :], out_offset=None, in_=gates_d[:, :], in_offset=at,
                                                bounds_check=T - 1, oob_is_err=False).then_inc(ox, 16)
                        pool.indirect_dma_start(out=yo[:, 0, 0, :], out_offset=None, in_=ys_d[:, :], in_offset=at,
                                                bounds_check=T - 1, oob_is_err=False).then_inc(ox, 16)
                        pool.indirect_dma_start(out=xg[:, 0, 0, :], out_offset=None, in_=h2_d[:, :],
                                                in_offset=at, bounds_check=T - 1, oob_is_err=False).then_inc(ox, 16)
                        pool.wait_ge(oy, 2)
                        pool.indirect_dma_start(out=ys_d[:, :], out_offset=at, in_=yo[:, 0, 0, :], in_offset=None,
                                                bounds_check=T - 1, oob_is_err=False).then_inc(oout, 16)
                        pool.wait_ge(oout, 16)

                    @block.tensor
                    def _(pe):
                        pe.wait_ge(ox, 48)
                        for k in range(KT):
                            mm = pe.transpose(ps[:, k // 4, k % 4 * P:(k % 4 + 1) * P], xg[:, 0, 0, k * P:(k + 1) * P], ident[:, :])
                        mm.then_inc(ot, 1)
                        pe.wait_ge(ocp, 1)
                        for wt, bank in ((wg, 2), (wu, 3)):
                            for f in range(2):
                                for k in range(KT):
                                    mm = pe.matmul(ps[:, bank, f * P:(f + 1) * P], wt[:, 0, k, f * P:(f + 1) * P], xgT[:, 0, k, 0:P],
                                                   start=k == 0, stop=k == KT - 1)
                        mm.then_inc(ogu, 1)
                        pe.wait_ge(oh, 1)
                        for q in range(2):
                            for f in range(2):
                                mm = pe.matmul(ps[:, 4 + q, :], hT[:, f, 0:P], wd[:, 0, f, q * 512:(q + 1) * 512], start=f == 0, stop=f == 1)
                            mm.then_inc(od, 1)

                    @block.scalar
                    def _(act):
                        act.wait_ge(ot, 1)
                        act.activation(xgT[:, 0, :, 0:P], ps[:, 0:2, :].rearrange("p b (k n) -> p (b k) n", n=P), ACT.Copy).then_inc(ocp, 1)
                        act.wait_ge(ogu, 1)
                        act.activation(sl[:, 0:2 * P], ps[:, 2, 0:2 * P], ACT.Silu).then_inc(os_, 1)

                    @block.vector
                    def _(dve):
                        dve.wait_ge(os_, 1)
                        dve.tensor_tensor(hT[:, :, 0:P], sl[:, 0:2 * P].rearrange("p (f n) -> p f n", f=2),
                                          ps[:, 3, 0:2 * P].rearrange("p (f n) -> p f n", f=2), ALU.mult).then_inc(oh, 1)
                        dve.wait_ge(oin, 80)
                        dve.wait_ge(ox, 48)
                        dve.tensor_tensor(pr[:, :], gr[:, :], on[:, :], ALU.mult).then_inc(osc, 1)
                        dve.wait_ge(osc, 1)
                        dve.tensor_reduce(wt_[:, :], pr[:, :], AX.X, ALU.add).then_inc(osc, 1)
                        dve.wait_ge(osc, 2)
                        for q in range(2):
                            dve.wait_ge(od, q + 1)
                            yq = yo[:, 0, 0, q * 512:(q + 1) * 512]
                            dve.scalar_tensor_tensor(out=yq, in0=ps[:, 4 + q, :], scalar=wt_[:, 0:1], in1=yq, op0=ALU.mult,
                                                     op1=ALU.add).then_inc(oy, 1)


def combine(nc, a, o, gcol, bcol, st, ys_d, dest, w8, ye_d, h2_d):
    RING = 8
    with ExitStack() as c:
        row = c.enter_context(nc.sbuf_tensor("row", [P, RING, D], F32))
        xr = c.enter_context(nc.sbuf_tensor("xr2", [P, 2, D], F32))
        ys = c.enter_context(nc.sbuf_tensor("ysr", [P, 3, D], F32))
        ring = [f"in{r}" for r in range(RING)]
        with Phase(nc, " ".join(ring) + " cleared used par_in x_in0 x_in1 dve_s var_ready root_ready y_ready yo0 yo1 yo2") as (block, sems):
            row_in = sems[:RING]
            cleared, used, par_in, x_in0, x_in1, dve_s, var_ready, root_ready, y_ready, *y_out = sems[RING:]
            x_in = (x_in0, x_in1)

            @block.sync
            def _(sp):
                sp.dma_start(gcol[:, :], a["ln2_g"][0].partition_broadcast(P)).then_inc(par_in, 16)
                sp.dma_start(bcol[:, :], a["ln2_b"][0].partition_broadcast(P)).then_inc(par_in, 16)
                for t in range(NT):
                    m = rows(t)
                    if t >= 2:
                        sp.wait_ge(y_ready, t - 1)
                    sp.dma_start(xr[:m, t % 2, :], h2_d[t * P:t * P + m, :]).then_inc(x_in[t % 2], 16)
                    if t >= 3:
                        sp.wait_ge(y_out[t % 3], 16 * (t // 3))
                    sp.dma_start(ys[:m, t % 3, :], ys_d[t * P:t * P + m, :]).then_inc(x_in[t % 2], 16)
                sp.wait_ge(par_in, 32)

            @block.gpsimd
            def _(pool):
                for r in range(RING):
                    pool.memset(row[:, r, :], 0.0).then_inc(cleared, 1)
                pool.wait_ge(cleared, RING)
                for n in range(NT * TOPK):
                    t, k = divmod(n, TOPK)
                    m = rows(t)
                    if n >= RING:
                        pool.wait_ge(used, n - RING + 1)
                    pool.indirect_dma_start(out=row[:m, n % RING, :], out_offset=None, in_=ye_d[:, :],
                                            in_offset=bass.IndirectOffsetOnAxis(ap=dest[:m, t, k:k + 1], axis=0),
                                            bounds_check=NE * CAP - 1, oob_is_err=False) \
                        .then_inc(row_in[n % RING], 16)

            @block.scalar
            def _(act):
                for t in range(NT):
                    m = rows(t)
                    act.wait_ge(var_ready, t + 1)
                    act.activation(st[:m, t % 2, 15:16], st[:m, t % 2, 14:15], ACT.Sqrt).then_inc(root_ready, 1)
                    act.wait_ge(y_ready, t + 1)
                    dst = o[0][0, t * P:t * P + m, :] if t < NT - 1 else o[1][0, :, :]
                    act.dma_start(dst, ys[:m, t % 3, :]).then_inc(y_out[t % 3], 16)
                for r in range(3):
                    act.wait_ge(y_out[r], 16 * 3)

            @block.vector
            def _(dve):
                ch = Chain(dve, dve_s)
                dve.wait_ge(par_in, 32)
                for t in range(NT):
                    m = rows(t)
                    y = ys[:m, t % 3, :]
                    dve.wait_ge(x_in[t % 2], 32 * (t // 2 + 1))
                    ch(dve.scalar_tensor_tensor(out=y, in0=xr[:m, t % 2, :], scalar=ALPHA, in1=y, op0=ALU.mult, op1=ALU.add))
                    for k in range(TOPK):
                        n = t * TOPK + k
                        dve.wait_ge(row_in[n % RING], 16 * (n // RING + 1))
                        dve.scalar_tensor_tensor(out=y, in0=row[:m, n % RING, :], scalar=w8[:m, t, k:k + 1], in1=y, op0=ALU.mult,
                                                 op1=ALU.add).then_inc(used, 1)
                        dve.wait_ge(used, n + 1)
                    layer_norm_rows(dve, ch, m, ys[:, t % 3, :], ys[:, t % 3, :], st[:, t % 2, :], gcol, var_ready, root_ready, t)
                    dve.tensor_tensor(y, y, bcol[:m, :], ALU.add).then_inc(y_ready, 1)


def mixture(nc, a, o, ps, ident, ones, gcol, bcol, st, xT, before, h2_d, tok_d, plan_d, gates_d, only_d, ys_d, ye_d):
    with ExitStack() as c:
        def sb(name, shape, dt=F32):
            return c.enter_context(nc.sbuf_tensor(name, shape, dt))
        dest = sb("dest", [P, NT, TOPK], U32)
        w8 = sb("w8", [P, NT, TOPK])
        with ExitStack() as c2:
            def sb2(name, shape, dt=F32):
                return c2.enter_context(nc.sbuf_tensor(name, shape, dt))
            tab = sb2("tab", [P, NE, 2], U32)
            with ExitStack() as c3:
                gates, chosen = (c3.enter_context(nc.sbuf_tensor(n, [P, NT, NE], F32)) for n in ("gates", "chosen"))
                picks = c3.enter_context(nc.sbuf_tensor("picks", [P, NT, TOPK], U32))
                router(nc, a, ps, xT, gates, chosen, picks)
                dispatch(nc, a, ps, ident, ones, before, xT, gates, chosen, picks, ys_d, dest, w8, tab, tok_d, plan_d,
             gates_d, only_d)
            bufs = (sb2("wg", [P, 2, KT, FE]), sb2("wu", [P, 2, KT, FE]), sb2("wd", [P, 2, 2, D]), sb2("xg", [P, 2, 2, D]),
                    sb2("sl", [P, 2 * CAP]), sb2("yo", [P, 2, 2, D]))
            experts(nc, a, ps, ident, tab, h2_d, ye_d, bufs)
            overflow(nc, a, ps, ident, h2_d, ys_d, tok_d, plan_d, gates_d, only_d, bufs)
        combine(nc, a, o, gcol, bcol, st, ys_d, dest, w8, ye_d, h2_d)


_INS = ["x_prompt", "x_sample", "cache_sb_k", "cache_sb_v", "state_hgrn", "ln_in_g", "ln_in_b", "w_in", "w_out", "hg_norm",
        "hg_lb_logits", "ln1_g", "ln1_b", "w_router", "router_bias", "w_exp_gate", "w_exp_up", "w_exp_down", "w_sh_gate",
        "w_sh_up", "w_sh_down", "ln2_g", "ln2_b"]
_OUTS = [(1, SEQ, D), (1, DEC, D), (1, 1, SEQ, HEADS, P), (1, 1, SEQ, HEADS, P), (1, 1, HEADS, P, P),
         (1, 1, DEC, HEADS, P), (1, 1, DEC, HEADS, P), (1, 1, HEADS, P, P)]


def kernel(**inputs):
    import concourse.bacc as bacc
    from concourse.bass_utils import run_bass_kernel_spmd

    nc = bacc.Bacc("TRN2", target_bir_lowering=False, num_devices=1)
    arrays, args = {}, {}
    for name in _INS:
        x = np.ascontiguousarray(inputs[name])
        arrays[f"in_{name}"] = x
        args[name] = nc.dram_tensor(f"in_{name}", x.shape, mybir.dt.from_np(x.dtype), kind="ExternalInput").ap()
    outs = [nc.dram_tensor(f"out_{i}", s, F32, kind="ExternalOutput").ap() for i, s in enumerate(_OUTS)]
    build(nc, args, outs)
    r = run_bass_kernel_spmd(nc, [arrays], core_ids=[0])
    return tuple(r.results[0][f"out_{i}"] for i in range(len(_OUTS)))
```

```python
from contextlib import ExitStack

import concourse.bass as bass
import numpy as np
from concourse import mybir

F32 = mybir.dt.float32
I32 = mybir.dt.int32
U32 = mybir.dt.uint32
F32R = mybir.dt.float32r
ACT = mybir.ActivationFunctionType
ALU = mybir.AluOpType
AX = mybir.AxisListType

P = 128
D = 1024
KT = D // P
SEQ, DEC, PAST = 1024, 64, 128
T = SEQ + DEC
NT = (T + P - 1) // P
HEADS = 8
HH = 4
HALVES = HEADS // HH
W512 = HH * P
NE, NGRP, TOPG, TOPK = 64, 8, 4, 8
EPG = NE // NGRP
FE = 256
ROUTE_SCALE = 2.5
NEG_BIG = -1e9
ALPHA = 2.0 ** 0.25
LN_EPS, RMS_EPS = 1e-5, 1e-6
LB_FLOOR = 1e-30
SCALE = P ** -0.5
LN_SHIFT = 50
LN2 = float(np.log(2.0))
CAP = 192
NOBODY = 4 * T
OVB = max(min(n * -(-(T - CAP) // P), (T * TOPK - n * (CAP + 1)) // P + n) for n in range(1, NE + 1) if n * (CAP + 1) <= T * TOPK)
SLOTS = NE * CAP + OVB * P
LEVELS = [1, 2, 4, 8, 16, 32, 64]
NL = len(LEVELS)
CHUNKS = [(0, 368), (368, 368), (736, 352)]
GW = 256
(C_SQ, C_SK, C_SV, C_HQ, C_HF, C_HI, C_HG, C_GS, C_GH) = range(0, 9 * D, D)


def rows(t):
    return P if t < NT - 1 else T - P * (NT - 1)


def absolute(dve, out, x):
    return dve.scalar_tensor_tensor(out=out, in0=x, scalar=-1.0, in1=x, op0=ALU.mult, op1=ALU.max)


class Chain:

    def __init__(self, eng, sem):
        self.eng, self.sem, self.n = eng, sem, 0

    def __call__(self, ins):
        self.n += 1
        ins.then_inc(self.sem, 1)
        self.eng.wait_ge(self.sem, self.n)


class Phase:

    def __init__(self, nc, names, software_dma=()):
        self.nc, self.stack = nc, ExitStack()
        self.sems = [self.stack.enter_context(nc.semaphore(n)) for n in names.split()]
        self.queued = [self.sems[names.split().index(n)] for n in software_dma]

    def __enter__(self):
        self.block_ctx = self.nc.Block()
        return self.block_ctx.__enter__(), self.sems

    def __exit__(self, *a):
        self.block_ctx.__exit__(*a)
        self.nc.all_engine_barrier()
        for s in self.queued:
            self.nc.gpsimd.dma_reset(range(s.num, s.num + 1))
            self.nc.gpsimd.sem_clear(s)
        for s in self.sems:
            self.nc.sync.sem_clear(s)
        self.nc.all_engine_barrier()
        self.stack.close()


def split_high(act, hi, x):
    return act.activation(hi, x, ACT.Copy)


def split_low(dve, lo, x, hi):
    return dve.tensor_tensor(lo, x, hi.bitcast(F32), ALU.subtract)


def split_product(pe, out, lh, ll, rh, rl, start, stop):
    pe.matmul(out, ll, rh, start=start, stop=False)
    pe.matmul(out, lh, rl, start=False, stop=False)
    return pe.matmul(out, lh, rh, start=False, stop=stop)


def layer_norm_rows(eng, ch, m, x, out, st, gg, sqrt_req, sqrt_done, n):
    for c in range(2):
        ch(eng.bn_stats(st[:m, 6 * c:6 * c + 6], x[:m, 512 * c:512 * c + 512]))
    ch(eng.bn_aggr(st[:m, 12:14], st[:m, 0:12]))
    eng.tensor_scalar(st[:m, 14:15], st[:m, 13:14], LN_EPS, None, ALU.add).then_inc(sqrt_req, 1)
    eng.wait_ge(sqrt_done, n + 1)
    ch(eng.reciprocal(st[:m, 16:17], st[:m, 15:16]))
    ch(eng.tensor_scalar(out[:m, :], x[:m, :], st[:m, 12:13], st[:m, 16:17], ALU.subtract, ALU.mult))
    ch(eng.tensor_tensor(out[:m, :], out[:m, :], gg[:m, :], ALU.mult))


def build(nc, a, o):
    ctx = ExitStack()
    with ctx:
        def sb(name, shape, dt=F32):
            return ctx.enter_context(nc.sbuf_tensor(name, shape, dt))

        def dram(name, shape, dt=F32):
            return nc.dram_tensor(name, shape, dt, kind="Internal").ap()

        xn_d = dram("xn_d", [NT * P, D])
        h2_d = dram("h2_d", [T, D])
        osb_d = dram("osb_d", [HALVES, NT * P, W512])
        ohg_d = dram("ohg_d", [HALVES, NT * P, W512])
        mT_d = dram("mT_d", [P, HEADS, T])

        ps = ctx.enter_context(nc.psum_tensor("ps", [P, 8, 512], F32))
        ident = sb("ident", [P, P])
        ones = sb("ones", [P, P])
        st = sb("st", [P, 2, 20])
        before = sb("before", [P, P])
        tok_d = dram("tok_d", [SLOTS, 1], U32)
        plan_d = dram("plan_d", [OVB + 1, 1], I32)
        gates_d = dram("gates_d", [T, NE])
        only_d = dram("only_d", [OVB, NE])
        ys_d = dram("ys_d", [T, D])
        ye_d = dram("ye_d", [NE * CAP, D])

        constants(nc, ident, ones, before)
        with ExitStack() as mix_ctx:
            def msb(name, shape, dt=F32):
                return mix_ctx.enter_context(nc.sbuf_tensor(name, shape, dt))
            xT = [msb(name, [P, KT, T], F32R) for name in ("xTh", "xTl")]
            input_norm(nc, a, xn_d, ps, ident, xT, st)
            tri = msb("tri", [P, 3, P])
            masks = msb("masks", [P, NL + 1, P])
            lbc = msb("lbc", [P, 3, HEADS])
            mixer_constants(nc, a, tri, masks, lbc)
            with nc.Fori(0, HALVES) as half:
                with ExitStack() as c2:
                    qT, kT, bT = (c2.enter_context(nc.sbuf_tensor(n, [P, HH, T], F32)) for n in ("qT", "kT", "bT"))
                    v = c2.enter_context(nc.sbuf_tensor("v", [P, NT, W512], F32))
                    with Weights(nc, "w_mix") as w:
                        project_qkv(nc, a, o, half, w, xT, ps, ident, qT, kT, v, bT)
                        attention(nc, a, half, w, ps, ident, tri, qT, kT, v, bT, osb_d)
                        project_hgrn(nc, a, half, w, xT, ps, lbc, qT, kT, bT, v)
                    with nc.sbuf_tensor("levels", [P, NL + 2, T], F32) as levels:
                        hgrn(nc, a, o, half, ps, ident, masks, levels, qT, kT, bT, v, ohg_d)
                with Weights(nc, "w_gate") as w, nc.sbuf_tensor("g1", [P, NT, W512], F32) as g1:
                    merge(nc, a, half, w, xT, ps, ident, g1, osb_d, ohg_d, mT_d)
        gcol, bcol = sb("gcol", [P, D]), sb("bcol", [P, D])
        hT = sb("h2T", [P, KT, T])
        output_projection(nc, a, ps, ident, gcol, bcol, st, mT_d, hT, xn_d, h2_d)
        mixture(nc, a, o, ps, ident, ones, gcol, bcol, st, hT, before, h2_d, tok_d, plan_d, gates_d, only_d, ys_d, ye_d)


def constants(nc, ident, ones, before):
    with Phase(nc, "set_up") as (block, (set_up,)):
        @block.gpsimd
        def _(pool):
            pool.memset(ident[:, :], 0.0).then_inc(set_up, 1)
            pool.memset(ones[:, :], 1.0).then_inc(set_up, 1)
            pool.memset(before[:, :], 1.0).then_inc(set_up, 1)
            pool.wait_ge(set_up, 3)
            pool.affine_select(out=before[:, :], in_=before[:, :], compare_op=ALU.is_ge, fill=0.0, base=-1,
                               pattern=[[1, P]], channel_multiplier=-1).then_inc(set_up, 1)
            pool.affine_select(out=ident[:, :], in_=ident[:, :], compare_op=ALU.not_equal, fill=1.0, base=0,
                               pattern=[[-1, P]], channel_multiplier=1).then_inc(set_up, 1)
            pool.wait_ge(set_up, 5)


def mixer_constants(nc, a, tri, masks, lbc):
    with Phase(nc, "memo pooled loaded dve act") as (block, (memo, pooled, loaded, dve_s, act_s)):
        @block.vector
        def _(dve):
            ch = Chain(dve, dve_s)
            dve.memset(tri[:, :, :], 1.0).then_inc(memo, 1)
            dve.memset(masks[:, :, :], 1.0).then_inc(memo, 1)
            dve.wait_ge(loaded, 16)
            lg = lbc[:, 0, :]
            ch(dve.tensor_tensor(lbc[:, 1, :], lg, lg, ALU.subtract))
            dve.wait_ge(act_s, 1)
            ch(dve.reciprocal(lbc[:, 0, :], lbc[:, 2, :]))
            ch(dve.tensor_tensor(lbc[:, 0, :], lbc[:, 0, :], lbc[:, 2, :], ALU.mult))
            ch(dve.tensor_tensor(lbc[:, 0, :], lbc[:, 0, :], lbc[:, 0, :], ALU.subtract))
            ch(dve.tensor_scalar(lbc[:, 0, :], lbc[:, 0, :], LB_FLOOR, None, ALU.max))
            ch(dve.tensor_scalar(lbc[:, 1, :], lbc[:, 0, :], -1.0, 1.0, ALU.mult, ALU.add))
            dve.wait_ge(act_s, 2)
            ch(dve.tensor_scalar(lbc[:, 0, :], lbc[:, 2, :], -LN_SHIFT * LN2, None, ALU.add))
            ch(dve.tensor_scalar(lbc[:, 2, :], lbc[:, 0, :], -1.0, None, ALU.mult))

        @block.scalar
        def _(act):
            act.wait_ge(dve_s, 1)
            act.activation(lbc[:, 2, :], lbc[:, 1, :], ACT.Exp).then_inc(act_s, 1)
            act.wait_ge(dve_s, 5)
            act.activation(lbc[:, 2, :], lbc[:, 0, :], ACT.Ln, scale=2.0 ** LN_SHIFT).then_inc(act_s, 1)

        @block.sync
        def _(sp):
            with nc.allow_non_contiguous_dma(reason="1024 numbers, once"):
                sp.dma_start(lbc[:, 0, :], a["hg_lb_logits"].rearrange("a (h c) -> c (a h)", c=P)).then_inc(loaded, 16)
            sp.wait_ge(loaded, 16)

        @block.gpsimd
        def _(pool):
            pool.wait_ge(memo, 2)
            n = 0

            def keep(ap, base, pattern, cm):
                nonlocal n
                pool.affine_select(out=ap, in_=ap, compare_op=ALU.is_ge, fill=0.0, base=base, pattern=pattern,
                                   channel_multiplier=cm).then_inc(pooled, 1)
                n += 1
                pool.wait_ge(pooled, n)

            keep(tri[:, 0, :], -1, [[1, P]], -1)
            keep(tri[:, 1, :], 0, [[-1, P]], 1)
            keep(tri[:, 2, :], -1, [[1, P]], -1)
            for i, h in enumerate(LEVELS):
                v = masks[:, i + 1, :].rearrange("p (g u) -> p g u", u=2 * h)
                keep(v, 0, [[-2 * h, P // (2 * h)], [0, 2 * h]], 1)
                keep(v, h - 1, [[2 * h, P // (2 * h)], [0, 2 * h]], -1)
                keep(v, -h, [[0, P // (2 * h)], [1, 2 * h]], 0)
            keep(masks[:, 0, :], 0, [[1, P]], -1)
            keep(masks[:, 0, :], 0, [[-1, P]], 1)


def input_norm(nc, a, xn_d, ps, ident, xT, st):
    with ExitStack() as c:
        gcol, bcol = (c.enter_context(nc.sbuf_tensor(n, [P, D], F32)) for n in ("gcol0", "bcol0"))
        xin = c.enter_context(nc.sbuf_tensor("xin", [P, 2, D], F32))
        y = c.enter_context(nc.sbuf_tensor("y", [P, 2, D], F32))
        with Phase(nc, "par_in x_in0 x_in1 dve_s var_ready root_ready y_ready t_done t_high t_low stored0 stored1") as (block, (
                par_in, x_in0, x_in1, dve_s, var_ready, root_ready, y_ready, t_done, t_high, t_low, stored0, stored1)):
            x_in, stored = (x_in0, x_in1), (stored0, stored1)

            @block.sync
            def _(sp):
                sp.dma_start(gcol[:, :], a["ln_in_g"].partition_broadcast(P)).then_inc(par_in, 16)
                sp.dma_start(bcol[:, :], a["ln_in_b"].partition_broadcast(P)).then_inc(par_in, 16)
                for t in range(NT):
                    m = rows(t)
                    if t >= 2:
                        sp.wait_ge(y_ready, t - 1)
                    src = a["x_prompt"][0, t * P:t * P + m, :] if t < NT - 1 else a["x_sample"][0, :, :]
                    sp.dma_start(xin[:m, t % 2, :], src).then_inc(x_in[t % 2], 16)

            def transposed(part, t, b):
                m = rows(t)
                return (part[:, 4 * b:4 * b + 4, t * P:t * P + m],
                        ps[:, 2 * (t % 2) + b, :].rearrange("p (k n) -> p k n", k=4)[:, :, 0:m])

            @block.vector
            def _(dve):
                def low(t):
                    for b in range(2):
                        dve.wait_ge(t_high, 2 * t + b + 1)
                        dst, src = transposed(xT[1], t, b)
                        split_low(dve, dst, src, transposed(xT[0], t, b)[0]).then_inc(t_low, 1)

                ch = Chain(dve, dve_s)
                dve.wait_ge(par_in, 32)
                for t in range(NT):
                    m = rows(t)
                    dve.wait_ge(x_in[t % 2], 16 * (t // 2 + 1))
                    if t >= 2:
                        dve.wait_ge(stored[t % 2], 16 * (t // 2))
                        dve.wait_ge(t_done, t - 1)
                    layer_norm_rows(dve, ch, m, xin[:, t % 2, :], y[:, t % 2, :], st[:, t % 2, :], gcol, var_ready, root_ready, t)
                    dve.tensor_tensor(y[:m, t % 2, :], y[:m, t % 2, :], bcol[:m, :], ALU.add).then_inc(y_ready, 1)
                    if t:
                        low(t - 1)
                low(NT - 1)

            @block.scalar
            def _(act):
                for t in range(NT):
                    m = rows(t)
                    act.wait_ge(var_ready, t + 1)
                    act.activation(st[:m, t % 2, 15:16], st[:m, t % 2, 14:15], ACT.Sqrt).then_inc(root_ready, 1)
                    act.wait_ge(y_ready, t + 1)
                    act.dma_start(xn_d[t * P:t * P + m, :], y[:m, t % 2, :]).then_inc(stored[t % 2], 16)
                    act.wait_ge(t_done, t + 1)
                    for b in range(2):
                        split_high(act, *transposed(xT[0], t, b)).then_inc(t_high, 1)
                act.wait_ge(stored[0], 16 * 5)
                act.wait_ge(stored[1], 16 * 4)

            @block.tensor
            def _(pe):
                for t in range(NT):
                    m = rows(t)
                    pe.wait_ge(y_ready, t + 1)
                    if t >= 2:
                        pe.wait_ge(t_low, 2 * (t - 1))
                    for k in range(KT):
                        mm = pe.transpose(ps[:, 2 * (t % 2) + k // 4, (k % 4) * P:(k % 4) * P + m],
                                          y[:m, t % 2, k * P:(k + 1) * P], ident[:m, :m])
                    mm.then_inc(t_done, 1)


class Weights:

    def __init__(self, nc, name):
        self.nc, self.name = nc, name

    def __enter__(self):
        self.stack = ExitStack()
        self.raw = self.stack.enter_context(self.nc.sbuf_tensor(self.name + "_raw", [P, KT, GW], F32))
        self.high, self.low = (self.stack.enter_context(self.nc.sbuf_tensor(self.name + n, [P, 2, KT, GW], F32R))
                               for n in ("_high", "_low"))
        return self

    def __exit__(self, *a):
        self.stack.close()


HGRN_COLS = (C_HF, C_HQ, C_HI)
AHEAD = 2


def load_group(sp, a, w, half, cols, g):
    src = a["w_in"][0].rearrange("(k p) n -> p k n", p=P)[:, :, bass.ds(half * W512 + cols[g // 2] + g % 2 * GW, GW)]
    return sp.dma_start(w.raw[:, :, :], src)


def load_groups(sp, a, w, half, cols, arrived, split, lo, hi):
    for g in range(lo, hi):
        if g > lo:
            sp.wait_ge(split, g - lo)
        load_group(sp, a, w, half, cols, g).then_inc(arrived, 16)


def split_group(pool, w, g, arrived, rounded, split, lo, used=None):
    pool.wait_ge(arrived, 16 * (g - lo + 1))
    if used:
        pool.wait_ge(*used)
    pool.tensor_copy(w.high[:, g % 2, :, :], w.raw[:, :, :]).then_inc(rounded, 1)
    pool.wait_ge(rounded, g - lo + 1)
    split_low(pool, w.low[:, g % 2, :, :], w.raw[:, :, :], w.high[:, g % 2, :, :]).then_inc(split, 1)


def first_high(act, w, arrived, rounded):
    act.wait_ge(arrived, 16)
    split_high(act, w.high[:, 0, :, :], w.raw[:, :, :]).then_inc(rounded, 1)


def first_low(dve, w, rounded, split):
    dve.wait_ge(rounded, 1)
    split_low(dve, w.low[:, 0, :, :], w.raw[:, :, :], w.high[:, 0, :, :]).then_inc(split, 1)


class Steps:

    def __init__(self, forms):
        self.list = []
        self.last = []
        for g, f in enumerate(x for form in forms for x in (form, form)):
            if f == "T":
                heads = GW // P
                self.list += [(g, f, (g % 2 * heads + e, c)) for e in range(heads) for c in range(3)]
            else:
                self.list += [(g, f, t) for t in range(NT)]
            self.last.append(len(self.list))

    def split(self, pool, w, arrived, rounded, split, mm_done, start, lo):
        for g in range(start, len(self.last)):
            split_group(pool, w, g, arrived, rounded, split, lo, (mm_done, self.last[g - 2]) if g >= 2 else None)


def group_columns(g):
    return slice(g % 2 * GW, (g % 2 + 1) * GW)


def project_step(pe, w, xT, ps, bank, g, f, i):
    for k in range(KT):
        if f == "T":
            c0, cw = CHUNKS[i[1]]
            e = i[0] * P - g % 2 * GW
            out, cols, toks = ps[:, bank, 0:cw], slice(e, e + P), slice(c0, c0 + cw)
            left, right = [p[:, g % 2, k, cols] for p in (w.high, w.low)], [p[:, k, toks] for p in xT]
        else:
            m = rows(i)
            out, toks = ps[:m, bank, 0:GW], slice(i * P, i * P + m)
            left, right = [p[:, k, toks] for p in xT], [p[:, g % 2, k, :] for p in (w.high, w.low)]
        mm = split_product(pe, out, *left, *right, k == 0, k == KT - 1)
    return mm


def products(pe, steps, w, xT, ps, banks, split, mm_done, read_done, lo=0):
    seen = set()
    for n, (g, f, i) in enumerate(steps.list):
        if g not in seen and g >= lo:
            seen.add(g)
            pe.wait_ge(split, g - lo + 1)
        if n >= banks:
            e = n - banks
            pe.wait_ge(read_done[e % len(read_done)], e // len(read_done) + 1)
        project_step(pe, w, xT, ps, n % banks, g, f, i).then_inc(mm_done, 1)


def project_qkv(nc, a, o, half, w, xT, ps, ident, qT, kT, v, room):
    cols = (C_SQ, C_SK, C_SV)
    steps = Steps("TTR")
    BANKS = 6
    with ExitStack() as c:
        krow = room[:, :, :].rearrange("p h t -> p (h t)")[:, 0:2 * W512].rearrange("p (b n) -> p b n", b=2)
        with Phase(nc, "arrived rounded split mm_done act_read dve_read k_done k_copied v_out kout0 kout1") as (block, (
                arrived, rounded, split, mm_done, act_read, dve_read, k_done, k_copied, v_out, kout0, kout1)):
            read, kout = (act_read, dve_read), (kout0, kout1)

            @block.sync
            def _(sp):
                load_groups(sp, a, w, half, cols, arrived, split, 0, 6)
                hs = bass.ds(half * HH, HH)
                for t in range(NT):
                    m = rows(t)
                    for g in (4, 5):
                        n = steps.last[g - 1] + t
                        sp.wait_ge(read[n % 2], n // 2 + 1)
                    dst = o[3][0, 0, t * P:t * P + m, hs, :] if t < NT - 1 else o[6][0, 0, :, hs, :]
                    sp.dma_start(dst, v[:m, t, :].rearrange("p (h c) -> p h c", h=HH)).then_inc(v_out, 16)
                for t in range(NT):
                    m = rows(t)
                    sp.wait_ge(k_copied, t + 1)
                    dst = o[2][0, 0, t * P:t * P + m, hs, :] if t < NT - 1 else o[5][0, 0, :, hs, :]
                    sp.dma_start(dst, krow[:m, t % 2, :].rearrange("p (h c) -> p h c", h=HH)).then_inc(kout[t % 2], 16)
                sp.wait_ge(v_out, 16 * NT)
                sp.wait_ge(kout[0], 16 * 5)
                sp.wait_ge(kout[1], 16 * 4)

            @block.gpsimd
            def _(pool):
                steps.split(pool, w, arrived, rounded, split, mm_done, 1, 0)

            @block.tensor
            def _(pe):
                products(pe, steps, w, xT, ps, BANKS, split, mm_done, read)
                pe.wait_ge(act_read, (steps.last[3] + 1) // 2)
                pe.wait_ge(dve_read, steps.last[3] // 2)
                for t in range(NT):
                    m = rows(t)
                    if t >= 2:
                        pe.wait_ge(k_copied, t - 1)
                    for h in range(HH):
                        mm = pe.transpose(ps[:m, BANKS + t % 2, h * P:(h + 1) * P], kT[:, h, t * P:t * P + m], ident[:, :])
                    mm.then_inc(k_done, 1)

            def copy_out(eng, copy, me):
                for n, (g, f, i) in enumerate(steps.list):
                    if n % 2 != me:
                        continue
                    eng.wait_ge(mm_done, n + 1)
                    if f == "T":
                        c0, cw = CHUNKS[i[1]]
                        dst = (qT, kT)[g // 2][:, i[0], c0:c0 + cw]
                        src = ps[:, n % BANKS, 0:cw]
                    else:
                        m = rows(i)
                        dst, src = v[:m, i, group_columns(g)], ps[:m, n % BANKS, 0:GW]
                    copy(dst, src).then_inc(read[me], 1)

            @block.scalar
            def _(act):
                first_high(act, w, arrived, rounded)
                copy_out(act, lambda d, s: act.activation(d, s, ACT.Copy), 0)

            @block.vector
            def _(dve):
                first_low(dve, w, rounded, split)
                copy_out(dve, dve.tensor_copy, 1)
                for t in range(NT):
                    m = rows(t)
                    dve.wait_ge(k_done, t + 1)
                    if t >= 2:
                        dve.wait_ge(kout[t % 2], 16 * (t // 2))
                    dve.tensor_copy(krow[:m, t % 2, :], ps[:m, BANKS + t % 2, :]).then_inc(k_copied, 1)


def attention_units():
    def tile(i):
        js = list(range(i, -1, -1)) if i < NT - 1 else [i, -1]
        return [(i, j, j == js[0], j == js[-1]) for j in js]
    streams = [sum((tile(i) for i in s), []) for s in ((7, 5, 4), (6, 3, 2, 1, 0, 8))]
    out = []
    assert len(streams[0]) == len(streams[1])
    for n in range(len(streams[0])):
        for s in range(2):
            out.append((s, *streams[s][n]))
    return out


def attention(nc, a, half, w, ps, ident, tri, qT, kT, v, room, osb_d):
    units = attention_units()
    NU = len(units)
    tiles = {}
    for s in range(2):
        for n, i in enumerate([u[1] for u in units if u[0] == s and u[4]]):
            tiles[s, i] = n
    seq = {}
    done_before = [0, 0]
    for u in units:
        seq[u] = done_before[u[0]]
        done_before[u[0]] += 1

    with ExitStack() as c:
        def sb(name, shape):
            return c.enter_context(nc.sbuf_tensor(name, shape, F32))
        ckr = sb("ckr", [PAST, W512])
        ckT = sb("ckT", [P, HH, PAST])
        cv = sb("cv", [PAST, W512])
        z, sp_, arg = (room[:, :, :].rearrange("p h t -> p (h t)")[:, i * W512:(i + n) * W512]
                       .rearrange("p (b n) -> p b n", b=n) for i, n in ((0, 3), (3, 3), (6, 2)))
        ob = sb("ob", [P, 2, W512])
        Z, C, O, X = (0, 1), (2, 3), (4, 5), 6
        with Phase(nc, "cache_in ct_done ct_copied z_done z_copied abs_done e_done l_done sp_done sp_masked c_done "
                       "arg_done w_done w_masked o_done o_copied out0 out1 dve_s arrived rounded split") as (block, (
                cache_in, ct_done, ct_copied, z_done, z_copied, abs_done, e_done, l_done, sp_done, sp_masked, c_done,
                arg_done, w_done, w_masked, o_done, o_copied, out0, out1, dve_s, arrived, rounded, split)):
            outs = (out0, out1)
            diag = [n for n, u in enumerate(units) if u[3]]
            finals = [n for n, u in enumerate(units) if u[4]]

            def shape(u):
                m = rows(u[1])
                return m, (m if u[1] == NT - 1 and u[2] >= 0 else P)

            def view(ap, m):
                return ap[:, 0:HH * m].rearrange("p (h t) -> p h t", h=HH)

            @block.sync
            def _(sp):
                hs = bass.ds(half * HH, HH)
                sp.dma_start(ckr[:, :].rearrange("p (h c) -> p h c", h=HH), a["cache_sb_k"][0, 0, :, hs, :]).then_inc(cache_in, 16)
                sp.dma_start(cv[:, :].rearrange("p (h c) -> p h c", h=HH), a["cache_sb_v"][0, 0, :, hs, :]).then_inc(cache_in, 16)
                load_groups(sp, a, w, half, HGRN_COLS, arrived, split, 0, AHEAD)
                for n, f in enumerate(finals):
                    s, i = units[f][:2]
                    m = rows(i)
                    sp.wait_ge(o_copied, n + 1)
                    sp.dma_start(osb_d[bass.ds(half, 1), i * P:i * P + m, :].rearrange("a p n -> (a p) n"),
                                 ob[:m, n % 2, :]).then_inc(outs[n % 2], 16)
                sp.wait_ge(out0, 16 * 5)
                sp.wait_ge(out1, 16 * 4)

            @block.tensor
            def _(pe):
                pe.wait_ge(cache_in, 32)
                for h in range(HH):
                    mm = pe.transpose(ps[:, X, h * P:(h + 1) * P], ckr[:, h * P:(h + 1) * P], ident[:, :])
                mm.then_inc(ct_done, 1)
                pe.wait_ge(ct_copied, 1)

                def scores(n):
                    u = units[n]
                    m, kr = shape(u)
                    if n >= 2:
                        pe.wait_ge(z_copied, n - 1)
                    for h in range(HH):
                        keys = ckT[:, h, :] if u[2] < 0 else kT[:, h, u[2] * P:u[2] * P + kr]
                        mm = pe.matmul(ps[:kr, Z[n % 2], h * m:(h + 1) * m], keys, qT[:, h, u[1] * P:u[1] * P + m],
                                       start=True, stop=True)
                    mm.then_inc(z_done, 1)

                def sums(n):
                    u = units[n]
                    m, kr = shape(u)
                    pe.wait_ge(sp_done, n + 1)
                    if u[3]:
                        pe.wait_ge(sp_masked, diag.index(n) + 1)
                        before = [k for k in range(n) if units[k][0] == u[0]]
                        if before:
                            pe.wait_ge(arg_done, before[-1] + 1)
                    pe.matmul(ps[:, C[u[0]], 0:HH * m], tri[:kr, 1, :], sp_[:kr, n % 3, 0:HH * m], start=u[3], stop=True,
                              skip_group_check=True).then_inc(c_done, 1)

                def carry(n):
                    u = units[n]
                    m, kr = shape(u)
                    pe.wait_ge(arg_done, n + 1)
                    if not u[4]:
                        pe.matmul(ps[:, C[u[0]], 0:HH * m], tri[:kr, 2, :], sp_[:kr, n % 3, 0:HH * m], start=False,
                                  stop=True, skip_group_check=True)

                def values(n):
                    u = units[n]
                    m, kr = shape(u)
                    pe.wait_ge(w_done, n + 1)
                    if u[3]:
                        pe.wait_ge(w_masked, diag.index(n) + 1)
                        k = tiles[u[0], u[1]]
                        if k:
                            f = [x for x in finals if x < n and units[x][0] == u[0]]
                            pe.wait_ge(o_copied, finals.index(f[-1]) + 1)
                    for h in range(HH):
                        vals = cv[:, h * P:(h + 1) * P] if u[2] < 0 else v[:kr, u[2], h * P:(h + 1) * P]
                        mm = pe.matmul(ps[:m, O[u[0]], h * P:(h + 1) * P], arg[:kr, n % 2, h * m:(h + 1) * m], vals,
                                       start=u[3] and h == 0, stop=u[4], skip_group_check=True)
                    mm.then_inc(o_done, 1)

                scores(0)
                scores(1)
                for n in range(NU + 1):
                    if n + 2 < NU:
                        scores(n + 2)
                    if n < NU:
                        sums(n)
                    if n >= 1:
                        carry(n - 1)
                        values(n - 1)

            @block.scalar
            def _(act):
                act.preload_act_table_set("natural_log_exp_and_others")
                act.wait_ge(ct_done, 1)
                act.activation(ckT[:, :, :], ps[:, X, :].rearrange("p (h c) -> p h c", h=HH), ACT.Copy).then_inc(ct_copied, 1)

                def front(n):
                    u = units[n]
                    m, kr = shape(u)
                    w_ = HH * m
                    act.wait_ge(z_done, n + 1)
                    if n >= 3:
                        act.wait_ge(arg_done, n - 2)
                    act.activation(z[:kr, n % 3, 0:w_], ps[:kr, Z[n % 2], 0:w_], ACT.Copy, scale=SCALE).then_inc(z_copied, 1)
                    if n >= 3:
                        act.wait_ge(o_done, n - 2)
                    act.wait_ge(abs_done, n + 1)
                    act.activation(sp_[:kr, n % 3, 0:w_], sp_[:kr, n % 3, 0:w_], ACT.Exp, scale=-1.0).then_inc(e_done, 1)
                    act.wait_ge(e_done, n + 1)
                    act.activation(sp_[:kr, n % 3, 0:w_], sp_[:kr, n % 3, 0:w_], ACT.Ln, bias=1.0).then_inc(l_done, 1)

                def back(n):
                    u = units[n]
                    m, kr = shape(u)
                    w_ = HH * m
                    act.wait_ge(arg_done, n + 1)
                    act.activation(arg[:kr, n % 2, 0:w_], arg[:kr, n % 2, 0:w_], ACT.Exp).then_inc(w_done, 1)

                for n in range(NU + 1):
                    if n < NU:
                        front(n)
                    if n >= 1:
                        back(n - 1)

            @block.vector
            def _(dve):
                ch = Chain(dve, dve_s)

                def front(n):
                    u = units[n]
                    m, kr = shape(u)
                    w_ = HH * m
                    dve.wait_ge(z_copied, n + 1)
                    if n >= 3:
                        dve.wait_ge(o_done, n - 2)
                    absolute(dve, sp_[:kr, n % 3, 0:w_], z[:kr, n % 3, 0:w_]).then_inc(abs_done, 1)

                def middle(n):
                    u = units[n]
                    m, kr = shape(u)
                    w_ = HH * m
                    dve.wait_ge(l_done, n + 1)
                    dve.scalar_tensor_tensor(out=sp_[:kr, n % 3, 0:w_], in0=z[:kr, n % 3, 0:w_], scalar=0.0,
                                             in1=sp_[:kr, n % 3, 0:w_], op0=ALU.max, op1=ALU.add).then_inc(sp_done, 1)

                def back(n):
                    u = units[n]
                    m, kr = shape(u)
                    w_ = HH * m
                    dve.wait_ge(c_done, n + 1)
                    if n >= 2:
                        dve.wait_ge(o_done, n - 1)
                    if u[3]:
                        ch(dve.tensor_tensor(arg[:kr, n % 2, 0:w_], z[:kr, n % 3, 0:w_], ps[:kr, C[u[0]], 0:w_], ALU.subtract))
                        dve.tensor_scalar(arg[:kr, n % 2, 0:w_], arg[:kr, n % 2, 0:w_], 0.0, None, ALU.min).then_inc(arg_done, 1)
                    else:
                        dve.tensor_tensor(arg[:kr, n % 2, 0:w_], z[:kr, n % 3, 0:w_], ps[:kr, C[u[0]], 0:w_],
                                          ALU.subtract).then_inc(arg_done, 1)

                def outputs(n):
                    if n < 0 or not units[n][4]:
                        return
                    k = finals.index(n)
                    m = rows(units[n][1])
                    dve.wait_ge(o_done, n + 1)
                    if k >= 2:
                        dve.wait_ge(outs[k % 2], 16 * (k // 2))
                    dve.tensor_copy(ob[:m, k % 2, :], ps[:m, O[units[n][0]], :]).then_inc(o_copied, 1)

                front(0)
                for n in range(NU):
                    middle(n)
                    if n + 1 < NU:
                        front(n + 1)
                    back(n)
                    outputs(n - 1)
                outputs(NU - 1)

            @block.gpsimd
            def _(pool):
                for k, n in enumerate(diag):
                    if k == 2:
                        for g in range(AHEAD):
                            split_group(pool, w, g, arrived, rounded, split, 0)
                    u = units[n]
                    m, kr = shape(u)
                    below = tri[:kr, 0:1, 0:m].to_broadcast([kr, HH, m])
                    pool.wait_ge(sp_done, n + 1)
                    s_ = view(sp_[:kr, n % 3, :], m)
                    pool.tensor_tensor(s_, s_, below, ALU.mult).then_inc(sp_masked, 1)
                    pool.wait_ge(w_done, n + 1)
                    w_ = view(arg[:kr, n % 2, :], m)
                    pool.tensor_tensor(w_, w_, below, ALU.mult).then_inc(w_masked, 1)


def project_hgrn(nc, a, half, w, xT, ps, lbc, qT, kT, bT, v):
    steps = Steps("TTR")
    BANKS = 8
    with ExitStack() as c:
        tmp = c.enter_context(nc.sbuf_tensor("ptmp", [P, T], F32))
        keep = c.enter_context(nc.sbuf_tensor("pkeep", [P, T], F32))
        low = c.enter_context(nc.sbuf_tensor("plow", [P, T], F32))
        with Phase(nc, "arrived rounded split mm_done act_read dve_s act_s") as (block, (
                arrived, rounded, split, mm_done, act_read, dve_s, act_s)):
            NS = len(steps.list)
            TURNS = 11
            SETUP = 2

            @block.sync
            def _(sp):
                load_groups(sp, a, w, half, HGRN_COLS, arrived, split, AHEAD, 6)

            @block.gpsimd
            def _(pool):
                steps.split(pool, w, arrived, rounded, split, mm_done, AHEAD, AHEAD)

            @block.tensor
            def _(pe):
                products(pe, steps, w, xT, ps, BANKS, split, mm_done, (act_read,), AHEAD)

            @block.scalar
            def _(act):
                n = 0

                def copy_out(lo, hi):
                    for n in range(lo, hi):
                        g, f, i = steps.list[n]
                        act.wait_ge(mm_done, n + 1)
                        if f == "T":
                            c0, cw = CHUNKS[i[1]]
                            act.activation((bT, qT)[g // 2][:, i[0], c0:c0 + cw], ps[:, n % BANKS, 0:cw],
                                           (ACT.Copy, ACT.Silu)[g // 2]).then_inc(act_read, 1)
                        else:
                            m = rows(i)
                            act.activation(v[:m, i, group_columns(g)], ps[:m, n % BANKS, 0:GW], ACT.Copy).then_inc(act_read, 1)

                def turn(*args, **kw):
                    nonlocal n
                    act.activation(*args, **kw).then_inc(act_s, 1)
                    n += 1
                    act.wait_ge(act_s, n)

                copied = 3
                copy_out(0, copied)
                for h in range(HH):
                    base = SETUP + TURNS * h
                    act.wait_ge(dve_s, base + 2)
                    turn(tmp[:, :], tmp[:, :], ACT.Exp, scale=-1.0)
                    turn(tmp[:, :], tmp[:, :], ACT.Ln, bias=1.0)
                    act.wait_ge(dve_s, base + 4)
                    turn(kT[:, h, :], kT[:, h, :], ACT.Exp)
                    act.wait_ge(dve_s, base + 7)
                    turn(tmp[:, :], tmp[:, :], ACT.Exp, scale=-1.0)
                    turn(tmp[:, :], tmp[:, :], ACT.Ln, bias=1.0)
                    copy_out(copied, copied + 7)
                    copied += 7
                copy_out(copied, NS)

            @block.vector
            def _(dve):
                ch = Chain(dve, dve_s)
                ch(dve.memset(keep[:, :], 1.0))
                ch(dve.memset(keep[:, 0:T:P], 0.0))
                for h in range(HH):
                    A = bT[:, h, :]
                    NLb = lbc[:, 2, bass.ds(half * HH + h, 1)]
                    om = lbc[:, 1, bass.ds(half * HH + h, 1)]
                    na = 5 * h
                    dve.wait_ge(act_read, 3 * h + 3)
                    ch(absolute(dve, tmp[:, :], A))
                    ch(dve.tensor_scalar(kT[:, h, :], A, 0.0, None, ALU.min))
                    dve.wait_ge(act_s, na + 2)
                    ch(dve.tensor_tensor(tmp[:, :], kT[:, h, :], tmp[:, :], ALU.subtract))
                    ch(dve.tensor_tensor(kT[:, h, :], tmp[:, :], A, ALU.subtract))
                    ch(dve.tensor_scalar(A, A, NLb, None, ALU.add))
                    ch(dve.scalar_tensor_tensor(out=low[:, :], in0=A, scalar=0.0, in1=tmp[:, :], op0=ALU.min,
                                                op1=ALU.subtract))
                    ch(absolute(dve, tmp[:, :], A))
                    dve.wait_ge(act_s, na + 5)
                    ch(dve.tensor_tensor(tmp[:, :], tmp[:, :], low[:, :], ALU.subtract))
                    ch(dve.tensor_scalar(tmp[:, :], tmp[:, :], 0.0, None, ALU.min))
                    ch(dve.tensor_tensor_scan(A, keep[:, :], tmp[:, :], 0.0, ALU.mult, ALU.add))
                    ch(dve.tensor_scalar(kT[:, h, :], kT[:, h, :], om, None, ALU.mult))


def hgrn(nc, a, o, half, ps, ident, masks, x, qT, kT, bT, v, ohg_d):
    PARTS = [(0, 512), (512, T - 512)]
    parts = [(h, *p) for h in range(HH) for p in PARTS]
    chunks = []
    for n, (h, c0, cw) in enumerate(parts):
        for c in range(c0, c0 + cw, P):
            chunks.append((n, h, c, min(P, T - c), c // P))
    NC = len(chunks)
    last_of = {n: max(i for i, k in enumerate(chunks) if k[0] == n) for n in range(len(parts))}
    first_of = {n: min(i for i, k in enumerate(chunks) if k[0] == n) for n in range(len(parts))}
    PER = 2 * NL + 2
    with ExitStack() as c:
        def sb(name, shape):
            return c.enter_context(nc.sbuf_tensor(name, shape, F32))
        pm = sb("pm", [P, 2, NL + 1, P])
        aT = sb("aT", [P, 2, P])
        ke = sb("ke", [P, 2, P])
        orow = sb("orow", [P, 2, P])
        eb = sb("eb", [P, HH, NT])
        S = sb("S", [P, 2, 4, P])
        O, KE, SU = (4, 5), 6, 7
        with Phase(nc, "zeroed s_in0 s_in1 diff_done exp_done eb_done x_done p_done masked a_done o_done o_copied o_out0 o_out1 "
                       "ke_done ke_copied su_done s_done s_out0 s_out1") as (block, (
                zeroed, s_in0, s_in1, diff_done, exp_done, eb_done, x_done, p_done, masked, a_done, o_done, o_copied, o_out0, o_out1,
                ke_done, ke_copied, su_done, s_done, s_out0, s_out1)):
            o_out, s_in, s_out = (o_out0, o_out1), (s_in0, s_in1), (s_out0, s_out1)

            def src_state(k):
                return 2 if k[4] == NT - 1 else k[4] % 2

            def dst_state(k):
                return 3 if k[4] == NT - 1 else (k[4] + 1) % 2

            def halves(n):
                h, c0, cw = parts[n]
                out = []
                for i, hw in enumerate(LEVELS):
                    w_ = cw // (2 * hw) * (2 * hw)
                    for side in range(2):
                        out.append((i, side, hw, c0, w_))
                return out

            def seg(ap, c0, w_, hw, side):
                return ap[:, c0:c0 + w_].rearrange("p (g u) -> p g u", u=2 * hw)[:, :, side * hw:side * hw + hw]

            def ends(c0, cw):
                out = [(c0, cw // P * P, P)]
                if cw % P:
                    out.append((c0 + cw // P * P, cw % P, cw % P))
                return out

            def put_states(sp, h):
                hd = bass.ds(half * HH + h, 1)
                sp.dma_start(o[4][0, 0, hd, :, :].rearrange("a c v -> (a c) v"), S[:, h % 2, 0, :]).then_inc(s_out[h % 2], 16)
                sp.dma_start(o[7][0, 0, hd, :, :].rearrange("a c v -> (a c) v"), S[:, h % 2, 3, :]).then_inc(s_out[h % 2], 16)

            @block.sync
            def _(sp):
                for h in range(HH + 1):
                    if h >= 2:
                        sp.wait_ge(s_done, NT * (h - 1))
                        put_states(sp, h - 2)
                    if h == HH:
                        break
                    if h >= 2:
                        sp.wait_ge(s_out[h % 2], 32 * (h // 2))
                    sp.dma_start(S[:, h % 2, 2, :], a["state_hgrn"][0, 0, bass.ds(half * HH + h, 1), :, :]
                                 .rearrange("a c v -> (a c) v")).then_inc(s_in[h % 2], 16)
                sp.wait_ge(s_done, NT * HH)
                put_states(sp, HH - 1)
                for b in range(2):
                    sp.wait_ge(s_out[b], 16 * HH)

            @block.gpsimd
            def _(pool):
                for n, (h, c0, cw) in enumerate(parts):
                    base = n * (NL + 2)
                    for i, side, hw, b0, w_ in halves(n):
                        if side == 0:
                            pool.wait_ge(exp_done, base + i + 1)
                        q = (kT, qT)[side][:, h, :]
                        xs = seg(x[:, i, :], b0, w_, hw, side)
                        pool.tensor_tensor(xs, xs, seg(q, b0, w_, hw, side), ALU.mult).then_inc(x_done, 1)
                    for i, q in ((NL, qT), (NL + 1, kT)):
                        pool.wait_ge(exp_done, base + i + 1)
                        xs = x[:, i, c0:c0 + cw]
                        pool.tensor_tensor(xs, xs, q[:, h, c0:c0 + cw], ALU.mult).then_inc(x_done, 1)

            @block.scalar
            def _(act):
                for h in range(HH):
                    act.activation(eb[:, h, 0:NT - 1], bT[:, h, P - 1:SEQ:P], ACT.Exp).then_inc(eb_done, 1)
                    act.activation(eb[:, h, NT - 1:NT], bT[:, h, T - 1:T], ACT.Exp).then_inc(eb_done, 1)

                def exps(n):
                    h, c0, cw = parts[n]
                    for i in range(NL + 2):
                        w_ = cw // (2 * LEVELS[i]) * (2 * LEVELS[i]) if i < NL else cw
                        act.wait_ge(diff_done, 2 * (NL + 2) * n + 2 * (i + 1))
                        act.activation(x[:, i, c0:c0 + w_], x[:, i, c0:c0 + w_], ACT.Exp).then_inc(exp_done, 1)

                def copies(j):
                    k = chunks[j]
                    m = k[3]
                    act.wait_ge(ke_done, j + 1)
                    if j >= 2:
                        act.wait_ge(su_done, j - 1)
                    act.activation(ke[:m, j % 2, :], ps[:m, KE, 0:P], ACT.Copy).then_inc(ke_copied, 1)
                    act.wait_ge(o_done, j + 1)
                    if j >= 2:
                        act.wait_ge(o_out[j % 2], 16 * (j // 2))
                    act.activation(orow[:m, j % 2, :], ps[:m, O[j % 2], 0:P], ACT.Copy).then_inc(o_copied, 1)
                    act.wait_ge(o_copied, j + 1)
                    act.dma_start(ohg_d[bass.ds(half, 1), k[4] * P:k[4] * P + m, k[1] * P:(k[1] + 1) * P]
                                  .rearrange("a p n -> (a p) n"), orow[:m, j % 2, :]).then_inc(o_out[j % 2], 16)

                exps(0)
                exps(1)
                for j in range(NC):
                    copies(j)
                    n = chunks[j][0]
                    if j == last_of[n] and n + 2 < len(parts):
                        exps(n + 2)
                act.wait_ge(o_out0, 16 * (NC // 2))
                act.wait_ge(o_out1, 16 * (NC // 2))

            @block.vector
            def _(dve):
                def diffs(n):
                    h, c0, cw = parts[n]
                    b = bT[:, h, :]
                    if n >= 2:
                        dve.wait_ge(o_done, last_of[n - 2] + 1)
                        dve.wait_ge(ke_done, last_of[n - 2] + 1)
                        dve.wait_ge(p_done, last_of[n - 2] + 1)
                    for i, side, hw, b0, w_ in halves(n):
                        mid = b[:, b0:b0 + w_].rearrange("p (g u) -> p g u", u=2 * hw)[:, :, hw - 1:hw] \
                            .to_broadcast([P, w_ // (2 * hw), hw])
                        bs, xs = seg(b, b0, w_, hw, side), seg(x[:, i, :], b0, w_, hw, side)
                        dve.tensor_tensor(xs, *((mid, bs) if side == 0 else (bs, mid)), ALU.subtract).then_inc(diff_done, 1)
                    dve.tensor_copy(x[:, NL, c0:c0 + cw], b[:, c0:c0 + cw]).then_inc(diff_done, 2)
                    es = ends(c0, cw)
                    for e0, ew, u in es:
                        g = ew // u
                        bs = b[:, e0:e0 + ew].rearrange("p (g u) -> p g u", u=u)
                        xs = x[:, NL + 1, e0:e0 + ew].rearrange("p (g u) -> p g u", u=u)
                        dve.tensor_tensor(xs, bs[:, :, u - 1:u].to_broadcast([P, g, u]), bs, ALU.subtract) \
                            .then_inc(diff_done, 2 // len(es))

                def scores(j):
                    n, h, c0, m, t = chunks[j]
                    s = NL + 1 if m == P else NL
                    dve.wait_ge(p_done, j + 1)
                    if j >= 2:
                        dve.wait_ge(a_done, j - 1)
                    pp = ps[:m, 2 * (j % 2):2 * (j % 2) + 2, :].rearrange("p b (l t) -> p (b l) t", l=4)[:, 0:s, 0:m]
                    dve.tensor_tensor(pm[:m, j % 2, 0:s, 0:m], pp, masks[:m, 0:s, 0:m], ALU.mult).then_inc(masked, 1)
                    dve.wait_ge(masked, j + 1)
                    if j >= 2:
                        dve.wait_ge(o_done, j - 1)
                    dve.tensor_reduce(aT[:m, j % 2, 0:m], pm[:m, j % 2, 0:s, 0:m].rearrange("p l t -> p t l"), AX.X,
                                      ALU.add).then_inc(a_done, 1)

                def state(j):
                    k = chunks[j]
                    dve.wait_ge(su_done, j + 1)
                    dve.wait_ge(o_done, max(j - 1, 1))
                    if j >= 1:
                        dve.wait_ge(s_done, j)
                    if k[4] == 0:
                        dve.wait_ge(eb_done, 2 * HH)
                    if k[4] == NT - 1:
                        dve.wait_ge(s_in[k[1] % 2], 16 * (k[1] // 2 + 1))
                    dve.scalar_tensor_tensor(out=S[:, k[1] % 2, dst_state(k), :], in0=S[:, k[1] % 2, src_state(k), :],
                                             scalar=eb[:, k[1], k[4]:k[4] + 1], in1=ps[:, SU, 0:P], op0=ALU.mult,
                                             op1=ALU.add).then_inc(s_done, 1)

                diffs(0)
                diffs(1)
                scores(0)
                for j in range(NC):
                    if j + 1 < NC:
                        n = chunks[j + 1][0]
                        if j + 1 == first_of[n] and n + 1 < len(parts):
                            diffs(n + 1)
                        scores(j + 1)
                    if chunks[j][4] == 0:
                        if chunks[j][1] >= 2:
                            dve.wait_ge(s_out[chunks[j][1] % 2], 32 * (chunks[j][1] // 2))
                        dve.memset(S[:, chunks[j][1] % 2, 0, :], 0.0).then_inc(zeroed, 1)
                        dve.wait_ge(zeroed, chunks[j][1] + 1)
                    state(j)

            @block.tensor
            def _(pe):
                def products(j):
                    n, h, c0, m, t = chunks[j]
                    if j == first_of[n]:
                        pe.wait_ge(x_done, PER * (n + 1))
                    if j >= 2:
                        pe.wait_ge(masked, j - 1)
                    b0 = 2 * (j % 2)
                    pe.matmul(ps[:m, b0, 0:m], kT[:, h, c0:c0 + m], qT[:, h, c0:c0 + m], start=True, stop=True)
                    for i in range(NL if m == P else NL - 1):
                        xs = x[:, i, c0:c0 + m]
                        mm = pe.matmul(ps[:m, b0 + (i + 1) // 4, (i + 1) % 4 * P:(i + 1) % 4 * P + m], xs, xs,
                                       start=True, stop=True)
                    mm.then_inc(p_done, 1)
                    if j >= 1:
                        pe.wait_ge(ke_copied, j)
                    pe.transpose(ps[:m, KE, 0:P], x[:, NL + 1, c0:c0 + m], ident[:, :]).then_inc(ke_done, 1)

                def outputs(j):
                    k = chunks[j]
                    n, h, c0, m, t = k
                    vals = v[:m, t, h * P:(h + 1) * P]
                    pe.wait_ge(a_done, j + 1)
                    if j >= 2:
                        pe.wait_ge(o_copied, j - 1)
                    pe.matmul(ps[:m, O[j % 2], 0:P], aT[:m, j % 2, 0:m], vals, start=True, stop=False)
                    if t == 0:
                        pe.wait_ge(zeroed, h + 1)
                    if t == NT - 1:
                        pe.wait_ge(s_in[h % 2], 16 * (h // 2 + 1))
                    elif j >= 1:
                        pe.wait_ge(s_done, j)
                    pe.matmul(ps[:m, O[j % 2], 0:P], x[:, NL, c0:c0 + m], S[:, h % 2, src_state(k), :], start=False,
                              stop=True).then_inc(o_done, 1)
                    pe.wait_ge(ke_copied, j + 1)
                    if j >= 1:
                        pe.wait_ge(s_done, j)
                    pe.matmul(ps[:, SU, 0:P], ke[:m, j % 2, :], vals, start=True, stop=True).then_inc(su_done, 1)

                products(0)
                for j in range(NC):
                    if j + 1 < NC and chunks[j + 1][0] == chunks[j][0]:
                        products(j + 1)
                        outputs(j)
                    else:
                        outputs(j)
                        if j + 1 < NC:
                            products(j + 1)


def merge(nc, a, half, w, xT, ps, ident, g1, osb_d, ohg_d, mT_d):
    cols = (C_HG, C_GH, C_GS)
    steps = Steps("RRR")
    BANKS = 6
    with ExitStack() as c:
        def sb(name, shape):
            return c.enter_context(nc.sbuf_tensor(name, shape, F32))
        og = sb("og", [P, NT, W512])
        oa = sb("oa", [P, NT, W512])
        s = sb("sg", [P, 2, GW])
        mT = sb("mT", [P, 2, HH, P])
        sq = sb("sq", [P, P])
        rs = sb("rs", [P, NT, 8])
        hn = sb("hn", [P, P])
        with Phase(nc, "arrived rounded split mm_done act_read loads squares var roots rstd s_done g0 g0n on prod m_done t_done t_copied m_out0 m_out1 dve_s") as (
                block, (arrived, rounded, split, mm_done, act_read, loads, squares, var, roots, rstd, s_done, g0, g0n, on, prod, m_done,
                        t_done, t_copied, m_out0, m_out1, dve_s)):
            m_out = (m_out0, m_out1)
            NH = 2 * NT
            HG = HH // 2

            @block.sync
            def _(sp):
                load_groups(sp, a, w, half, cols, arrived, split, 0, 1)
                sp.dma_start(hn[:, :], a["hg_norm"][0].partition_broadcast(P)).then_inc(loads, 16)
                for buf, d in ((og, ohg_d), (oa, osb_d)):
                    sp.dma_start(buf[:, 0:NT - 1, :], d[bass.ds(half, 1), 0:SEQ, :].rearrange("a (t p) n -> p (a t) n", p=P)).then_inc(loads, 16)
                    sp.dma_start(buf[:DEC, NT - 1, :], d[bass.ds(half, 1), SEQ:T, :].rearrange("a p n -> (a p) n")).then_inc(loads, 16)
                for g in range(1, 6):
                    sp.wait_ge(split, g)
                    load_group(sp, a, w, half, cols, g).then_inc(arrived, 16)
                for t in range(NT):
                    m = rows(t)
                    sp.wait_ge(t_copied, t + 1)
                    sp.dma_start(mT_d[:, bass.ds(half * HH, HH), t * P:t * P + m], mT[:, t % 2, :, 0:m]).then_inc(m_out[t % 2], 16)
                sp.wait_ge(m_out[0], 16 * 5)
                sp.wait_ge(m_out[1], 16 * 4)
                sp.wait_ge(loads, 80)

            def turn(pe, t):
                m = rows(t)
                pe.wait_ge(m_done, NT + t + 1)
                if t >= 2:
                    pe.wait_ge(t_copied, t - 1)
                for h in range(HH):
                    mm = pe.transpose(ps[:, BANKS + t % 2, h * P:h * P + m], g1[:m, t, h * P:(h + 1) * P], ident[:m, :m])
                mm.then_inc(t_done, 1)

            @block.tensor
            def _(pe):
                for n, (g, f, t) in enumerate(steps.list):
                    if t == 0:
                        pe.wait_ge(split, g + 1)
                    if n >= BANKS:
                        pe.wait_ge(s_done, n - BANKS + 1)
                        e = n - BANKS
                        if e < NH:
                            pe.wait_ge(g0, e + 1)
                    project_step(pe, w, xT, ps, n % BANKS, g, f, t).then_inc(mm_done, 1)
                    if g == 5 and t >= 2:
                        turn(pe, t - 2)
                for t in (NT - 2, NT - 1):
                    turn(pe, t)

            @block.scalar
            def _(act):
                first_high(act, w, arrived, rounded)
                act.wait_ge(loads, 80)
                for t in range(NT):
                    m = rows(t)
                    for h in range(HH):
                        act.activation(sq[:m, :], og[:m, t, h * P:(h + 1) * P], ACT.Square,
                                       accum_out=rs[:m, t, h:h + 1]).then_inc(squares, 1)
                        act.wait_ge(squares, HH * t + h + 1)
                for t in range(NT):
                    m = rows(t)
                    act.wait_ge(var, t + 1)
                    act.activation(rs[:m, t, 4:8], rs[:m, t, 4:8], ACT.Sqrt).then_inc(roots, 1)

                def copy(t):
                    m = rows(t)
                    act.wait_ge(t_done, t + 1)
                    if t >= 2:
                        act.wait_ge(m_out[t % 2], 16 * (t // 2))
                    act.activation(mT[:, t % 2, :, 0:m],
                                   ps[:, BANKS + t % 2, :].rearrange("p (h n) -> p h n", h=HH)[:, :, 0:m], ACT.Copy).then_inc(t_copied, 1)

                for n, (g, f, t) in enumerate(steps.list):
                    m = rows(t)
                    act.wait_ge(mm_done, n + 1)
                    if n >= 2:
                        e = n - 2
                        if e < NH:
                            act.wait_ge(g0, e + 1)
                        elif e < 2 * NH:
                            act.wait_ge(prod, e - NH + 1)
                        else:
                            act.wait_ge(m_done, e - 2 * NH + 1)
                    act.activation(s[:m, n % 2, :], ps[:m, n % BANKS, 0:GW], ACT.Sigmoid).then_inc(s_done, 1)
                    if g == 5 and t >= 3:
                        copy(t - 3)
                for t in (NT - 3, NT - 2, NT - 1):
                    copy(t)

            @block.vector
            def _(dve):
                ch = Chain(dve, dve_s)
                first_low(dve, w, rounded, split)
                for t in range(NT):
                    m = rows(t)
                    dve.wait_ge(squares, HH * (t + 1))
                    dve.tensor_scalar(rs[:m, t, 4:8], rs[:m, t, 0:4], 1.0 / P, RMS_EPS, ALU.mult, ALU.add).then_inc(var, 1)
                for t in range(NT):
                    m = rows(t)
                    dve.wait_ge(roots, t + 1)
                    ch(dve.reciprocal(rs[:m, t, 0:4], rs[:m, t, 4:8]))
                for n, (g, f, t) in enumerate(steps.list):
                    m = rows(t)
                    cols_ = group_columns(g)
                    gate = g1[:m, t, cols_]
                    dve.wait_ge(s_done, n + 1)
                    if n < NH:
                        dve.tensor_tensor(gate, s[:m, n % 2, :], ps[:m, n % BANKS, 0:GW], ALU.mult).then_inc(g0, 1)
                        dve.wait_ge(g0, n + 1)
                        for h in range(g % 2 * HG, (g % 2 + 1) * HG):
                            hs = slice(h * P, (h + 1) * P)
                            dve.scalar_tensor_tensor(out=g1[:m, t, hs], in0=og[:m, t, hs], scalar=rs[:m, t, h:h + 1],
                                                     in1=g1[:m, t, hs], op0=ALU.mult, op1=ALU.mult).then_inc(g0n, 1)
                    elif n < 2 * NH:
                        dve.wait_ge(on, n - NH + 1)
                        dve.tensor_tensor(gate, gate, s[:m, n % 2, :], ALU.mult).then_inc(prod, 1)
                    else:
                        ch(dve.tensor_tensor(oa[:m, t, cols_], oa[:m, t, cols_], s[:m, n % 2, :], ALU.mult))
                        dve.wait_ge(prod, n - 2 * NH + 1)
                        dve.tensor_tensor(gate, gate, oa[:m, t, cols_], ALU.add).then_inc(m_done, 1)

            @block.gpsimd
            def _(pool):
                split_group(pool, w, 1, arrived, rounded, split, 0)
                pool.wait_ge(loads, 80)
                for g in range(2):
                    for t in range(NT):
                        m = rows(t)
                        pool.wait_ge(g0n, HG * (NT * g + t + 1))
                        gv = g1[:m, t, group_columns(g)].rearrange("p (h c) -> p h c", h=HG)
                        pool.tensor_tensor(gv, gv, hn[:m, :].unsqueeze(1).to_broadcast([m, HG, P]), ALU.mult).then_inc(on, 1)
                    split_group(pool, w, g + 2, arrived, rounded, split, 0, (mm_done, steps.last[g]))
                for g in (4, 5):
                    split_group(pool, w, g, arrived, rounded, split, 0, (mm_done, steps.last[g - 2]))


def output_projection(nc, a, ps, ident, gcol, bcol, st, mT_d, xT, xn_d, h2_d):
    with ExitStack() as c:
        wo = c.enter_context(nc.sbuf_tensor("wo", [P, HEADS, D], F32))
        woh, wol = (c.enter_context(nc.sbuf_tensor(n, [P, HEADS, D], F32R)) for n in ("woh", "wol"))
        mT = c.enter_context(nc.sbuf_tensor("mTo", [P, 2, HEADS, P], F32))
        mh, ml = (c.enter_context(nc.sbuf_tensor(n, [P, 2, HEADS, P], F32R)) for n in ("mTh", "mTl"))
        xr = c.enter_context(nc.sbuf_tensor("xr", [P, 2, D], F32))
        y = c.enter_context(nc.sbuf_tensor("y1", [P, 2, D], F32))
        with Phase(nc, "par_in wo_in0 wo_in1 w_high w_low m_in0 m_in1 m_high m_low x_in0 x_in1 mm_done sum_done dve_s var_ready root_ready y_ready t_done t_act stored0 stored1") as (block, (
                par_in, wo_in0, wo_in1, w_high, w_low, m_in0, m_in1, m_high, m_low, x_in0, x_in1, mm_done, sum_done, dve_s, var_ready, root_ready, y_ready, t_done, t_act, stored0, stored1)):
            x_in, m_in, stored = (x_in0, x_in1), (m_in0, m_in1), (stored0, stored1)

            def block_columns(b):
                return slice(b * 512, (b + 1) * 512)

            @block.sync
            def _(sp):
                for b in range(2):
                    sp.dma_start(wo[:, :, block_columns(b)], a["w_out"][0].rearrange("(k p) n -> p k n", p=P)[:, :, block_columns(b)]) \
                        .then_inc((wo_in0, wo_in1)[b], 16)
                sp.dma_start(gcol[:, :], a["ln1_g"][0].partition_broadcast(P)).then_inc(par_in, 16)
                sp.dma_start(bcol[:, :], a["ln1_b"][0].partition_broadcast(P)).then_inc(par_in, 16)
                for t in range(NT):
                    m = rows(t)
                    if t >= 2:
                        sp.wait_ge(m_low, t - 1)
                    sp.dma_start(mT[:, t % 2, :, 0:m], mT_d[:, :, t * P:t * P + m]).then_inc(m_in[t % 2], 16)
                    if t >= 2:
                        sp.wait_ge(sum_done, t - 1)
                    sp.dma_start(xr[:m, t % 2, :], xn_d[t * P:t * P + m, :]).then_inc(x_in[t % 2], 16)
                sp.wait_ge(par_in, 32)

            @block.tensor
            def _(pe):
                def turn(t):
                    m = rows(t)
                    pe.wait_ge(y_ready, t + 1)
                    if t >= 2:
                        pe.wait_ge(t_act, 2 * (t - 1))
                    for k in range(KT):
                        mm = pe.transpose(ps[:, 4 + 2 * (t % 2) + k // 4, (k % 4) * P:(k % 4) * P + m],
                                          y[:m, t % 2, k * P:(k + 1) * P], ident[:m, :m])
                    mm.then_inc(t_done, 1)

                for t in range(NT):
                    m = rows(t)
                    if t >= 2:
                        pe.wait_ge(sum_done, t - 1)
                    pe.wait_ge(m_low, t + 1)
                    for b in range(2):
                        if t == 0:
                            pe.wait_ge(w_low, b + 1)
                        for k in range(HEADS):
                            mm = split_product(pe, ps[:m, 2 * (t % 2) + b, :], mh[:, t % 2, k, 0:m], ml[:, t % 2, k, 0:m],
                                               woh[:, k, block_columns(b)], wol[:, k, block_columns(b)], k == 0, k == HEADS - 1)
                    mm.then_inc(mm_done, 1)
                    if t >= 1:
                        turn(t - 1)
                turn(NT - 1)

            @block.vector
            def _(dve):
                ch = Chain(dve, dve_s)
                for b in range(2):
                    dve.wait_ge(w_high, b + 1)
                    split_low(dve, wol[:, :, block_columns(b)], wo[:, :, block_columns(b)], woh[:, :, block_columns(b)]).then_inc(w_low, 1)
                dve.wait_ge(par_in, 32)
                for t in range(NT):
                    m = rows(t)
                    dve.wait_ge(mm_done, t + 1)
                    dve.wait_ge(x_in[t % 2], 16 * (t // 2 + 1))
                    if t >= 2:
                        dve.wait_ge(stored[t % 2], 16 * (t // 2))
                        dve.wait_ge(t_done, t - 1)
                    pp = ps[:m, 2 * (t % 2):2 * (t % 2) + 2, :].rearrange("p b n -> p (b n)")
                    dve.scalar_tensor_tensor(out=y[:m, t % 2, :], in0=xr[:m, t % 2, :], scalar=ALPHA, in1=pp, op0=ALU.mult,
                                             op1=ALU.add).then_inc(sum_done, 1)
                    dve.wait_ge(sum_done, t + 1)
                    layer_norm_rows(dve, ch, m, y[:, t % 2, :], y[:, t % 2, :], st[:, t % 2, :], gcol, var_ready, root_ready, t)
                    dve.tensor_tensor(y[:m, t % 2, :], y[:m, t % 2, :], bcol[:m, :], ALU.add).then_inc(y_ready, 1)

            @block.gpsimd
            def _(pool):
                for t in range(NT):
                    m = rows(t)
                    tile = [x[:, t % 2, :, 0:m] for x in (mT, mh, ml)]
                    pool.wait_ge(m_in[t % 2], 16 * (t // 2 + 1))
                    if t >= 2:
                        pool.wait_ge(mm_done, t - 1)
                    pool.tensor_copy(tile[1], tile[0]).then_inc(m_high, 1)
                    pool.wait_ge(m_high, t + 1)
                    split_low(pool, tile[2], tile[0], tile[1]).then_inc(m_low, 1)

            @block.scalar
            def _(act):
                for b in range(2):
                    act.wait_ge((wo_in0, wo_in1)[b], 16)
                    split_high(act, woh[:, :, block_columns(b)], wo[:, :, block_columns(b)]).then_inc(w_high, 1)
                for t in range(NT):
                    m = rows(t)
                    act.wait_ge(var_ready, t + 1)
                    act.activation(st[:m, t % 2, 15:16], st[:m, t % 2, 14:15], ACT.Sqrt).then_inc(root_ready, 1)
                    act.wait_ge(y_ready, t + 1)
                    act.dma_start(h2_d[t * P:t * P + m, :], y[:m, t % 2, :]).then_inc(stored[t % 2], 16)
                    act.wait_ge(t_done, t + 1)
                    for b in range(2):
                        act.activation(xT[:, 4 * b:4 * b + 4, t * P:t * P + m],
                                       ps[:, 4 + 2 * (t % 2) + b, :].rearrange("p (k n) -> p k n", k=4)[:, :, 0:m],
                                       ACT.Copy).then_inc(t_act, 1)
                act.wait_ge(stored[0], 16 * 5)
                act.wait_ge(stored[1], 16 * 4)


def router(nc, a, ps, xT, gates, chosen, picks):
    with ExitStack() as c:
        def sb(name, shape):
            return c.enter_context(nc.sbuf_tensor(name, shape, F32))
        wr = sb("wr", [P, KT, NE])
        rb = sb("rb", [P, NE])
        s = sb("rs_", [P, 2, NE])
        sbm = sb("sbm", [P, NE])
        rep = sb("rep", [P, NE])
        g8 = sb("g8", [P, NGRP, 8])
        gs = sb("gs", [P, NGRP])
        cmp_ = sb("cmp_", [P, 2, NGRP, NGRP])
        earlier = sb("earlier", [P, NGRP, NGRP])
        rank = sb("rank", [P, 3, NGRP])
        top = sb("top", [P, 8])
        tot = sb("tot", [P, 2])
        with Phase(nc, "r_in pooled memo mm_done s_done dve_s") as (block, (r_in, pooled, memo, mm_done, s_done, dve_s)):
            @block.sync
            def _(sp):
                sp.dma_start(wr[:, :, :], a["w_router"][0].rearrange("(k p) n -> p k n", p=P)).then_inc(r_in, 16)
                sp.dma_start(rb[:, :], a["router_bias"][0].partition_broadcast(P)).then_inc(r_in, 16)
                sp.wait_ge(r_in, 32)

            @block.gpsimd
            def _(pool):
                pool.memset(earlier[:, :, :], 1.0).then_inc(memo, 1)
                pool.wait_ge(memo, 1)
                pool.affine_select(out=earlier[:, :, :], in_=earlier[:, :, :], compare_op=ALU.is_ge, fill=0.0, base=-1,
                                   pattern=[[1, NGRP], [-1, NGRP]], channel_multiplier=0).then_inc(pooled, 1)

            @block.tensor
            def _(pe):
                pe.wait_ge(r_in, 32)
                for t in range(NT):
                    m = rows(t)
                    if t >= 2:
                        pe.wait_ge(s_done, t - 1)
                    for k in range(KT):
                        mm = pe.matmul(ps[:m, t % 2, 0:NE], xT[:, k, t * P:t * P + m], wr[:, k, :], start=k == 0, stop=k == KT - 1)
                    mm.then_inc(mm_done, 1)

            STEPS = 27

            @block.scalar
            def _(act):
                for t in range(NT):
                    m = rows(t)
                    act.wait_ge(mm_done, t + 1)
                    if t >= 2:
                        act.wait_ge(dve_s, STEPS * (t - 1))
                    act.activation(s[:m, t % 2, :], ps[:m, t % 2, 0:NE], ACT.Sigmoid).then_inc(s_done, 1)

            @block.vector
            def _(dve):
                ch = Chain(dve, dve_s)
                dve.wait_ge(pooled, 1)
                dve.wait_ge(r_in, 32)
                for t in range(NT):
                    m = rows(t)
                    sc = s[:m, t % 2, :]
                    B = [m, NGRP, NGRP]
                    dve.wait_ge(s_done, t + 1)
                    ch(dve.tensor_tensor(sbm[:m, :], sc, rb[:m, :], ALU.add))
                    for g in range(NGRP):
                        ch(dve.max(g8[:m, g, :], sbm[:m, g * EPG:(g + 1) * EPG]))
                    ch(dve.tensor_tensor(gs[:m, :], g8[:m, :, 0], g8[:m, :, 1], ALU.add))
                    own, other = gs[:m, :].unsqueeze(2).to_broadcast(B), gs[:m, :].unsqueeze(1).to_broadcast(B)
                    ch(dve.tensor_tensor(cmp_[:m, 0, :, :], other, own, ALU.is_gt))
                    ch(dve.tensor_tensor(cmp_[:m, 1, :, :], other, own, ALU.is_equal))
                    ch(dve.tensor_tensor(cmp_[:m, 1, :, :], cmp_[:m, 1, :, :], earlier[:m, :, :], ALU.mult))
                    ch(dve.tensor_tensor(cmp_[:m, 0, :, :], cmp_[:m, 0, :, :], cmp_[:m, 1, :, :], ALU.add))
                    ch(dve.tensor_reduce(rank[:m, 0, :], cmp_[:m, 0, :, :], AX.X, ALU.add))
                    ch(dve.tensor_scalar(rank[:m, 1, :], rank[:m, 0, :], float(TOPG), None, ALU.is_lt))
                    ch(dve.tensor_scalar(rank[:m, 2, :], rank[:m, 1, :], -1.0, -NEG_BIG, ALU.add, ALU.mult))
                    v3 = sbm[:m, :].rearrange("p (g e) -> p g e", g=NGRP)
                    ch(dve.tensor_tensor(v3, v3, rank[:m, 1, :].unsqueeze(2).to_broadcast([m, NGRP, EPG]), ALU.mult))
                    ch(dve.tensor_tensor(v3, v3, rank[:m, 2, :].unsqueeze(2).to_broadcast([m, NGRP, EPG]), ALU.add))
                    ch(dve.max(top[:m, :], sbm[:m, :]))
                    ch(dve.max_index(picks[:m, t, :], top[:m, :], sbm[:m, :]))
                    ch(dve.match_replace(rep[:m, :], top[:m, :], sbm[:m, :], 4 * NEG_BIG))
                    ch(dve.tensor_scalar(chosen[:m, t, :], rep[:m, :], 2 * NEG_BIG, None, ALU.is_lt))
                    ch(dve.tensor_tensor(gates[:m, t, :], chosen[:m, t, :], sc, ALU.mult))
                    ch(dve.tensor_reduce(tot[:m, 0:1], gates[:m, t, :], AX.X, ALU.add))
                    ch(dve.reciprocal(tot[:m, 1:2], tot[:m, 0:1]))
                    ch(dve.tensor_scalar(gates[:m, t, :], gates[:m, t, :], tot[:m, 1:2], ROUTE_SCALE, ALU.mult, ALU.mult))
                    assert ch.n == STEPS * (t + 1), ch.n




def dispatch(nc, a, ps, ident, ones, before, xT, gates, chosen, picks, ys_d, dest, w8, tab, tok_d, plan_d,
             gates_d, only_d):
    FILL = SLOTS // P
    order = []
    for n in range(2 * len(CHUNKS)):
        order += [(t, None) for t in range(2 * n, min(2 * n + 2, NT))] + [(None, n)]
    assert SLOTS % P == 0
    with ExitStack() as c:
        def sb(name, shape, dt=F32):
            return c.enter_context(nc.sbuf_tensor(name, shape, dt))
        wg, wu, wd = sb("swg", [P, KT, FE]), sb("swu", [P, KT, FE]), sb("swd", [P, 2, D])
        hT, sl, ys = sb("shT", [P, 2, T]), sb("ssl", [P, 2, 512]), sb("ys", [P, 2, D])
        only = sb("only", [P, NE])
        fill = sb("fill", [P, FILL], U32)
        tokens = sb("tokens", [P, NT], U32)
        num = sb("num", [P, 4, NE])
        numi = sb("numi", [P, NE], I32)
        rowi = sb("rowi", [P, 1], I32)
        rowf = sb("rowf", [P, 2])
        cnt = sb("cnt", [P, 4, NE])
        slot = sb("slot", [P, 2, NE])
        hot = sb("hot", [P, TOPK, NE])
        prod = sb("prod_", [P, TOPK, NE])
        pf = sb("pf", [P, TOPK])
        df = sb("df", [P, TOPK])
        one64 = sb("one64", [P, NE])
        plan = sb("plan", [P, 2], I32)
        planf = sb("planf", [P, 2])
        tb = sb("tb", [NE, CAP], U32)
        tbf = sb("tbf", [NE, CAP])
        POS, CNT, TB = 5, 6, 7
        PLAN = 29
        steps = [(f, ci) for f in range(2) for ci in range(3)]
        dsteps = [(t, b) for t in range(NT) for b in range(2)]
        with Phase(nc, "pooled filled w_in pos_done cnt_done dve_s slot_read dest_done sent plan_out tb_in tb_f tbT_done tab_s "
                       "gu_done s_done h_done d_done y_act y_dve yo0 yo1") as (block, (
                pooled, filled, w_in, pos_done, cnt_done, dve_s, slot_read, dest_done, sent, plan_out, tb_in, tb_f, tbT_done,
                tab_s, gu_done, s_done, h_done, d_done, y_act, y_dve, yo0, yo1)):
            y_out = (yo0, yo1)

            @block.gpsimd
            def _(pool):
                pool.memset(fill[:, :], NOBODY).then_inc(pooled, 1)
                pool.iota(tokens[:, :], pattern=[[P, NT]], base=0, channel_multiplier=1).then_inc(pooled, 1)
                pool.iota(numi[:, :], pattern=[[1, NE]], base=0, channel_multiplier=0).then_inc(pooled, 1)
                pool.iota(rowi[:, :], pattern=[[0, 1]], base=0, channel_multiplier=1).then_inc(pooled, 1)
                pool.wait_ge(pooled, 4)
                pool.wait_ge(filled, 16)
                for t in range(NT):
                    m = rows(t)
                    pool.wait_ge(dest_done, t + 1)
                    for k in range(TOPK):
                        pool.indirect_dma_start(out=tok_d[:, :], out_offset=bass.IndirectOffsetOnAxis(ap=dest[:m, t, k:k + 1], axis=0),
                                                in_=tokens[:m, t:t + 1], in_offset=None).then_inc(sent, 16)

            @block.sync
            def _(sp):
                sp.wait_ge(pooled, 4)
                sp.dma_start(tok_d.rearrange("(p n) o -> p (n o)", p=P), fill[:, :]).then_inc(filled, 16)
                for dst, n in ((wg, "w_sh_gate"), (wu, "w_sh_up"), (wd, "w_sh_down")):
                    sp.dma_start(dst[:, :, :], a[n][0].rearrange("(k p) n -> p k n", p=P)).then_inc(w_in, 16)
                sp.wait_ge(dve_s, PLAN)
                sp.dma_start(plan_d[0:OVB, :], plan[0:OVB, 0:1]).then_inc(plan_out, 16)
                sp.dma_start(plan_d[OVB:OVB + 1, :], plan[0:1, 1:2]).then_inc(plan_out, 16)
                sp.dma_start(only_d[:, :], only[0:OVB, :]).then_inc(plan_out, 16)
                sp.dma_start(gates_d[0:SEQ, :].rearrange("(t p) e -> p t e", p=P), gates[:, 0:NT - 1, :]).then_inc(plan_out, 16)
                sp.dma_start(gates_d[SEQ:T, :], gates[:DEC, NT - 1, :]).then_inc(plan_out, 16)
                for t in range(NT):
                    m = rows(t)
                    sp.wait_ge(y_act, t + 1)
                    sp.wait_ge(y_dve, t + 1)
                    sp.dma_start(ys_d[t * P:t * P + m, :], ys[:m, t % 2, :]).then_inc(y_out[t % 2], 16)
                sp.wait_ge(sent, 16 * NT * TOPK)
                sp.dma_start(tb[:, :], tok_d[0:NE * CAP, :].rearrange("(e s) o -> e (s o)", e=NE)).then_inc(tb_in, 16)
                sp.wait_ge(tb_in, 16)
                sp.wait_ge(plan_out, 80)
                sp.wait_ge(y_out[0], 16 * 5)
                sp.wait_ge(y_out[1], 16 * 4)

            @block.vector
            def _(dve):
                ch = Chain(dve, dve_s)
                NUM, BASE, STEP, FREE = (num[:, k, :] for k in range(4))
                dve.wait_ge(pooled, 4)
                ch(dve.tensor_copy(NUM, numi[:, :]))
                ch(dve.tensor_copy(rowf[:, 0:1], rowi[:, :]))
                ch(dve.tensor_scalar(BASE, NUM, float(CAP), None, ALU.mult))
                ch(dve.memset(one64[:, :], 1.0))
                dve.wait_ge(cnt_done, 1)
                ch(dve.tensor_scalar(cnt[:, 0, :], ps[:, CNT, 0:NE], float(CAP), None, ALU.subtract))
                for k in range(7):
                    ch(dve.tensor_scalar(cnt[:, 1, :], cnt[:, 0, :], float(P * k), None, ALU.is_gt))
                    if k == 0:
                        ch(dve.tensor_copy(cnt[:, 2, :], cnt[:, 1, :]))
                    else:
                        ch(dve.tensor_tensor(cnt[:, 2, :], cnt[:, 2, :], cnt[:, 1, :], ALU.add))
                ch(dve.tensor_tensor_scan(cnt[:, 3, :], one64[:, :], cnt[:, 2, :], 0.0, ALU.mult, ALU.add))
                ch(dve.tensor_tensor(cnt[:, 1, :], cnt[:, 3, :], cnt[:, 2, :], ALU.subtract))
                ch(dve.tensor_scalar(STEP, cnt[:, 1, :], float(P), float(NE * CAP - CAP), ALU.mult, ALU.add))
                ch(dve.tensor_tensor(STEP, STEP, BASE, ALU.subtract))
                ch(dve.tensor_scalar(cnt[:, 0, :], cnt[:, 3, :], rowf[:, 0:1], None, ALU.is_le))
                ch(dve.tensor_reduce(planf[:, 0:1], cnt[:, 0, :], AX.X, ALU.add))
                ch(dve.tensor_scalar(planf[:, 0:1], planf[:, 0:1], float(NE - 1), None, ALU.min))
                ch(dve.tensor_copy(planf[:, 1:2], cnt[:, 3, NE - 1:NE]))
                ch(dve.tensor_copy(plan[:, :], planf[:, :]))
                ch(dve.tensor_scalar(only[:, :], NUM, planf[:, 0:1], None, ALU.is_equal))
                assert ch.n == PLAN, ch.n
                def slots(t):
                    m = rows(t)
                    if t:
                        dve.wait_ge(slot_read, t)
                    dve.wait_ge(pos_done, t + 1)
                    pos = ps[:m, POS, 0:NE]
                    ch(dve.tensor_scalar(slot[:m, 0, :], pos, float(CAP), None, ALU.is_ge))
                    ch(dve.tensor_tensor(slot[:m, 0, :], slot[:m, 0, :], STEP[:m, :], ALU.mult))
                    dve.tensor_tensor(slot[:m, 0, :], slot[:m, 0, :], pos, ALU.add).then_inc(slot_read, 1)
                    dve.wait_ge(slot_read, t + 1)
                    ch(dve.tensor_tensor(slot[:m, 0, :], slot[:m, 0, :], BASE[:m, :], ALU.add))
                    ch(dve.tensor_copy(pf[:m, :], picks[:m, t, :]))
                    B = [m, TOPK, NE]
                    ch(dve.tensor_tensor(hot[:m, :, :], NUM[:m, :].unsqueeze(1).to_broadcast(B),
                                         pf[:m, :].unsqueeze(2).to_broadcast(B), ALU.is_equal))
                    ch(dve.tensor_tensor(prod[:m, :, :], hot[:m, :, :], slot[:m, 0, :].unsqueeze(1).to_broadcast(B), ALU.mult))
                    ch(dve.tensor_reduce(df[:m, :], prod[:m, :, :], AX.X, ALU.add))
                    dve.tensor_copy(dest[:m, t, :], df[:m, :]).then_inc(dest_done, 1)
                    ch(dve.tensor_tensor(prod[:m, :, :], hot[:m, :, :], gates[:m, t, :].unsqueeze(1).to_broadcast(B), ALU.mult))
                    ch(dve.tensor_reduce(w8[:m, t, :], prod[:m, :, :], AX.X, ALU.add))
                    ch(dve.tensor_scalar(pf[:m, :], df[:m, :], float(NE * CAP), None, ALU.is_lt))
                    ch(dve.tensor_tensor(w8[:m, t, :], w8[:m, t, :], pf[:m, :], ALU.mult))

                def hidden(n):
                    f, ci = steps[n]
                    c0, cw = CHUNKS[ci]
                    dve.wait_ge(s_done, n + 1)
                    dve.tensor_tensor(hT[:, f, c0:c0 + cw], sl[:, n % 2, 0:cw], ps[:, 2 * (n % 2) + 1, 0:cw], ALU.mult).then_inc(h_done, 1)

                for t, n in order:
                    slots(t) if n is None else hidden(n)
                for n, (t, b) in enumerate(dsteps):
                    if n % 2 == 0:
                        continue
                    m = rows(t)
                    dve.wait_ge(d_done, n + 1)
                    if t >= 2:
                        dve.wait_ge(y_out[t % 2], 16 * (t // 2))
                    dve.tensor_copy(ys[:m, t % 2, b * 512:(b + 1) * 512], ps[:m, 2 + n % 3, :]).then_inc(y_dve, 1)
                dve.wait_ge(tb_in, 16)
                dve.tensor_copy(tbf[:, :], tb[:, :]).then_inc(tb_f, 1)
                dve.wait_ge(tbT_done, 1)
                dve.tensor_copy(tab[:, :, 0], ps[:, TB, 0:NE]).then_inc(tab_s, 1)
                dve.tensor_copy(tab[:CAP - P, :, 1], ps[:CAP - P, TB, NE:2 * NE]).then_inc(tab_s, 1)

            @block.scalar
            def _(act):
                for n, (f, ci) in enumerate(steps):
                    c0, cw = CHUNKS[ci]
                    act.wait_ge(gu_done, n + 1)
                    if n >= 2:
                        act.wait_ge(h_done, n - 1)
                    act.activation(sl[:, n % 2, 0:cw], ps[:, 2 * (n % 2), 0:cw], ACT.Silu).then_inc(s_done, 1)
                for n, (t, b) in enumerate(dsteps):
                    if n % 2:
                        continue
                    m = rows(t)
                    act.wait_ge(d_done, n + 1)
                    if t >= 2:
                        act.wait_ge(y_out[t % 2], 16 * (t // 2))
                    act.activation(ys[:m, t % 2, b * 512:(b + 1) * 512], ps[:m, 2 + n % 3, :], ACT.Copy).then_inc(y_act, 1)

            @block.tensor
            def _(pe):
                for t in range(NT):
                    m = rows(t)
                    mm = pe.matmul(ps[:, CNT, 0:NE], ones[:m, :], chosen[:m, t, :], start=t == 0, stop=t == NT - 1)
                mm.then_inc(cnt_done, 1)
                def before_tokens(t):
                    m = rows(t)
                    if t:
                        pe.wait_ge(slot_read, t)
                    mm = pe.matmul(ps[:m, POS, 0:NE], before[:m, :m], chosen[:m, t, :], start=True, stop=t == 0)
                    for u in range(t):
                        mm = pe.matmul(ps[:m, POS, 0:NE], ones[:, :m], chosen[:, u, :], start=False, stop=u == t - 1)
                    mm.then_inc(pos_done, 1)

                def gate_up(n):
                    f, ci = steps[n]
                    c0, cw = CHUNKS[ci]
                    if n == 0:
                        pe.wait_ge(w_in, 48)
                    if n >= 2:
                        pe.wait_ge(h_done, n - 1)
                    for wt, bank in ((wg, 2 * (n % 2)), (wu, 2 * (n % 2) + 1)):
                        for k in range(KT):
                            mm = pe.matmul(ps[:, bank, 0:cw], wt[:, k, f * P:(f + 1) * P], xT[:, k, c0:c0 + cw],
                                           start=k == 0, stop=k == KT - 1)
                    mm.then_inc(gu_done, 1)

                for t, n in order:
                    before_tokens(t) if n is None else gate_up(n)
                pe.wait_ge(h_done, len(steps))
                for n, (t, b) in enumerate(dsteps):
                    m = rows(t)
                    if n >= 3:
                        e = n - 3
                        pe.wait_ge(*((y_dve, e // 2 + 1) if e % 2 else (y_act, e // 2 + 1)))
                    for f in range(2):
                        mm = pe.matmul(ps[:m, 2 + n % 3, :], hT[:, f, t * P:t * P + m], wd[:, f, b * 512:(b + 1) * 512],
                                       start=f == 0, stop=f == 1)
                    mm.then_inc(d_done, 1)
                pe.wait_ge(tb_f, 1)
                pe.transpose(ps[:, TB, 0:NE], tbf[:, 0:P], ident[:NE, :NE])
                pe.transpose(ps[:CAP - P, TB, NE:2 * NE], tbf[:, P:CAP], ident[:NE, :NE]).then_inc(tbT_done, 1)


def experts(nc, a, ps, ident, tab, h2_d, ye_d, bufs):
    wg, wu, wd, xg, sl, yo = bufs
    C2 = CAP - P
    GB, UB, TB, DB = 0, 2, 5, (4, 1, 2, 3)
    with ExitStack() as c:
        def sb(name, shape, dt=F32):
            return c.enter_context(nc.sbuf_tensor(name, shape, dt))
        idx = sb("idx", [P, 2, 2], U32)
        wgh, wgl, wuh, wul = (sb(n, [P, KT, FE], F32R) for n in ("wgh", "wgl", "wuh", "wul"))
        wdh, wdl = (sb(n, [P, 2, D], F32R) for n in ("wdh", "wdl"))
        xhl = sb("xghl", [P, KT, 2 * CAP], F32R)
        xh, xl = xhl[:, :, 0:CAP], xhl[:, :, CAP:2 * CAP]
        gate, up = sb("gate", [P, 2 * CAP]), sb("up", [P, 2 * CAP])
        hT = sb("hT", [P, 2 * CAP])
        hh, hl = (sb(n, [P, 2, 2, CAP], F32R) for n in ("hTh", "hTl"))
        with Phase(nc, "cleared gu_part gu_sum g_in0 g_in1 u_in0 u_in1 d_in0 d_in1 idx_ready x_in0 x_in1 t_done x_high x_low gh gl uh ul dh dl "
                       "g_done u_done s_done h_s h_high h_done d_done y_ready st0 st1") as (block, (
                cleared, gu_part, gu_sum, gi0, gi1, ui0, ui1, di0, di1, idx_ready, xi0, xi1, t_done, x_high, x_low, gh, gl, uh, ul, dh, dl,
                g_done, u_done, s_done, h_s, h_high, h_done, d_done, y_ready, st0, st1)):
            g_in, u_in, d_in, x_in, stored = (gi0, gi1), (ui0, ui1), (di0, di1), (xi0, xi1), (st0, st1)
            high, low = (gh, uh, dh), (gl, ul, dl)
            GATE, UP, DOWN = range(3)

            def source(n, e):
                return a[n][0, bass.ds(e, 1), :, :].rearrange("o (k p) n -> p (o k) n", p=P)

            def every_expert(eng, body):
                def one(e):
                    body(e, e % 2, lambda d: (e + d) // 2)
                for e in range(3):
                    one(e)
                with eng.Fori(2, NE // 2 - 1) as j:
                    for r in range(2):
                        body(2 * j + r - 1, 1 - r, lambda d: j + (r - 1 + d) // 2)
                for e in range(NE - 3, NE):
                    one(e)

            def at_least(e, n):
                return not isinstance(e, int) or e >= n

            def at_most(e, n):
                return not isinstance(e, int) or e <= n

            def high_part(act, which, e, b, uses):
                arrived, raw, hi = ((g_in, wg, wgh), (u_in, wu, wuh), (d_in, wd, wdh))[which]
                act.wait_ge(arrived[b], 16 * (uses + 1))
                if at_least(e, 1):
                    if which == DOWN:
                        act.wait_ge(d_done, 4 * e)
                    else:
                        act.wait_ge((g_done, u_done)[which], e)
                split_high(act, hi[:, :, :], raw[:, b, :, :]).then_inc(high[which], 1)

            def low_part(dve, which, e, b):
                raw, hi, lo = ((wg, wgh, wgl), (wu, wuh, wul), (wd, wdh, wdl))[which]
                dve.wait_ge(high[which], e + 1)
                split_low(dve, lo[:, :, :], raw[:, b, :, :], hi[:, :, :]).then_inc(low[which], 1)

            def transposed(part):
                return ((part[:, :, 0:P], ps[:, TB:TB + 2, :].rearrange("p b (k n) -> p (b k) n", n=P)),
                        (part[:, :, P:CAP], ps[:, TB + 2, 0:KT * C2].rearrange("p (k n) -> p k n", n=C2)))

            @block.sync
            def _(sp):
                def load(which, e, b):
                    arrived, raw, n = ((g_in, wg, "w_exp_gate"), (u_in, wu, "w_exp_up"), (d_in, wd, "w_exp_down"))[which]
                    sp.dma_start(raw[:, b, :, :], source(n, e)).then_inc(arrived[b], 16)

                def store(e, b):
                    sp.wait_ge(y_ready, 4 * e + 4)
                    sp.dma_start(ye_d[bass.ds(e * CAP, P), :], yo[:, b, 0, :]).then_inc(stored[b], 16)
                    sp.dma_start(ye_d[bass.ds(e * CAP + P, C2), :], yo[:C2, b, 1, :]).then_inc(stored[b], 16)

                for b in range(2):
                    for which in range(3):
                        load(which, b, b)

                def body(e, b, half):
                    if at_most(e, NE - 3):
                        for which in (GATE, UP):
                            sp.wait_ge(low[which], e + 1)
                            load(which, e + 2, b)
                    if at_least(e, 2):
                        store(e - 2, b)
                    if at_least(e, 1) and at_most(e, NE - 2):
                        sp.wait_ge(low[DOWN], e)
                        load(DOWN, e + 1, 1 - b)
                every_expert(sp, body)
                for e in (NE - 2, NE - 1):
                    store(e, e % 2)
                for b in range(2):
                    sp.wait_ge(stored[b], 16 * NE)

            @block.gpsimd
            def _(pool):
                pool.memset(xg[:, 0, :, :], 0.0).then_inc(cleared, 1)
                pool.memset(xg[:, 1, :, :], 0.0).then_inc(cleared, 1)
                pool.wait_ge(cleared, 2)
                last_row = pool.to_reg(T - 1)

                def body(e, b, half):
                    if at_least(e, 2):
                        pool.wait_ge(x_in[b], 32 * half(0))
                        pool.wait_ge(t_done, e - 1)
                    pool.tensor_copy(idx[:, b, 0:1], tab[:, bass.ds(e, 1), 0]).then_inc(idx_ready, 1)
                    pool.tensor_copy(idx[:C2, b, 1:2], tab[:C2, bass.ds(e, 1), 1]).then_inc(idx_ready, 1)
                    pool.wait_ge(idx_ready, 2)
                    pool.sem_clear(idx_ready)
                    for j, m in ((0, P), (1, C2)):
                        pool.indirect_dma_start(out=xg[:m, b, j, :], out_offset=None, in_=h2_d[:, :],
                                                in_offset=bass.IndirectOffsetOnAxis(ap=idx[:m, b, j:j + 1], axis=0),
                                                bounds_check=last_row, oob_is_err=False).then_inc(x_in[b], 16)
                every_expert(pool, body)

            @block.tensor
            def _(pe):
                def turn(e, b, uses):
                    pe.wait_ge(x_in[b], 32 * (uses + 1))
                    if at_least(e, 1):
                        pe.wait_ge(x_low, 2 * e)
                    for k in range(KT):
                        pe.transpose(ps[:, TB + k // 4, k % 4 * P:(k % 4 + 1) * P], xg[:, b, 0, k * P:(k + 1) * P], ident[:, :])
                    for k in range(KT):
                        mm = pe.transpose(ps[:, TB + 2, k * C2:(k + 1) * C2], xg[:C2, b, 1, k * P:(k + 1) * P], ident[:C2, :C2])
                    mm.then_inc(t_done, 1)

                def down(e, b, following):
                    pe.wait_ge(low[DOWN], e + 1)
                    pe.wait_ge(h_done, e + 1)
                    for n in range(4):
                        j, q = divmod(n, 2)
                        m = (P, C2)[j]
                        if following and n in (1, 2):
                            pe.wait_ge(gu_sum, 2 * e + n + 2)
                        if n == 0 and at_least(e, 1):
                            pe.wait_ge(y_ready, 4 * e - 3)
                        for f in range(2):
                            mm = split_product(pe, ps[:m, DB[n], :], hh[:, b, f, j * P:j * P + m], hl[:, b, f, j * P:j * P + m],
                                               wdh[:, f, q * 512:(q + 1) * 512], wdl[:, f, q * 512:(q + 1) * 512], f == 0, f == 1)
                        mm.then_inc(d_done, 1)

                turn(0, 0, 0)

                def body(e, b, half):
                    pe.wait_ge(x_low, 2 * e + 2)
                    for which, wh, wl, bank, done in ((GATE, wgh, wgl, GB, g_done), (UP, wuh, wul, UB, u_done)):
                        pe.wait_ge(low[which], e + 1)
                        for f in range(2):
                            if at_least(e, 2) and bank + f:
                                pe.wait_ge(y_ready, 4 * e - 8 + DB.index(bank + f) + 1)
                            elif at_least(e, 1) and not bank + f:
                                pe.wait_ge(gu_sum, 2 * e)
                            for k in range(KT):
                                cols = slice(f * P, (f + 1) * P)
                                pe.matmul(ps[:, bank + f, 0:2 * CAP], wh[:, k, cols], xhl[:, k, :], start=k == 0, stop=False,
                                          skip_group_check=True)
                                mm = pe.matmul(ps[:, bank + f, 0:CAP], wl[:, k, cols], xh[:, k, :], start=False,
                                               stop=k == KT - 1, skip_group_check=True)
                        mm.then_inc(done, 1)
                    if at_most(e, NE - 2):
                        turn(e + 1, 1 - b, half(1))
                    if at_least(e, 1):
                        down(e - 1, 1 - b, True)
                every_expert(pe, body)
                down(NE - 1, 1, False)

            @block.scalar
            def _(act):
                def x_high_part(e):
                    act.wait_ge(t_done, e + 1)
                    for dst, src in transposed(xh):
                        split_high(act, dst, src).then_inc(x_high, 1)

                def copy_rows(e, b, uses):
                    for n in range(4):
                        j, q = divmod(n, 2)
                        m = (P, C2)[j]
                        act.wait_ge(d_done, 4 * e + n + 1)
                        if n == 0 and at_least(e, 2):
                            act.wait_ge(stored[b], 32 * uses)
                        act.activation(yo[:m, b, j, q * 512:(q + 1) * 512], ps[:m, DB[n], :], ACT.Copy).then_inc(y_ready, 1)

                high_part(act, GATE, 0, 0, 0)
                x_high_part(0)
                high_part(act, UP, 0, 0, 0)

                def body(e, b, half):
                    if at_least(e, 1):
                        high_part(act, DOWN, e - 1, 1 - b, half(-1))
                    if at_most(e, NE - 2):
                        high_part(act, GATE, e + 1, 1 - b, half(1))
                    act.wait_ge(gu_sum, 2 * e + 1)
                    if at_least(e, 1):
                        act.wait_ge(h_s, e)
                    act.activation(sl[:, :], gate[:, :], ACT.Silu).then_inc(s_done, 1)
                    if at_most(e, NE - 2):
                        x_high_part(e + 1)
                        high_part(act, UP, e + 1, 1 - b, half(1))
                    if at_least(e, 1):
                        copy_rows(e - 1, 1 - b, half(-1))
                every_expert(act, body)
                high_part(act, DOWN, NE - 1, 1, NE // 2 - 1)
                copy_rows(NE - 1, 1, NE // 2 - 1)

            @block.vector
            def _(dve):
                def x_low_part(e):
                    for n, ((dst, src), (hi, _)) in enumerate(zip(transposed(xl), transposed(xh))):
                        dve.wait_ge(x_high, 2 * e + n + 1)
                        split_low(dve, dst, src, hi).then_inc(x_low, 1)

                low_part(dve, GATE, 0, 0)
                x_low_part(0)
                low_part(dve, UP, 0, 0)

                def body(e, b, half):
                    if at_least(e, 1):
                        low_part(dve, DOWN, e - 1, 1 - b)
                    if at_most(e, NE - 2):
                        low_part(dve, GATE, e + 1, 1 - b)
                    dve.wait_ge(u_done, e + 1)
                    for n, (bank, whole) in enumerate(((GB, gate), (UB, up))):
                        if at_least(e, 1) and n == 0:
                            dve.wait_ge(s_done, e)
                        two = whole[:, :].rearrange("p (f n) -> p f n", f=2)
                        dve.tensor_copy(two, ps[:, bank:bank + 2, CAP:2 * CAP]).then_inc(gu_part, 1)
                        dve.wait_ge(gu_part, 2 * e + n + 1)
                        dve.tensor_tensor(two, two, ps[:, bank:bank + 2, 0:CAP], ALU.add).then_inc(gu_sum, 1)
                    dve.wait_ge(gu_sum, 2 * e + 2)
                    dve.wait_ge(s_done, e + 1)
                    dve.tensor_tensor(hT[:, :], sl[:, :], up[:, :], ALU.mult).then_inc(h_s, 1)
                    dve.wait_ge(h_s, e + 1)
                    if at_least(e, 2):
                        dve.wait_ge(d_done, 4 * e - 4)
                    flat = [t[:, b, :, :].rearrange("p f n -> p (f n)") for t in (hh, hl)]
                    dve.tensor_copy(flat[0], hT[:, :]).then_inc(h_high, 1)
                    dve.wait_ge(h_high, e + 1)
                    split_low(dve, flat[1], hT[:, :], flat[0]).then_inc(h_done, 1)
                    if at_most(e, NE - 2):
                        x_low_part(e + 1)
                        low_part(dve, UP, e + 1, 1 - b)
                every_expert(dve, body)
                low_part(dve, DOWN, NE - 1, 1)


def overflow(nc, a, ps, ident, h2_d, ys_d, tok_d, plan_d, gates_d, only_d, bufs):
    wg, wu, wd, xg, sl, yo = bufs
    with ExitStack() as c:
        idx = c.enter_context(nc.sbuf_tensor("oidx", [P, 1], U32))
        gr, on, pr = (c.enter_context(nc.sbuf_tensor(n, [P, NE], F32)) for n in ("ogr", "oon", "opr"))
        wt_ = c.enter_context(nc.sbuf_tensor("ow", [P, 1], F32))
        xgT = c.enter_context(nc.sbuf_tensor("oxT", [P, 1, KT, P], F32))
        hT = c.enter_context(nc.sbuf_tensor("ohT", [P, 2, P], F32))
        total = nc.values_load(plan_d[OVB:OVB + 1, 0:1], min_val=0, max_val=OVB)
        c.enter_context(nc.If(total > 0))
        with nc.Fori(0, OVB) as i:
            with nc.If(i < total):
                with Phase(nc, "oin ocl ox ot ocp ogu os oh od osc oy oout", ("ox", "oout")) as (block, (
                        oin, cleared, ox, ot, ocp, ogu, os_, oh, od, osc, oy, oout)):
                    first = NE * CAP + i * P

                    @block.sync
                    def _(sp):
                        sp.dma_start(idx[:, :], tok_d[bass.ds(first, P), :]).then_inc(oin, 16)
                        e = sp.value_load(plan_d[bass.ds(i, 1), 0:1], min_val=0, max_val=NE - 1)
                        for dst, n in ((wg, "w_exp_gate"), (wu, "w_exp_up"), (wd, "w_exp_down")):
                            sp.dma_start(dst[:, 0, :, :], a[n][0, bass.ds(e, 1), :, :].rearrange("o (k p) n -> p (o k) n", p=P)) \
                                .then_inc(oin, 16)
                        sp.dma_start(on[:, :], only_d[bass.ds(i, 1), :].rearrange("o e -> (o e)").partition_broadcast(P)).then_inc(oin, 16)

                    @block.gpsimd
                    def _(pool):
                        pool.memset(gr[:, :], 0.0).then_inc(cleared, 1)
                        pool.memset(yo[:, 0, 0, :], 0.0).then_inc(cleared, 1)
                        pool.wait_ge(cleared, 2)
                        pool.wait_ge(oin, 80)
                        at = bass.IndirectOffsetOnAxis(ap=idx[:, :], axis=0)
                        pool.indirect_dma_start(out=gr[:, :], out_offset=None, in_=gates_d[:, :], in_offset=at,
                                                bounds_check=T - 1, oob_is_err=False).then_inc(ox, 16)
                        pool.indirect_dma_start(out=yo[:, 0, 0, :], out_offset=None, in_=ys_d[:, :], in_offset=at,
                                                bounds_check=T - 1, oob_is_err=False).then_inc(ox, 16)
                        pool.indirect_dma_start(out=xg[:, 0, 0, :], out_offset=None, in_=h2_d[:, :],
                                                in_offset=at, bounds_check=T - 1, oob_is_err=False).then_inc(ox, 16)
                        pool.wait_ge(oy, 2)
                        pool.indirect_dma_start(out=ys_d[:, :], out_offset=at, in_=yo[:, 0, 0, :], in_offset=None,
                                                bounds_check=T - 1, oob_is_err=False).then_inc(oout, 16)
                        pool.wait_ge(oout, 16)

                    @block.tensor
                    def _(pe):
                        pe.wait_ge(ox, 48)
                        for k in range(KT):
                            mm = pe.transpose(ps[:, k // 4, k % 4 * P:(k % 4 + 1) * P], xg[:, 0, 0, k * P:(k + 1) * P], ident[:, :])
                        mm.then_inc(ot, 1)
                        pe.wait_ge(ocp, 1)
                        for wt, bank in ((wg, 2), (wu, 3)):
                            for f in range(2):
                                for k in range(KT):
                                    mm = pe.matmul(ps[:, bank, f * P:(f + 1) * P], wt[:, 0, k, f * P:(f + 1) * P], xgT[:, 0, k, 0:P],
                                                   start=k == 0, stop=k == KT - 1)
                        mm.then_inc(ogu, 1)
                        pe.wait_ge(oh, 1)
                        for q in range(2):
                            for f in range(2):
                                mm = pe.matmul(ps[:, 4 + q, :], hT[:, f, 0:P], wd[:, 0, f, q * 512:(q + 1) * 512], start=f == 0, stop=f == 1)
                            mm.then_inc(od, 1)

                    @block.scalar
                    def _(act):
                        act.wait_ge(ot, 1)
                        act.activation(xgT[:, 0, :, 0:P], ps[:, 0:2, :].rearrange("p b (k n) -> p (b k) n", n=P), ACT.Copy).then_inc(ocp, 1)
                        act.wait_ge(ogu, 1)
                        act.activation(sl[:, 0:2 * P], ps[:, 2, 0:2 * P], ACT.Silu).then_inc(os_, 1)

                    @block.vector
                    def _(dve):
                        dve.wait_ge(os_, 1)
                        dve.tensor_tensor(hT[:, :, 0:P], sl[:, 0:2 * P].rearrange("p (f n) -> p f n", f=2),
                                          ps[:, 3, 0:2 * P].rearrange("p (f n) -> p f n", f=2), ALU.mult).then_inc(oh, 1)
                        dve.wait_ge(oin, 80)
                        dve.wait_ge(ox, 48)
                        dve.tensor_tensor(pr[:, :], gr[:, :], on[:, :], ALU.mult).then_inc(osc, 1)
                        dve.wait_ge(osc, 1)
                        dve.tensor_reduce(wt_[:, :], pr[:, :], AX.X, ALU.add).then_inc(osc, 1)
                        dve.wait_ge(osc, 2)
                        for q in range(2):
                            dve.wait_ge(od, q + 1)
                            yq = yo[:, 0, 0, q * 512:(q + 1) * 512]
                            dve.scalar_tensor_tensor(out=yq, in0=ps[:, 4 + q, :], scalar=wt_[:, 0:1], in1=yq, op0=ALU.mult,
                                                     op1=ALU.add).then_inc(oy, 1)


def combine(nc, a, o, ps, ident, gcol, bcol, st, ys_d, dest, w8, ye_d, h2_d):
    PK = 5
    VK = TOPK - PK
    with ExitStack() as c:
        row = c.enter_context(nc.sbuf_tensor("row", [P, TOPK, D], F32))
        diag = c.enter_context(nc.sbuf_tensor("diag", [P, 2, PK, P], F32))
        xr = c.enter_context(nc.sbuf_tensor("xr2", [P, 2, D], F32))
        ys = c.enter_context(nc.sbuf_tensor("ysr", [P, 3, D], F32))
        ring = [f"in{r}" for r in range(TOPK)]
        with Phase(nc, " ".join(ring) + " cleared pe_used dve_used diag_done sum_read par_in x_in0 x_in1 dve_s var_ready root_ready y_ready yo0 yo1 yo2") as (block, sems):
            row_in = sems[:TOPK]
            cleared, pe_used, dve_used, diag_done, sum_read, par_in, x_in0, x_in1, dve_s, var_ready, root_ready, y_ready, *y_out = sems[TOPK:]
            x_in = (x_in0, x_in1)

            @block.sync
            def _(sp):
                sp.dma_start(gcol[:, :], a["ln2_g"][0].partition_broadcast(P)).then_inc(par_in, 16)
                sp.dma_start(bcol[:, :], a["ln2_b"][0].partition_broadcast(P)).then_inc(par_in, 16)
                for t in range(NT):
                    m = rows(t)
                    if t >= 2:
                        sp.wait_ge(sum_read, t - 1)
                    sp.dma_start(xr[:m, t % 2, :], h2_d[t * P:t * P + m, :]).then_inc(x_in[t % 2], 16)
                    if t >= 3:
                        sp.wait_ge(y_out[t % 3], 16 * (t // 3))
                    sp.dma_start(ys[:m, t % 3, :], ys_d[t * P:t * P + m, :]).then_inc(x_in[t % 2], 16)
                sp.wait_ge(par_in, 32)

            @block.gpsimd
            def _(pool):
                for r in range(PK, TOPK):
                    pool.memset(row[:, r, :], 0.0).then_inc(cleared, 1)
                pool.wait_ge(cleared, TOPK)
                for n in range(NT * TOPK):
                    t, k = divmod(n, TOPK)
                    m = rows(t)
                    if t and k < PK:
                        pool.wait_ge(pe_used, PK * (t - 1) + k + 1)
                    elif t:
                        pool.wait_ge(dve_used, VK * (t - 1) + k - PK + 1)
                    pool.indirect_dma_start(out=row[:m, n % TOPK, :], out_offset=None, in_=ye_d[:, :],
                                            in_offset=bass.IndirectOffsetOnAxis(ap=dest[:m, t, k:k + 1], axis=0),
                                            bounds_check=NE * CAP - 1, oob_is_err=False) \
                        .then_inc(row_in[n % TOPK], 16)

            @block.tensor
            def _(pe):
                for t in range(NT):
                    m = rows(t)
                    if t >= 2:
                        pe.wait_ge(sum_read, t - 1)
                    pe.wait_ge(x_in[t % 2], 32 * (t // 2 + 1))
                    for k in range(-1, PK):
                        if k < 0:
                            left, right = ident[:m, :m], ys[:m, t % 3, :]
                        else:
                            left, right = diag[:m, t % 2, k, 0:m], row[:m, k, :]
                            pe.wait_ge(row_in[k], 16 * (t + 1))
                            pe.wait_ge(diag_done, PK * t + k + 1)
                        for b in range(2):
                            mm = pe.matmul(ps[:m, 2 * (t % 2) + b, :], left, right[:, b * 512:(b + 1) * 512], start=k < 0,
                                           stop=k == PK - 1)
                        if k >= 0:
                            mm.then_inc(pe_used, 1)

            @block.scalar
            def _(act):
                def diagonals(t):
                    m = rows(t)
                    if t >= 2:
                        act.wait_ge(pe_used, PK * (t - 1))
                    for k in range(PK):
                        act.activation(diag[:m, t % 2, k, 0:m], ident[:m, :m], ACT.Copy, scale=w8[:m, t, k:k + 1]).then_inc(diag_done, 1)

                diagonals(0)
                for t in range(NT):
                    if t + 1 < NT:
                        diagonals(t + 1)
                    m = rows(t)
                    act.wait_ge(var_ready, t + 1)
                    act.activation(st[:m, t % 2, 15:16], st[:m, t % 2, 14:15], ACT.Sqrt).then_inc(root_ready, 1)
                    act.wait_ge(y_ready, t + 1)
                    dst = o[0][0, t * P:t * P + m, :] if t < NT - 1 else o[1][0, :, :]
                    act.dma_start(dst, ys[:m, t % 3, :]).then_inc(y_out[t % 3], 16)
                for r in range(3):
                    act.wait_ge(y_out[r], 16 * 3)

            @block.vector
            def _(dve):
                ch = Chain(dve, dve_s)
                for r in range(PK):
                    dve.memset(row[:, r, :], 0.0).then_inc(cleared, 1)
                dve.wait_ge(par_in, 32)
                for t in range(NT):
                    m = rows(t)
                    y = ys[:m, t % 3, :]
                    dve.wait_ge(x_in[t % 2], 32 * (t // 2 + 1))
                    dve.wait_ge(pe_used, PK * (t + 1))
                    sums = ps[:m, 2 * (t % 2):2 * (t % 2) + 2, :].rearrange("p b n -> p (b n)")
                    dve.scalar_tensor_tensor(out=y, in0=xr[:m, t % 2, :], scalar=ALPHA, in1=sums, op0=ALU.mult, op1=ALU.add) \
                        .then_inc(sum_read, 1)
                    dve.wait_ge(sum_read, t + 1)
                    for k in range(PK, TOPK):
                        dve.wait_ge(row_in[k], 16 * (t + 1))
                        dve.scalar_tensor_tensor(out=y, in0=row[:m, k, :], scalar=w8[:m, t, k:k + 1], in1=y, op0=ALU.mult,
                                                 op1=ALU.add).then_inc(dve_used, 1)
                        dve.wait_ge(dve_used, VK * t + k - PK + 1)
                    layer_norm_rows(dve, ch, m, ys[:, t % 3, :], ys[:, t % 3, :], st[:, t % 2, :], gcol, var_ready, root_ready, t)
                    dve.tensor_tensor(y, y, bcol[:m, :], ALU.add).then_inc(y_ready, 1)


def mixture(nc, a, o, ps, ident, ones, gcol, bcol, st, xT, before, h2_d, tok_d, plan_d, gates_d, only_d, ys_d, ye_d):
    with ExitStack() as c:
        def sb(name, shape, dt=F32):
            return c.enter_context(nc.sbuf_tensor(name, shape, dt))
        dest = sb("dest", [P, NT, TOPK], U32)
        w8 = sb("w8", [P, NT, TOPK])
        with ExitStack() as c2:
            def sb2(name, shape, dt=F32):
                return c2.enter_context(nc.sbuf_tensor(name, shape, dt))
            tab = sb2("tab", [P, NE, 2], U32)
            with ExitStack() as c3:
                gates, chosen = (c3.enter_context(nc.sbuf_tensor(n, [P, NT, NE], F32)) for n in ("gates", "chosen"))
                picks = c3.enter_context(nc.sbuf_tensor("picks", [P, NT, TOPK], U32))
                router(nc, a, ps, xT, gates, chosen, picks)
                dispatch(nc, a, ps, ident, ones, before, xT, gates, chosen, picks, ys_d, dest, w8, tab, tok_d, plan_d,
             gates_d, only_d)
            bufs = (sb2("wg", [P, 2, KT, FE]), sb2("wu", [P, 2, KT, FE]), sb2("wd", [P, 2, 2, D]), sb2("xg", [P, 2, 2, D]),
                    sb2("sl", [P, 2 * CAP]), sb2("yo", [P, 2, 2, D]))
            experts(nc, a, ps, ident, tab, h2_d, ye_d, bufs)
            overflow(nc, a, ps, ident, h2_d, ys_d, tok_d, plan_d, gates_d, only_d, bufs)
        combine(nc, a, o, ps, ident, gcol, bcol, st, ys_d, dest, w8, ye_d, h2_d)


_INS = ["x_prompt", "x_sample", "cache_sb_k", "cache_sb_v", "state_hgrn", "ln_in_g", "ln_in_b", "w_in", "w_out", "hg_norm",
        "hg_lb_logits", "ln1_g", "ln1_b", "w_router", "router_bias", "w_exp_gate", "w_exp_up", "w_exp_down", "w_sh_gate",
        "w_sh_up", "w_sh_down", "ln2_g", "ln2_b"]
_OUTS = [(1, SEQ, D), (1, DEC, D), (1, 1, SEQ, HEADS, P), (1, 1, SEQ, HEADS, P), (1, 1, HEADS, P, P),
         (1, 1, DEC, HEADS, P), (1, 1, DEC, HEADS, P), (1, 1, HEADS, P, P)]


def kernel(**inputs):
    import concourse.bacc as bacc
    from concourse.bass_utils import run_bass_kernel_spmd

    nc = bacc.Bacc("TRN2", target_bir_lowering=False, num_devices=1)
    arrays, args = {}, {}
    for name in _INS:
        x = np.ascontiguousarray(inputs[name])
        arrays[f"in_{name}"] = x
        args[name] = nc.dram_tensor(f"in_{name}", x.shape, mybir.dt.from_np(x.dtype), kind="ExternalInput").ap()
    outs = [nc.dram_tensor(f"out_{i}", s, F32, kind="ExternalOutput").ap() for i, s in enumerate(_OUTS)]
    build(nc, args, outs)
    r = run_bass_kernel_spmd(nc, [arrays], core_ids=[0])
    return tuple(r.results[0][f"out_{i}"] for i in range(len(_OUTS)))
```
